# Optimizing a Trainium2 kernel written in Bass

```python
import math
import jax, jax.numpy as jnp
from jax import lax
import numpy as np

D_MODEL = 1024
BATCH = 1
SEQ = 256
DEPTH = 2

CHUNK = 64
ROPE_THETA = 10000.0
LN_EPS = 1e-5
DEEPNORM_ALPHA = (2.0 * DEPTH) ** 0.25
DEEPNORM_BETA = (8.0 * DEPTH) ** -0.25
MASK_VALUE = -1e30

RET_HEADS = 4
RET_DK = D_MODEL // RET_HEADS
RET_DV = 2 * RET_DK
RET_QK_WIDTH = RET_HEADS * RET_DK
RET_V_WIDTH = RET_HEADS * RET_DV
RET_IN_WIDTH = 2 * RET_QK_WIDTH + 2 * RET_V_WIDTH

SWA_HEADS = 16
SWA_KV_HEADS = 2
SWA_HEAD_DIM = D_MODEL // SWA_HEADS
SWA_GROUP = SWA_HEADS // SWA_KV_HEADS
WINDOW = 128
WINDOW_CHUNKS = WINDOW // CHUNK
SWA_Q_WIDTH = SWA_HEADS * SWA_HEAD_DIM
SWA_KV_WIDTH = SWA_KV_HEADS * SWA_HEAD_DIM
SWA_IN_WIDTH = SWA_Q_WIDTH + 2 * SWA_KV_WIDTH

MOE_GROUPS = 4
MOE_EXPERTS_PER_GROUP = 4
MOE_TOP_K = 2
MOE_D_FF = 256

N_MIXERS = 2
N_RET_LAYERS = (DEPTH + N_MIXERS - 1) // N_MIXERS
N_SWA_LAYERS = DEPTH // N_MIXERS

kernel_name = "hybrid_retention_swa_sink_hier_moe"

def rope(x, positions):
    d = x.shape[-1]
    half = d // 2
    inv_freq = ROPE_THETA ** (-jnp.arange(0, d, 2, dtype=jnp.float32) / d)
    ang = positions.astype(jnp.float32)[..., None] * inv_freq
    cos = jnp.cos(ang)[:, :, None, :]
    sin = jnp.sin(ang)[:, :, None, :]
    xf = x.astype(jnp.float32)
    x1, x2 = xf[..., :half], xf[..., half:]
    out = jnp.concatenate([x1 * cos - x2 * sin, x1 * sin + x2 * cos], axis=-1)
    return out.astype(x.dtype)

def layer_norm(x, gain, bias):
    xf = x.astype(jnp.float32)
    mu = jnp.mean(xf, axis=-1, keepdims=True)
    xc = xf - mu
    var = jnp.mean(jnp.square(xc), axis=-1, keepdims=True)
    return (xc * lax.rsqrt(var + LN_EPS) * gain + bias).astype(x.dtype)

def retention_mixer(x, positions, w_in, w_out, gn_gain):
    B, S, _ = x.shape
    n = S // CHUNK
    proj = x @ w_in
    q, k, v, g = jnp.split(
        proj, [RET_QK_WIDTH, 2 * RET_QK_WIDTH, 2 * RET_QK_WIDTH + RET_V_WIDTH], axis=-1)
    q = rope(q.reshape(B, S, RET_HEADS, RET_DK), positions)
    k = rope(k.reshape(B, S, RET_HEADS, RET_DK), positions) * (RET_DK ** -0.5)
    v = v.reshape(B, S, RET_HEADS, RET_DV)

    def to_chunks(t):
        return t.reshape(B, n, CHUNK, RET_HEADS, t.shape[-1]).transpose(1, 0, 3, 2, 4)

    qc, kc, vc = to_chunks(q), to_chunks(k), to_chunks(v)

    log_gamma = jnp.log1p(-(2.0 ** (-5.0 - jnp.arange(RET_HEADS, dtype=jnp.float32))))
    idx = jnp.arange(CHUNK, dtype=jnp.float32)
    intra_decay = jnp.exp(log_gamma[:, None, None] * jnp.abs(idx[:, None] - idx[None, :]))
    q_decay = jnp.exp(log_gamma[:, None] * (idx + 1.0))[..., None]
    k_decay = jnp.exp(log_gamma[:, None] * (CHUNK - 1.0 - idx))[..., None]
    chunk_decay = jnp.exp(log_gamma * CHUNK)[:, None, None]

    scores = jnp.einsum('nbhld,nbhmd->nbhlm', qc, kc) * intra_decay
    intra = jnp.einsum('nbhlm,nbhmv->nbhlv', scores, vc)

    def step(state, inp):
        q_i, k_i, v_i = inp
        inter_i = jnp.einsum('bhld,bhdv->bhlv', q_i * q_decay, state)
        state = state * chunk_decay + jnp.einsum('bhmd,bhmv->bhdv', k_i * k_decay, v_i)
        return state, inter_i

    state0 = jnp.zeros((B, RET_HEADS, RET_DK, RET_DV), jnp.float32)
    _, inter = lax.scan(step, state0, (qc, kc, vc))

    o = (intra + inter).astype(jnp.float32)
    mu = jnp.mean(o, axis=-1, keepdims=True)
    oc = o - mu
    var = jnp.mean(jnp.square(oc), axis=-1, keepdims=True)
    o = oc * lax.rsqrt(var + LN_EPS)
    o = o.transpose(1, 0, 3, 2, 4).reshape(B, S, RET_V_WIDTH) * gn_gain
    return (jax.nn.silu(g) * o.astype(x.dtype)) @ w_out

def swa_mixer(x, positions, w_in, b_in, sinks, w_out):
    B, S, _ = x.shape
    n = S // CHUNK
    proj = x @ w_in + b_in
    q, k, v = jnp.split(proj, [SWA_Q_WIDTH, SWA_Q_WIDTH + SWA_KV_WIDTH], axis=-1)
    q = rope(q.reshape(B, S, SWA_HEADS, SWA_HEAD_DIM), positions)
    k = rope(k.reshape(B, S, SWA_KV_HEADS, SWA_HEAD_DIM), positions)
    v = v.reshape(B, S, SWA_KV_HEADS, SWA_HEAD_DIM)
    qc = q.reshape(B, n, CHUNK, SWA_KV_HEADS, SWA_GROUP, SWA_HEAD_DIM)

    def band(t):
        tc = t.reshape(B, n, CHUNK, SWA_KV_HEADS, SWA_HEAD_DIM)
        tp = jnp.pad(tc, ((0, 0), (WINDOW_CHUNKS - 1, 0), (0, 0), (0, 0), (0, 0)))
        return jnp.concatenate([tp[:, j:j + n] for j in range(WINDOW_CHUNKS)], axis=2)

    kb, vb = band(k), band(v)
    s = jnp.einsum('bnlgrd,bnmgd->bgrnlm', qc, kb).astype(jnp.float32) * (SWA_HEAD_DIM ** -0.5)
    key_chunk = (jnp.arange(n)[:, None] - (WINDOW_CHUNKS - 1)
                 + jnp.arange(WINDOW_CHUNKS * CHUNK)[None, :] // CHUNK)
    valid = key_chunk >= 0
    s = jnp.where(valid[:, None, :], s, MASK_VALUE)
    sink = jnp.broadcast_to(
        sinks.astype(jnp.float32).reshape(SWA_KV_HEADS, SWA_GROUP)[None, :, :, None, None, None],
        s.shape[:-1] + (1,))
    p = jax.nn.softmax(jnp.concatenate([s, sink], axis=-1), axis=-1)[..., :-1]
    o = jnp.einsum('bgrnlm,bnmgd->bnlgrd', p.astype(x.dtype), vb)
    return o.reshape(B, S, SWA_Q_WIDTH) @ w_out

def hier_moe(x, w_group, b_group, w_router, b_router, w_in, w_out):
    B, S, D = x.shape
    t = x.reshape(B * S, D)
    group_logits = (t @ w_group + b_group).astype(jnp.float32)
    group_probs = jax.nn.softmax(group_logits, axis=-1)
    g_sel = jnp.argmax(group_logits, axis=-1)
    g_gate = jnp.take_along_axis(group_probs, g_sel[:, None], axis=1)
    exp_logits = (t @ w_router + b_router).astype(jnp.float32).reshape(
        -1, MOE_GROUPS, MOE_EXPERTS_PER_GROUP)
    sel_logits = jnp.take_along_axis(exp_logits, g_sel[:, None, None], axis=1)[:, 0]
    top_val, top_idx = lax.top_k(sel_logits, MOE_TOP_K)
    top_w = jax.nn.softmax(top_val, axis=-1)
    expert_w = jnp.sum(jax.nn.one_hot(top_idx, MOE_EXPERTS_PER_GROUP, dtype=jnp.float32)
                       * top_w[..., None], axis=1)
    combine = (jax.nn.one_hot(g_sel, MOE_GROUPS, dtype=jnp.float32)[:, :, None]
               * (g_gate * expert_w)[:, None, :]).astype(t.dtype)
    out = jnp.zeros_like(t)
    for gi in range(MOE_GROUPS):
        h = jnp.einsum('td,edf->tef', t, w_in[gi])
        a, u = jnp.split(h, 2, axis=-1)
        act = jax.nn.silu(a) * u * combine[:, gi, :, None]
        out = out + jnp.einsum('tef,efd->td', act, w_out[gi])
    return out.reshape(B, S, D)

def setup_inputs(seed: int = 0) -> dict:
    key = jax.random.key(seed)
    ks = jax.random.split(key, 20)
    f32 = jnp.float32
    beta = DEEPNORM_BETA

    x = jax.random.normal(ks[0], (BATCH, SEQ, D_MODEL), f32)
    offset = jax.random.randint(ks[1], (BATCH, 1), 0, 4096, dtype=jnp.int32)
    positions = offset + jnp.arange(SEQ, dtype=jnp.int32)[None, :]

    ret_col_scale = jnp.concatenate([
        jnp.ones((2 * RET_QK_WIDTH,), f32), jnp.full((RET_V_WIDTH,), beta, f32),
        jnp.ones((RET_V_WIDTH,), f32)])
    ret_w_in = (jax.random.normal(ks[2], (N_RET_LAYERS, D_MODEL, RET_IN_WIDTH), f32)
                * D_MODEL ** -0.5 * ret_col_scale)
    ret_w_out = (jax.random.normal(ks[3], (N_RET_LAYERS, RET_V_WIDTH, D_MODEL), f32)
                 * RET_V_WIDTH ** -0.5 * beta)
    ret_gn_gain = 1.0 + 0.02 * jax.random.normal(ks[4], (N_RET_LAYERS, RET_V_WIDTH), f32)

    swa_col_scale = jnp.concatenate([
        jnp.ones((SWA_Q_WIDTH + SWA_KV_WIDTH,), f32), jnp.full((SWA_KV_WIDTH,), beta, f32)])
    swa_w_in = (jax.random.normal(ks[5], (N_SWA_LAYERS, D_MODEL, SWA_IN_WIDTH), f32)
                * D_MODEL ** -0.5 * swa_col_scale)
    swa_b_in = 0.02 * jax.random.normal(ks[6], (N_SWA_LAYERS, SWA_IN_WIDTH), f32)
    swa_sinks = jax.random.normal(ks[7], (N_SWA_LAYERS, SWA_HEADS), f32)
    swa_w_out = (jax.random.normal(ks[8], (N_SWA_LAYERS, SWA_Q_WIDTH, D_MODEL), f32)
                 * SWA_Q_WIDTH ** -0.5 * beta)

    n_exp = MOE_GROUPS * MOE_EXPERTS_PER_GROUP
    moe_w_group = jax.random.normal(ks[9], (DEPTH, D_MODEL, MOE_GROUPS), f32) * D_MODEL ** -0.5
    moe_b_group = 0.01 * jax.random.normal(ks[10], (DEPTH, MOE_GROUPS), f32)
    moe_w_router = jax.random.normal(ks[11], (DEPTH, D_MODEL, n_exp), f32) * D_MODEL ** -0.5
    moe_b_router = 0.01 * jax.random.normal(ks[12], (DEPTH, n_exp), f32)
    moe_w_in = (jax.random.normal(
        ks[13], (DEPTH, MOE_GROUPS, MOE_EXPERTS_PER_GROUP, D_MODEL, 2 * MOE_D_FF), f32)
        * D_MODEL ** -0.5)
    moe_w_out = (jax.random.normal(
        ks[14], (DEPTH, MOE_GROUPS, MOE_EXPERTS_PER_GROUP, MOE_D_FF, D_MODEL), f32)
        * MOE_D_FF ** -0.5 * beta)

    ln_gain = 1.0 + 0.02 * jax.random.normal(ks[15], (DEPTH, 2, D_MODEL), f32)
    ln_bias = 0.02 * jax.random.normal(ks[16], (DEPTH, 2, D_MODEL), f32)

    return {"x": x, "positions": positions,
            "ret_w_in": ret_w_in, "ret_w_out": ret_w_out, "ret_gn_gain": ret_gn_gain,
            "swa_w_in": swa_w_in, "swa_b_in": swa_b_in, "swa_sinks": swa_sinks,
            "swa_w_out": swa_w_out,
            "moe_w_group": moe_w_group, "moe_b_group": moe_b_group,
            "moe_w_router": moe_w_router, "moe_b_router": moe_b_router,
            "moe_w_in": moe_w_in, "moe_w_out": moe_w_out,
            "ln_gain": ln_gain, "ln_bias": ln_bias}

def reference(x, positions, ret_w_in, ret_w_out, ret_gn_gain, swa_w_in, swa_b_in, swa_sinks,
              swa_w_out, moe_w_group, moe_b_group, moe_w_router, moe_b_router, moe_w_in,
              moe_w_out, ln_gain, ln_bias):
    for i in range(DEPTH):
        j = i // N_MIXERS
        if i % N_MIXERS == 0:
            mix = retention_mixer(x, positions, ret_w_in[j], ret_w_out[j], ret_gn_gain[j])
        else:
            mix = swa_mixer(x, positions, swa_w_in[j], swa_b_in[j], swa_sinks[j], swa_w_out[j])
        x = layer_norm(DEEPNORM_ALPHA * x + mix, ln_gain[i, 0], ln_bias[i, 0])
        ffn = hier_moe(x, moe_w_group[i], moe_b_group[i], moe_w_router[i], moe_b_router[i],
                       moe_w_in[i], moe_w_out[i])
        x = layer_norm(DEEPNORM_ALPHA * x + ffn, ln_gain[i, 1], ln_bias[i, 1])
    return x


_drawn_inputs = setup_inputs


def setup_inputs(seed=0):
    import zlib

    import numpy as np

    out = dict(_drawn_inputs(seed))
    spreads = {}
    factors = {'ret_gn_gain': 6.186,
     'swa_b_in': 7.545,
     'swa_sinks': 26.659,
     'moe_b_group': 8.0,
     'moe_b_router': 32.108}
    for name, (base, spread) in spreads.items():
        noise = np.random.default_rng([zlib.crc32(name.encode()), seed]).standard_normal(out[name].shape)
        drawn = base * np.exp(spread * noise) if base else spread * noise
        out[name] = __import__('jax').numpy.asarray(drawn.astype(out[name].dtype))
    for name, factor in factors.items():
        out[name] = (out[name] * factor).astype(out[name].dtype)
    return out
```

```python
from contextlib import ExitStack

import numpy as np

import concourse.bass as bass
from concourse import mybir

F32 = mybir.dt.float32
I32 = mybir.dt.int32
ALU = mybir.AluOpType
ACT = mybir.ActivationFunctionType
AX = mybir.AxisListType

P = 128
S = 256
TT = S // P
D = 1024
KT = D // P
BANK = 512
UNIT = 4096
RING = 6
CHUNK = 64
ALPHA = (2.0 * 2) ** 0.25
LN_EPS = 1e-5

HR, DK, DV = 4, 256, 512
HS, KVH, HD = 16, 2, 64
HPG = HS // KVH
QKW = HS * HD + KVH * HD
SWA_IN = QKW + KVH * HD
NROT = QKW // (HD // 2)

G, E, FF = 4, 4, 256
FT = FF // P
NR = G + G * E
NE = G * E
SLOTS = 64
PAIRS = NE // 2
NSL = NE * SLOTS
ROUNDS_MAX = -(-S // SLOTS)
assert 2 * SLOTS == P and 2 * FF == BANK

RET_UNITS = 3 * HR + HR
MOE_UNITS = G * (E + E // 2)
SWA_UNITS = 6
GROUP_UNITS = MOE_UNITS // G
MOE_SLOT = RET_UNITS % RING
assert GROUP_UNITS == RING and SWA_UNITS == RING and (RET_UNITS + SWA_UNITS) % RING == MOE_SLOT

C_FREQ_R, C_FREQ_S, C_IDENT, C_TRI, C_ONES, C_IOTA, C_TIE, C_END = np.cumsum(
    [0, 1, 32, P, P, P, SLOTS, G]).tolist()
NANG = S + TT * 32
TWO_PI = 2.0 * np.pi
TWO_PI_A = 6.28125
TWO_PI_B = float(np.round((TWO_PI - TWO_PI_A) * 2**22) / 2**22)
TWO_PI_C = TWO_PI - TWO_PI_A - TWO_PI_B
ROUND_MAGIC = 1.5 * 2**23
PI_BELOW = 3.1415925


def build(nc, d, out):
    with ExitStack() as ctx:
        def sb(name, shape, dt=F32):
            return ctx.enter_context(nc.sbuf_tensor(name, shape, dt))

        def sem(name):
            return ctx.enter_context(nc.semaphore(name))

        ps = ctx.enter_context(nc.psum_tensor("ps", [P, 8, BANK], F32))
        ring = sb("ring", [P, RING, UNIT])
        x_tok = sb("x_tok", [P, TT, D])
        xT = sb("xT", [P, KT, S])
        z = sb("z", [P, TT, D])
        ln_rows = sb("ln_rows", [P, 2, D])
        swa_bias = sb("swa_bias", [P, SWA_IN])
        cst = sb("cst", [P, C_END])
        sin = sb("sin", [P, NANG])
        cos = sb("cos", [P, NANG])
        pos_i = sb("pos_i", [P, S + TT], I32)
        w_router = sb("w_router", [P, 2, KT, NR])
        b_router = sb("b_router", [P, 2, NR])
        gn_gain = sb("gn_gain", [P, HR * DV // P])
        sinks = sb("sinks", [P, 8])
        stats = sb("stats", [P, TT, 2, 6])
        mean_var = sb("mean_var", [P, TT, 2])
        rstd = sb("rstd", [P, TT])
        var_eps = sb("var_eps", [P, TT])
        minus_half = sb("minus_half", [P, 1])
        work = sb("work", [P, 14336])

        ident = cst[:, C_IDENT:C_IDENT + P]
        tri = cst[:, C_TRI:C_TRI + P]
        ones = cst[:, C_ONES:C_ONES + P]
        iota = cst[:, C_IOTA:C_IOTA + SLOTS]
        tie = cst[:, C_TIE:C_TIE + G]

        def carve(start, *dims):
            n = int(np.prod(dims))
            view = work[:, start:start + n]
            names = "abcd"[:len(dims)]
            if len(dims) > 1:
                view = view.rearrange(f"p ({' '.join(names)}) -> p {' '.join(names)}",
                                      **{c: k for c, k in zip(names[1:], dims[1:])})
            return view, start + n

        qT, o = carve(0, 2, 2, S)
        kT, o = carve(o, 2, 2, S)
        v_ret, o = carve(o, 2, TT, DV)
        g_ret, o = carve(o, 2, TT, DV)
        yT, o = carve(o, HR * DV // P, S)
        rotA, o = carve(o, 2, S)
        rotB, o = carve(o, 2, S)
        prT, o = carve(o, 2, 3 * P)
        decay, o = carve(o, HR, 3 * P)
        angle, o = carve(o, NANG)
        turns, o = carve(o, NANG)
        assert o <= 14336, o
        xsT, o = carve(0, KT, NSL)
        onehot, o = carve(o, TT, NSL)
        onehotT, o = carve(o, PAIRS, S)
        y_slots, o = carve(o, D)
        silu_a, o = carve(o, FF)
        act_sl, o = carve(o, FF)
        actT, o = carve(o, FT, P)
        assert o <= 14336, o
        q_rows, o = carve(0, TT, QKW)
        swA, o = carve(o, QKW)
        swB, o = carve(o, QKW)
        swa_end = o
        sqT, o = carve(o, 4, HPG, CHUNK)
        skT, o = carve(o, 6 * CHUNK)
        v_win, o = carve(o, 3, P)
        probs, o = carve(o, 2, 8, P)
        probsT, o = carve(o, 8, P)
        oT = carve(swa_end - 2 * QKW, HPG, S)[0]
        assert o <= 14336, o
        s_max = sb("s_max", [P, 8])
        s_negm = sb("s_negm", [P, 2, 8])
        s_dsink = sb("s_dsink", [P, 2, 8])
        s_esink = sb("s_esink", [P, 2, 8])
        s_sum = sb("s_sum", [P, 2, 8])
        s_rden = sb("s_rden", [P, 8])
        logits = sb("logits", [P, TT, NR])
        r_max = sb("r_max", [P, TT, 3])
        r_eq = sb("r_eq", [P, TT, G])
        r_tie = sb("r_tie", [P, TT])
        r_diff = sb("r_diff", [P, TT, G])
        r_exp = sb("r_exp", [P, TT, G])
        r_gate = sb("r_gate", [P, TT])
        r_pick = sb("r_pick", [P, TT, G, E])
        r_sel = sb("r_sel", [P, TT, E])
        r_dt = sb("r_dt", [P, TT])
        r_et = sb("r_et", [P, TT])
        r_w = sb("r_w", [P, TT, 2])
        oh_group = sb("oh_group", [P, TT, G])
        oh_first = sb("oh_first", [P, TT, E])
        oh_second = sb("oh_second", [P, TT, E])
        combine = sb("combine", [P, TT, NE])
        chosen = sb("chosen", [P, TT, NE])
        picked = sb("picked", [P, TT, E])
        weight = sb("weight", [P, TT, E])
        cw_slots = sb("cw_slots", [P, PAIRS])
        key = sb("key", [P, TT, NE])
        n_over = sb("n_over", [1, ROUNDS_MAX + 1])
        more_rounds = sb("more_rounds", [1, 1], I32)

        trig_in = sem("trig_in")
        xT_in = sem("xT_in")
        x_in = sem("x_in")
        decay_in = sem("decay_in")
        params_in = sem("params_in")
        ln_in = sem("ln_in")
        out_stored = sem("out_stored")
        loaded = [[sem(f"loaded{L}_{s}") for s in range(RING)] for L in range(2)]
        dve_step = sem("dve_step")
        angles_done = sem("angles_done")
        trig_done = sem("trig_done")
        proj_done = sem("proj_done")
        rope_read = sem("rope_read")
        vg_done = sem("vg_done")
        qk_ready = sem("qk_ready")
        ret_scores = sem("ret_scores")
        ret_masked = sem("ret_masked")
        ret_o = sem("ret_o")
        gn_stats = sem("gn_stats")
        gn_rstd = sem("gn_rstd")
        gn_gated = sem("gn_gated")
        y_ready = sem("y_ready")
        yT_ps = sem("yT_ps")
        yT_ready = sem("yT_ready")
        mix_done = sem("mix_done")
        mix_out_used = sem("mix_out_used")
        z_ready = sem("z_ready")
        ln_stats = sem("ln_stats")
        ln_rstd = sem("ln_rstd")
        x_ready = sem("x_ready")
        pool_const = sem("pool_const")
        xT_ps = sem("xT_ps")
        xT_ready = sem("xT_ready")
        sproj_done = sem("sproj_done")
        sproj_read = sem("sproj_read")
        rotB_done = sem("rotB_done")
        rot_done = sem("rot_done")
        sqk_ps = sem("sqk_ps")
        sqk_ready = sem("sqk_ready")
        swa_scores = sem("swa_scores")
        max_done = sem("max_done")
        exp_done = sem("exp_done")
        probs_ready = sem("probs_ready")
        probsT_ps = sem("probsT_ps")
        probsT_ready = sem("probsT_ready")
        pv_done = sem("pv_done")
        oT_ready = sem("oT_ready")
        M = [{n: sem(f"{n}{L}") for n in (
            "logits_ps", "exp_arg", "exp_val", "group_ready", "chosen_ready", "rank_ps", "rounds_ready",
            "keys_ready", "onehot_ready", "combine_ready", "gather_ps", "gather_act", "gather_dve",
            "ohT_ps", "ohT_ready", "cw_ps", "cw_ready", "h_done", "silu_done", "act_done", "actT_ps",
            "actT_ready", "y_done", "y_act", "y_dve", "scattered", "sums_done", "z_scaled", "z_added")} for L in range(2)]

        def load_rounds(eng, L):
            eng.wait_ge(M[L]["rounds_ready"], 1)
            return eng.value_load(more_rounds[0:1, 0:1], min_val=0, max_val=ROUNDS_MAX - 1) + 1

        def slot_uses(slot):
            return len(range(slot, RET_UNITS, RING))

        block = ctx.enter_context(nc.Block())

        @block.sync
        def _(sp):
            def load(L, slot, src, cols=UNIT):
                sp.dma_start(ring[:, slot, 0:cols], src).then_inc(loaded[L][slot], 16)

            def ret_unit_used(u):
                if u < 3 * HR:
                    sp.wait_ge(proj_done, 6 * (u // 3) + 2 * (u % 3) + 2)
                elif u < RET_UNITS - 1:
                    sp.wait_ge(mix_out_used, u - 3 * HR + 1)
                else:
                    sp.wait_ge(mix_done, 4)

            def swa_unit_used(u):
                if u < 3:
                    sp.wait_ge(sproj_done, 2 * u + 2)
                elif u < SWA_UNITS - 1:
                    sp.wait_ge(mix_out_used, HR - 1 + u - 3 + 1)
                else:
                    sp.wait_ge(mix_done, 8)

            def moe_unit_used(L, j, groups):
                sp.wait_ge(M[L]["h_done" if j % 3 < 2 else "y_done"], groups * 2 - 1 + j // 3)

            def mixture(L, slot_used):
                def group(g, before):
                    for j in range(RING):
                        before(j)
                        if j % 3 < 2:
                            src = d["w_moe_in"][L, bass.ds(g * E + (j // 3) * 2 + j % 3, 1)]
                        else:
                            src = d["w_moe_out"][L, bass.ds(g * (E // 2) + j // 3, 1)]
                        load(L, (MOE_SLOT + j) % RING, src.rearrange("a p n -> p (a n)"))

                group(0, slot_used)
                with sp.Fori(1, G) as g:
                    group(g, lambda j: moe_unit_used(L, j, g))
                rounds = load_rounds(sp, L)
                with sp.If(rounds > 1):
                    with sp.Fori(1, rounds) as r:
                        with sp.Fori(0, G) as g:
                            group(g, lambda j: moe_unit_used(L, j, r * G + g))
                return rounds

            sp.dma_start(xT[:, :, :], d["x_cols"]).then_inc(xT_in, 16)
            sp.dma_start(pos_i[:, 0:S], d["pos_row"].to_broadcast([P, S])).then_inc(trig_in, 16)
            sp.dma_start(pos_i[:, S:S + TT], d["pos_col"]).then_inc(trig_in, 16)
            sp.dma_start(cst[:, :], d["consts"]).then_inc(trig_in, 16)
            for u in range(RET_UNITS):
                if u >= RING:
                    ret_unit_used(u - RING)
                load(0, u % RING, d["w_ret_in"][u] if u < 3 * HR else d["w_ret_out"][u - 3 * HR])
            rounds = mixture(0, lambda j: ret_unit_used(RET_UNITS - RING + j))
            for u in range(SWA_UNITS):
                slot = (MOE_SLOT + u) % RING
                moe_unit_used(0, u, rounds * G)
                if u < 2:
                    load(1, slot, d["w_swa_in"][u])
                elif u == 2:
                    load(1, slot, d["w_swa_kv"], KT * 2 * KVH * HD)
                else:
                    first, n = ((0, 4), (4, 2), (6, 2))[u - 3]
                    load(1, slot, d["w_swa_out"][:, first * D:(first + n) * D], n * D)
            mixture(1, swa_unit_used)
            for t in range(TT):
                sp.wait_ge(x_ready, 4 * 3 + 2 * t + 2)
                sp.dma_start(out.rearrange("a (t p) n -> p (a t) n", p=P)[:, t, :],
                             x_tok[:, t, :]).then_inc(out_stored, 16)
            sp.wait_ge(out_stored, 16 * TT)

        @block.tensor
        def _(pe):
            mm = nc.tensor.matmul

            def unit(L, slot, nth, cols=UNIT):
                pe.wait_ge(loaded[L][slot], 16 * nth)
                return ring[:, slot, 0:cols]

            def project_qk(h):
                w = unit(0, 3 * h % RING, 3 * h // RING + 1).rearrange("p (k n) -> p k n", k=KT)
                if h == 0:
                    pe.wait_ge(xT_in, 16)
                for j in range(2):
                    if h > 0:
                        pe.wait_ge(vg_done, 4 * (h - 1) + 2 + j)
                    for half in range(2):
                        for k in range(KT):
                            last = mm(ps[:, j, half * S:(half + 1) * S],
                                      w[:, k, (2 * j + half) * P:(2 * j + half + 1) * P], xT[:, k, :],
                                      start=(k == 0), stop=(k == KT - 1))
                    last.then_inc(proj_done, 1)

            def project_vg(h, j, t):
                u = 3 * h + j
                w = unit(0, u % RING, u // RING + 1).rearrange("p (k n) -> p k n", k=KT)
                if (j, t) == (1, 0):
                    if h > 0:
                        pe.wait_ge(vg_done, 4 * h)
                elif (j, t) == (2, 1):
                    pe.wait_ge(vg_done, 4 * h + 1)
                else:
                    pe.wait_ge(rope_read, 2 * h + j)
                i = 2 * j + t
                for k in range(KT):
                    last = mm(ps[:, i % 3, :], xT[:, k, t * P:(t + 1) * P], w[:, k, :],
                              start=(k == 0), stop=(k == KT - 1))
                last.then_inc(proj_done, 1)

            def ret_score(h):
                pe.wait_ge(qk_ready, 2 * h + 2)
                if h > 0:
                    pe.wait_ge(ret_masked, h)
                q, k = qT[:, h % 2], kT[:, h % 2]
                for half in range(2):
                    mm(ps[:, 3, 0:S], k[:, half, 0:P], q[:, half, :], start=(half == 0), stop=(half == 1))
                for half in range(2):
                    last = mm(ps[:, 3, S:S + P], k[:, half, P:S], q[:, half, P:S],
                              start=(half == 0), stop=(half == 1))
                last.then_inc(ret_scores, 1)

            def ret_value(h):
                pe.wait_ge(ret_masked, h + 1)
                pe.wait_ge(vg_done, 4 * h + 2)
                if h > 0:
                    pe.wait_ge(gn_gated, 2 * h)
                pr, v = prT[:, h % 2], v_ret[:, h % 2]
                mm(ps[:, 4, :], pr[:, 0:P], v[:, 0], start=True, stop=True).then_inc(ret_o, 1)
                mm(ps[:, 5, :], pr[:, P:S], v[:, 0], start=True, stop=False)
                mm(ps[:, 5, :], pr[:, S:S + P], v[:, 1], start=False, stop=True).then_inc(ret_o, 1)

            def ret_transpose(h):
                if h == 0:
                    pe.wait_ge(trig_in, 48)
                for t in range(TT):
                    pe.wait_ge(y_ready, 2 * h + t + 1)
                    if h > 0:
                        pe.wait_ge(yT_ready, 2 * (h - 1) + t + 1)
                    for j in range(DV // P):
                        last = nc.tensor.transpose(ps[:, 6 + t, j * P:(j + 1) * P],
                                                   g_ret[:, h % 2, t, j * P:(j + 1) * P], ident)
                    last.then_inc(yT_ps, 1)

            def ret_output(h):
                u = 3 * HR + h
                w = unit(0, u % RING, u // RING + 1).rearrange("p (k n) -> p k n", n=D)
                pe.wait_ge(yT_ready, 2 * h + 2)
                if h == 0:
                    pe.wait_ge(vg_done, 4 * HR)
                    pe.wait_ge(ret_masked, HR)
                for t in range(TT):
                    for n in range(2):
                        for k in range(DV // P):
                            last = mm(ps[:, 2 * t + n, :], yT[:, h * 4 + k, t * P:(t + 1) * P],
                                      w[:, k, n * BANK:(n + 1) * BANK], start=(h == 0 and k == 0),
                                      stop=(h == HR - 1 and k == DV // P - 1))
                        if h == HR - 1:
                            last.then_inc(mix_done, 1)
                if h < HR - 1:
                    last.then_inc(mix_out_used, 1)

            def transpose_x(n):
                for t in range(TT):
                    for half in range(2):
                        pe.wait_ge(x_ready, 4 * n + 2 * t + half + 1)
                        for j in range(4):
                            k = 4 * half + j
                            last = nc.tensor.transpose(ps[:, 4 + 2 * t + half, j * P:(j + 1) * P],
                                                       x_tok[:, t, k * P:(k + 1) * P], ident)
                        last.then_inc(xT_ps, 1)

            def mixture(L, used):
                m = M[L]
                transpose_x(2 * L)
                for t in range(TT):
                    pe.wait_ge(xT_ready, 8 * L + 2 * t + 2)
                    if t == 0:
                        pe.wait_ge(params_in, 80)
                        pe.wait_ge(z_ready, 8 * L + 4)
                    for k in range(KT):
                        last = mm(ps[:, 0, t * 32:t * 32 + NR], xT[:, k, t * P:(t + 1) * P],
                                  w_router[:, L, k, :], start=(k == 0), stop=(k == KT - 1))
                    last.then_inc(m["logits_ps"], 1)
                pe.wait_ge(m["chosen_ready"], 1)
                mm(ps[:, 1, 0:NE], tri, chosen[:, 0, :], start=True, stop=True)
                mm(ps[:, 1, NE:2 * NE], ones, chosen[:, 0, :], start=True, stop=False)
                mm(ps[:, 1, NE:2 * NE], tri, chosen[:, 1, :], start=False, stop=True)
                mm(ps[:, 1, 2 * NE:3 * NE], ones, chosen[:, 0, :], start=True, stop=False)
                mm(ps[:, 1, 2 * NE:3 * NE], ones, chosen[:, 1, :], start=False, stop=True)\
                    .then_inc(m["rank_ps"], 1)
                rounds = load_rounds(pe, L)

                def unit_of(i, j, n, nth):
                    slot = (MOE_SLOT + 3 * (i % 2) + j) % RING
                    pe.wait_ge(loaded[L][slot], (nth + i // 2 + used(slot) + 1) * 16)
                    return ring[:, slot, :].rearrange("p (k n) -> p k n", n=n)

                def hidden(i, first, base, w):
                    for k in range(first, first + KT // 2):
                        for e in range(2):
                            last = mm(ps[e * SLOTS:(e + 1) * SLOTS, 4, :],
                                      xsT[:, k, (2 * i + e) * SLOTS:(2 * i + e + 1) * SLOTS],
                                      w[e][:, k, :], start=(k == 0), stop=(k == KT - 1))
                    if first:
                        last.then_inc(m["h_done"], 1)

                def transpose_act(i, base):
                    pe.wait_ge(m["act_done"], base + i + 1)
                    for f in range(FT):
                        last = nc.tensor.transpose(ps[:, 5, f * P:(f + 1) * P],
                                                   act_sl[:, f * P:(f + 1) * P], ident)
                    last.then_inc(m["actT_ps"], 1)

                def project_back(i, base, nth):
                    w = unit_of(i, 2, D, nth)
                    pe.wait_ge(m["actT_ready"], base + i + 1)
                    for f in range(FT):
                        for n in range(2):
                            for e in range(2):
                                last = mm(ps[e * SLOTS:(e + 1) * SLOTS, 6 + n, :],
                                          actT[:, f, e * SLOTS:(e + 1) * SLOTS],
                                          w[:, e * FT + f, n * BANK:(n + 1) * BANK],
                                          start=(f == 0), stop=(f == FT - 1))
                    last.then_inc(m["y_done"], 1)

                def scatter(i, base):
                    pe.wait_ge(m["y_act"], base + i + 1)
                    pe.wait_ge(m["y_dve"], base + i + 1)
                    for t in range(TT):
                        for n in range(2):
                            last = mm(ps[:, 2 * t + n, :], onehotT[:, i, t * P:(t + 1) * P],
                                      y_slots[:, n * BANK:(n + 1) * BANK],
                                      start=(i == 0), stop=(i == PAIRS - 1))
                            if i == PAIRS - 1:
                                last.then_inc(m["sums_done"], 1)
                    if i < PAIRS - 1:
                        last.then_inc(m["scattered"], 1)

                def transpose_onehot():
                    for i in range(PAIRS):
                        for t in range(TT):
                            c = (i * TT + t) * P
                            last = nc.tensor.transpose(ps[:, c // BANK, c % BANK:c % BANK + P],
                                                       onehot[:, t, i * P:(i + 1) * P], ident)
                        if i % 2:
                            last.then_inc(m["ohT_ps"], 1)

                def gather(r, half):
                    for q in range(half * KT, (half + 1) * KT):
                        if q % KT >= 3 or half:
                            pe.wait_ge(m["gather_act" if (q - 3) % 2 == 0 else "gather_dve"],
                                       r * KT + (q - 3) // 2 + 1)
                        for t in range(TT):
                            last = mm(ps[:, 5 + q % 3, :], x_tok[:, t, q % KT * P:(q % KT + 1) * P],
                                      onehot[:, t, half * BANK:(half + 1) * BANK],
                                      start=(t == 0), stop=(t == TT - 1))
                        last.then_inc(m["gather_ps"], 1)

                def slot_weights():
                    pe.wait_ge(m["combine_ready"], 1)
                    for i in range(PAIRS):
                        for t in range(TT):
                            last = mm(ps[:, 0, 2 * i:2 * i + 2], onehot[:, t, i * P:(i + 1) * P],
                                      combine[:, t, 2 * i:2 * i + 2], start=(t == 0), stop=(t == TT - 1))
                    last.then_inc(m["cw_ps"], 1)

                with pe.Fori(0, rounds) as r:
                    base, nth = r * PAIRS, r * G
                    pe.wait_ge(m["onehot_ready"], r + 1)
                    gather(r, 0)
                    for i in range(PAIRS):
                        w = [unit_of(i, e, 2 * FF, nth) for e in range(2)]
                        if i == 0:
                            pe.wait_ge(m["gather_act"], r * KT + KT // 2)
                            pe.wait_ge(m["gather_dve"], r * KT + KT // 2)
                        if i > 0:
                            pe.wait_ge(m["act_done"], base + i)
                        hidden(i, 0, base, w)
                        if i == 0:
                            slot_weights()
                        else:
                            if i == PAIRS // 2 - 1:
                                pe.wait_ge(m["gather_act"], (r + 1) * KT)
                                pe.wait_ge(m["gather_dve"], (r + 1) * KT)
                            transpose_act(i - 1, base)
                        hidden(i, KT // 2, base, w)
                        if i == 0:
                            pe.wait_ge(m["cw_ready"], r + 1)
                            transpose_onehot()
                        if i == 2:
                            pe.wait_ge(m["ohT_ready"], r * 4 + 4)
                        if i > 1:
                            scatter(i - 2, base)
                        if i > 0:
                            project_back(i - 1, base, nth)
                        if i == PAIRS // 2 - 2:
                            pe.wait_ge(m["y_act"], base + i)
                            pe.wait_ge(m["y_dve"], base + i)
                            gather(r, 1)
                    transpose_act(PAIRS - 1, base)
                    scatter(PAIRS - 2, base)
                    project_back(PAIRS - 1, base, nth)
                    scatter(PAIRS - 1, base)

            def attention():
                transpose_x(1)
                for u in range(3):
                    slot = (MOE_SLOT + u) % RING
                    n = BANK if u < 2 else 2 * KVH * HD
                    w = unit(1, slot, 1, KT * n).rearrange("p (k n) -> p k n", k=KT)
                    for t in range(TT):
                        if u == 0:
                            pe.wait_ge(xT_ready, 4 + 2 * t + 2)
                        if u == 0 and t == 0:
                            pe.wait_ge(z_ready, 8)
                        for k in range(KT):
                            last = mm(ps[:, 2 * u + t, 0:n], xT[:, k, t * P:(t + 1) * P], w[:, k, :],
                                      start=(k == 0), stop=(k == KT - 1))
                        last.then_inc(sproj_done, 1)
                for t in range(TT):
                    pe.wait_ge(rot_done, t + 1)
                    for i in range(HPG):
                        last = nc.tensor.transpose(
                            ps[:, (6, 0)[t] + i // 4, (i % 4) * P:(i % 4 + 1) * P],
                            q_rows[:, t, i * P:(i + 1) * P], ident)
                        if i % 4 == 3:
                            last.then_inc(sqk_ps, 1)
                    nc.tensor.transpose(ps[:, 4 + t, 0:P], q_rows[:, t, HS * HD:QKW], ident)\
                        .then_inc(sqk_ps, 1)

                def scores(c):
                    width = P if c else CHUNK
                    start = (0, 0, 4 * CHUNK, 2 * CHUNK)[c]
                    if c == 0:
                        pe.wait_ge(sqk_ready, 4 * TT)
                    if c >= 2:
                        pe.wait_ge(exp_done, c - 1)
                    for kv in range(KVH):
                        rows = slice(kv * HD, (kv + 1) * HD)
                        for pair in range(HPG // 2):
                            last = mm(ps[:, 2 + 2 * (c % 2) + kv, pair * P:pair * P + width],
                                      sqT[rows, c, 2 * pair:2 * pair + 2, :].rearrange("p a n -> p (a n)"),
                                      skT[rows, start:start + width], start=True, stop=True)
                    last.then_inc(swa_scores, 1)

                def transpose_probs(c):
                    width = P if c else CHUNK
                    pe.wait_ge(probs_ready, c + 1)
                    if c >= 1:
                        pe.wait_ge(probsT_ready, 2 * c)
                    for i in range(8):
                        last = nc.tensor.transpose(ps[0:width, 6 + i // 4, (i % 4) * P:(i % 4 + 1) * P],
                                                   probs[:, c % 2, i, 0:width], ident)
                    last.then_inc(probsT_ps, 1)

                def values(c):
                    width = P if c else CHUNK
                    pe.wait_ge(probsT_ready, 2 * c + 2)
                    if c >= 2:
                        pe.wait_ge(oT_ready, c - 1)
                    for kv in range(KVH):
                        last = mm(ps[kv * HD:(kv + 1) * HD, c % 2, :],
                                  v_win[0:width, (0, 0, 2, 1)[c], kv * HD:(kv + 1) * HD],
                                  probsT[0:width, 4 * kv:4 * kv + 4, :], start=True, stop=True)
                    last.then_inc(pv_done, 1)

                scores(0)
                scores(1)
                for c in range(4):
                    if c + 2 < 4:
                        scores(c + 2)
                    transpose_probs(c)
                    values(c)
                pe.wait_ge(oT_ready, 4)
                for u in range(3):
                    first, n = ((0, 4), (4, 2), (6, 2))[u]
                    slot = (MOE_SLOT + 3 + u) % RING
                    w = unit(1, slot, 1, n * D).rearrange("p (k n) -> p k n", n=D)
                    for t in range(TT):
                        for half in range(2):
                            for k in range(n):
                                last = mm(ps[:, 2 * t + half, :], oT[:, first + k, t * P:(t + 1) * P],
                                          w[:, k, half * BANK:(half + 1) * BANK],
                                          start=(first + k == 0), stop=(first + k == HPG - 1))
                            if u == 2:
                                last.then_inc(mix_done, 1)
                    if u < 2:
                        last.then_inc(mix_out_used, 1)

            for h in range(HR):
                project_qk(h)
                if h > 0:
                    ret_score(h - 1)
                project_vg(h, 1, 0)
                if h > 0:
                    ret_value(h - 1)
                project_vg(h, 1, 1)
                project_vg(h, 2, 0)
                if h > 0:
                    ret_transpose(h - 1)
                project_vg(h, 2, 1)
            ret_score(HR - 1)
            ret_value(HR - 1)
            ret_output(0)
            ret_output(1)
            ret_transpose(HR - 1)
            ret_output(2)
            ret_output(3)
            mixture(0, slot_uses)
            attention()
            mixture(1, lambda slot: 1)

        @block.scalar
        def _(act):
            af = nc.scalar.activation
            act.dma_start(decay, d["decay"]).then_inc(decay_in, 16)
            act.dma_start(gn_gain[:, :], d["gn_gain"]).then_inc(params_in, 16)
            act.dma_start(w_router[:, :, :, :], d["w_router"]).then_inc(params_in, 16)
            act.dma_start(b_router[:, :, :].rearrange("p l n -> p (l n)"),
                          d["b_router"].to_broadcast([P, 2 * NR])).then_inc(params_in, 16)
            act.dma_start(sinks[:, :], d["sinks"]).then_inc(params_in, 16)
            act.dma_start(swa_bias[:, :], d["swa_bias"].to_broadcast([P, SWA_IN])).then_inc(params_in, 16)
            act.dma_start(x_tok[:, :, :], d["x_rows"]).then_inc(x_in, 16)
            act.wait_ge(angles_done, 1)
            af(sin[:, :], angle, ACT.Sin).then_inc(trig_done, 1)
            act.wait_ge(angles_done, 2)
            af(cos[:, :], turns, ACT.Sin).then_inc(trig_done, 1)

            def copy_out(h, j, t):
                act.wait_ge(proj_done, 6 * h + 2 * j + t + 1)
                if h >= 2 and t == 0:
                    if j == 1:
                        act.wait_ge(ret_o, 2 * (h - 1))
                    else:
                        act.wait_ge(yT_ps, 2 * (h - 1))
                dst = (v_ret if j == 1 else g_ret)[:, h % 2, t, :]
                af(dst, ps[:, (2 * j + t) % 3, :], ACT.Copy if j == 1 else ACT.Silu)\
                    .then_inc(vg_done, 1)

            def scale_y(h):
                for t in range(TT):
                    act.wait_ge(gn_gated, 2 * h + t + 1)
                    act.wait_ge(gn_rstd, 2 * h + t + 1)
                    y = g_ret[:, h % 2, t, :]
                    af(y, y, ACT.Copy, scale=rstd[:, t:t + 1]).then_inc(y_ready, 1)

            for h in range(HR):
                copy_out(h, 1, 0)
                copy_out(h, 1, 1)
                if h > 0:
                    scale_y(h - 1)
                copy_out(h, 2, 0)
                copy_out(h, 2, 1)
            scale_y(HR - 1)

            def copy_xT(n):
                for i in range(4):
                    act.wait_ge(xT_ps, 4 * n + i + 1)
                    t, half = i // 2, i % 2
                    af(xT[:, 4 * half:4 * half + 4, t * P:(t + 1) * P],
                       ps[:, 4 + i, :].rearrange("p (k n) -> p k n", n=P), ACT.Copy)\
                        .then_inc(xT_ready, 1)

            def mixture(L):
                m = M[L]
                copy_xT(2 * L)
                act.wait_ge(x_ready, 8 * L + 4)
                af(z[:, :, :], x_tok[:, :, :], ACT.Copy, scale=ALPHA).then_inc(m["z_scaled"], 1)
                act.wait_ge(m["exp_arg"], 1)
                af(r_exp[:, :, :], r_diff[:, :, :], ACT.Exp).then_inc(m["exp_val"], 1)
                act.wait_ge(m["exp_arg"], 2)
                af(r_et[:, :], r_dt[:, :], ACT.Exp).then_inc(m["exp_val"], 1)
                rounds = load_rounds(act, L)
                with act.Fori(0, rounds) as r:
                    def gathered(half):
                        for q in range(half * KT, (half + 1) * KT, 2):
                            act.wait_ge(m["gather_ps"], r * 2 * KT + q + 1)
                            af(xsT[:, q % KT, half * BANK:(half + 1) * BANK], ps[:, 5 + q % 3, :],
                               ACT.Copy).then_inc(m["gather_act"], 1)

                    gathered(0)
                    for i in range(PAIRS + 1):
                        if i < PAIRS:
                            act.wait_ge(m["h_done"], r * PAIRS + i + 1)
                            af(silu_a, ps[:, 4, 0:FF], ACT.Silu).then_inc(m["silu_done"], 1)
                        if i == 0:
                            for j in range(4):
                                act.wait_ge(m["ohT_ps"], r * 4 + j + 1)
                                af(onehotT[:, 2 * j:2 * j + 2, :],
                                   ps[:, j, :].rearrange("p (g n) -> p g n", n=S), ACT.Copy)\
                                    .then_inc(m["ohT_ready"], 1)
                        if i > 0:
                            act.wait_ge(m["y_done"], r * PAIRS + i)
                            if i > 1:
                                act.wait_ge(m["scattered"], r * (PAIRS - 1) + i - 1)
                            af(y_slots[:, 0:BANK], ps[:, 6, :], ACT.Copy).then_inc(m["y_act"], 1)
                        if i == PAIRS // 2 - 2:
                            gathered(1)

            mixture(0)

            copy_xT(1)
            for t in range(TT):
                for half in range(2):
                    act.wait_ge(sqk_ps, 3 * t + half + 1)
                    af(sqT[:, 2 * t:2 * t + 2, 4 * half:4 * half + 4, :].rearrange("p c i n -> p i c n"),
                       ps[:, (6, 0)[t] + half, :].rearrange("p (i c n) -> p i c n", i=4, c=2), ACT.Copy)\
                        .then_inc(sqk_ready, 1)
                act.wait_ge(sqk_ps, 3 * t + 3)
                af(skT[:, t * P:(t + 1) * P], ps[:, 4 + t, 0:P], ACT.Copy).then_inc(sqk_ready, 1)
                at, of = ((5, CHUNK), (4, 0))[t]
                af(skT[:, at * CHUNK:(at + 1) * CHUNK], ps[:, 4 + t, of:of + CHUNK], ACT.Copy)\
                    .then_inc(sqk_ready, 1)
            for c in range(4):
                width = P if c else CHUNK
                act.wait_ge(max_done, c + 1)
                if c >= 2:
                    act.wait_ge(probsT_ps, c - 1)
                for i in range(8):
                    af(probs[:, c % 2, i, 0:width], ps[:, 2 + 2 * (c % 2) + i // 4, (i % 4) * P:(i % 4) * P + width],
                       ACT.Exp, bias=s_negm[:, c % 2, i:i + 1], scale=HD ** -0.5, accum_out=s_sum[:, c % 2, i:i + 1])
                af(s_esink[:, c % 2, :], s_dsink[:, c % 2, :], ACT.Exp).then_inc(exp_done, 1)
            mixture(1)

        @block.vector
        def _(dve):
            tt, ts = nc.vector.tensor_tensor, nc.vector.tensor_scalar
            stt = nc.vector.scalar_tensor_tensor
            steps = [0]

            def then(ins):
                steps[0] += 1
                ins.then_inc(dve_step, 1)
                dve.wait_ge(dve_step, steps[0])

            dve.wait_ge(trig_in, 48)
            then(nc.vector.tensor_copy(turns[:, 0:S + TT], pos_i[:, :]))
            ts(angle[:, 0:S], turns[:, 0:S], cst[:, C_FREQ_R:C_FREQ_R + 1], None, ALU.mult)
            for t in range(TT):
                last = ts(angle[:, S + 32 * t:S + 32 * (t + 1)], cst[:, C_FREQ_S:C_FREQ_S + 32],
                          turns[:, S + t:S + t + 1], None, ALU.mult)
            then(last)
            then(ts(turns, angle, 1.0 / TWO_PI, ROUND_MAGIC, ALU.mult, ALU.add))
            then(ts(turns, turns, ROUND_MAGIC, None, ALU.subtract))
            for part in (TWO_PI_A, TWO_PI_B, TWO_PI_C):
                then(stt(angle, turns, -part, angle, ALU.mult, ALU.add))
            then(ts(angle, angle, PI_BELOW, -PI_BELOW, ALU.min, ALU.max))
            stt(turns, angle, -1.0, angle, ALU.mult, ALU.min).then_inc(angles_done, 1)
            dve.wait_ge(angles_done, 1)
            ts(turns, turns, np.pi / 2, None, ALU.add).then_inc(angles_done, 1)

            def rotate(h, j):
                if h == 0 and j == 0:
                    dve.wait_ge(trig_done, 2)
                dve.wait_ge(proj_done, 6 * h + j + 1)
                if h or j:
                    dve.wait_ge(qk_ready, 2 * h + j)
                x = ps[:, j, :].rearrange("p (a n) -> p a n", a=2)
                tt(rotA, x, cos[:, 0:S].unsqueeze(1).to_broadcast([P, 2, S]), ALU.mult)
                tt(rotB, x, sin[:, 0:S].unsqueeze(1).to_broadcast([P, 2, S]), ALU.mult)\
                    .then_inc(rope_read, 1)
                dve.wait_ge(rope_read, 2 * h + j + 1)
                if h >= 2:
                    dve.wait_ge(ret_scores, h - 1)
                dst = (qT if j == 0 else kT)[:, h % 2]
                tt(dst[:, 0], rotA[:, 0], rotB[:, 1], ALU.subtract)
                tt(dst[:, 1], rotB[:, 0], rotA[:, 1], ALU.add).then_inc(qk_ready, 1)

            def mask(h):
                dve.wait_ge(ret_scores, h + 1)
                if h == 0:
                    dve.wait_ge(decay_in, 16)
                if h >= 2:
                    dve.wait_ge(ret_o, 2 * (h - 1))
                tt(prT[:, h % 2], ps[:, 3, 0:3 * P], decay[:, h], ALU.mult).then_inc(ret_masked, 1)

            def norm_gate(h):
                for t in range(TT):
                    dve.wait_ge(ret_o, 2 * h + t + 1)
                    then(nc.vector.bn_stats(stats[:, t, 0, :], ps[:, 4 + t, :]))
                    if h > 0:
                        dve.wait_ge(gn_rstd, 2 * h)
                    nc.vector.bn_aggr(mean_var[:, t, :], stats[:, t, 0, :]).then_inc(gn_stats, 1)
                for t in range(TT):
                    dve.wait_ge(gn_stats, 2 * h + t + 1)
                    dve.wait_ge(vg_done, 4 * h + 2 + t + 1)
                    y = g_ret[:, h % 2, t, :]
                    stt(y, ps[:, 4 + t, :], mean_var[:, t, 0:1], y, ALU.subtract, ALU.mult)\
                        .then_inc(gn_gated, 1)

            def copy_yT(h):
                for t in range(TT):
                    dve.wait_ge(yT_ps, 2 * h + t + 1)
                    if h == 0 and t == 0:
                        dve.wait_ge(params_in, 80)
                    tt(yT[:, 4 * h:4 * h + 4, t * P:(t + 1) * P],
                       ps[:, 6 + t, :].rearrange("p (k n) -> p k n", n=P),
                       gn_gain[:, 4 * h:4 * h + 4].unsqueeze(2).to_broadcast([P, 4, P]), ALU.mult)\
                        .then_inc(yT_ready, 1)

            for h in range(HR):
                rotate(h, 0)
                rotate(h, 1)
                if h > 0:
                    mask(h - 1)
                    norm_gate(h - 1)
                    copy_yT(h - 1)
            mask(HR - 1)
            norm_gate(HR - 1)
            copy_yT(HR - 1)

            def mixer_residual(L):
                for i in range(4):
                    dve.wait_ge(mix_done, 4 * L + i + 1)
                    if L == 0 and i == 0:
                        dve.wait_ge(x_in, 16)
                    cols = slice((i % 2) * BANK, (i % 2 + 1) * BANK)
                    stt(z[:, i // 2, cols], x_tok[:, i // 2, cols], ALPHA, ps[:, i, :],
                        ALU.mult, ALU.add).then_inc(z_ready, 1)

            def layer_norm(n):
                for t in range(TT):
                    dve.wait_ge(z_ready, 4 * n + 2 * t + 2)
                    for half in range(2):
                        last = nc.vector.bn_stats(stats[:, t, half, :],
                                                  z[:, t, half * BANK:(half + 1) * BANK])
                    then(last)
                    nc.vector.bn_aggr(mean_var[:, t, :], stats[:, t, :, :].rearrange("p a b -> p (a b)"))\
                        .then_inc(ln_stats, 1)
                    dve.wait_ge(ln_stats, 2 * n + t + 1)
                    if t == 0:
                        dve.wait_ge(ln_in, 16 * (n + 1))
                    then(stt(z[:, t, :], z[:, t, :], mean_var[:, t, 0:1], ln_rows[:, 0, :],
                             ALU.subtract, ALU.mult))
                    dve.wait_ge(ln_rstd, 2 * n + t + 1)
                    for half in range(2):
                        cols = slice(half * BANK, (half + 1) * BANK)
                        stt(x_tok[:, t, cols], z[:, t, cols], rstd[:, t:t + 1], ln_rows[:, 1, cols],
                            ALU.mult, ALU.add).then_inc(x_ready, 1)

            def first_max(dst, values, n, m):
                then(nc.vector.tensor_reduce(r_max[:, :, m], values, AX.X, ALU.max))
                then(tt(r_eq[:, :, :], values, r_max[:, :, m:m + 1].to_broadcast([P, TT, n]),
                        ALU.is_equal))
                then(tt(r_eq[:, :, :], r_eq[:, :, :], tie.unsqueeze(1).to_broadcast([P, TT, n]),
                        ALU.mult))
                then(nc.vector.tensor_reduce(r_tie[:, :], r_eq[:, :, :], AX.X, ALU.max))
                return tt(dst, r_eq[:, :, :], r_tie[:, :].unsqueeze(2).to_broadcast([P, TT, n]),
                          ALU.is_equal)

            def mixture(L):
                m = M[L]
                dve.wait_ge(m["logits_ps"], 2)
                then(tt(logits[:, :, :], ps[:, 0, 0:2 * 32].rearrange("p (t n) -> p t n", t=TT)[:, :, 0:NR],
                        b_router[:, L:L + 1, :].to_broadcast([P, TT, NR]), ALU.add))
                first_max(oh_group[:, :, :], logits[:, :, 0:G], G, 0).then_inc(m["group_ready"], 1)
                tt(r_diff[:, :, :], logits[:, :, 0:G], r_max[:, :, 0:1].to_broadcast([P, TT, G]),
                   ALU.subtract).then_inc(m["exp_arg"], 1)
                dve.wait_ge(m["group_ready"], 1)
                then(tt(r_pick[:, :, :, :], logits[:, :, G:NR].rearrange("p t (g e) -> p t g e", g=G),
                        oh_group[:, :, :].unsqueeze(3).to_broadcast([P, TT, G, E]), ALU.mult))
                then(nc.vector.tensor_reduce(r_sel[:, :, :], r_pick[:, :, :, :]
                                             .rearrange("p t g e -> p t e g"), AX.X, ALU.add))
                then(first_max(oh_first[:, :, :], r_sel[:, :, :], E, 1))
                then(stt(r_sel[:, :, :], oh_first[:, :, :], -3e38, r_sel[:, :, :], ALU.mult, ALU.add))
                then(first_max(oh_second[:, :, :], r_sel[:, :, :], E, 2))
                then(tt(picked[:, :, :], oh_first[:, :, :], oh_second[:, :, :], ALU.add))
                of_group = oh_group[:, :, :].unsqueeze(3).to_broadcast([P, TT, G, E])
                tt(chosen[:, :, :].rearrange("p t (g e) -> p t g e", g=G), of_group,
                   picked[:, :, :].unsqueeze(2).to_broadcast([P, TT, G, E]), ALU.mult)\
                    .then_inc(m["chosen_ready"], 1)
                tt(r_dt[:, :], r_max[:, :, 2], r_max[:, :, 1], ALU.subtract).then_inc(m["exp_arg"], 1)
                dve.wait_ge(m["rank_ps"], 1)
                dve.wait_ge(m["chosen_ready"], 1)
                then(stt(key[:, :, :].rearrange("p t g -> p (t g)"), ps[:, 1, 0:TT * NE], 1.0,
                         chosen[:, :, :].rearrange("p t g -> p (t g)"), ALU.add, ALU.mult))
                ts(key[:, :, :], key[:, :, :], -1.0, None, ALU.add).then_inc(m["keys_ready"], 1)
                then(nc.vector.tensor_reduce(n_over[0:1, 0:1], ps[0:1, 1, 2 * NE:3 * NE], AX.X, ALU.max))
                for i in range(1, ROUNDS_MAX):
                    last = ts(n_over[0:1, i:i + 1], n_over[0:1, 0:1], i * SLOTS + 0.5, None, ALU.is_gt)
                then(last)
                then(nc.vector.tensor_reduce(n_over[0:1, ROUNDS_MAX:ROUNDS_MAX + 1],
                                             n_over[0:1, 1:ROUNDS_MAX], AX.X, ALU.add))
                nc.vector.tensor_copy(more_rounds[0:1, 0:1], n_over[0:1, ROUNDS_MAX:ROUNDS_MAX + 1])\
                    .then_inc(m["rounds_ready"], 1)
                dve.wait_ge(m["exp_val"], 1)
                then(nc.vector.tensor_reduce(r_gate[:, :], r_exp[:, :, :], AX.X, ALU.add))
                then(nc.vector.reciprocal(r_gate[:, :], r_gate[:, :]))
                dve.wait_ge(m["exp_val"], 2)
                then(ts(r_w[:, :, 0], r_et[:, :], 1.0, None, ALU.add))
                then(nc.vector.reciprocal(r_w[:, :, 0], r_w[:, :, 0]))
                then(tt(r_w[:, :, 0], r_w[:, :, 0], r_gate[:, :], ALU.mult))
                then(tt(r_w[:, :, 1], r_w[:, :, 0], r_et[:, :], ALU.mult))
                tt(oh_first[:, :, :], oh_first[:, :, :], r_w[:, :, 0:1].to_broadcast([P, TT, E]), ALU.mult)
                then(tt(oh_second[:, :, :], oh_second[:, :, :],
                        r_w[:, :, 1:2].to_broadcast([P, TT, E]), ALU.mult))
                then(tt(weight[:, :, :], oh_first[:, :, :], oh_second[:, :, :], ALU.add))
                tt(combine[:, :, :].rearrange("p t (g e) -> p t g e", g=G), of_group,
                   weight[:, :, :].unsqueeze(2).to_broadcast([P, TT, G, E]), ALU.mult)\
                    .then_inc(m["combine_ready"], 1)
                rounds = load_rounds(dve, L)
                with dve.Fori(0, rounds) as r:
                    dve.wait_ge(m["keys_ready"], r + 1)
                    for t in range(TT):
                        last = tt(onehot[:, t, :].rearrange("p (e n) -> p e n", n=SLOTS),
                                  iota.unsqueeze(1).to_broadcast([P, NE, SLOTS]),
                                  key[:, t, :].unsqueeze(2).to_broadcast([P, NE, SLOTS]), ALU.is_equal)
                    last.then_inc(m["onehot_ready"], 1)
                    dve.wait_ge(m["onehot_ready"], r + 1)
                    ts(key[:, :, :], key[:, :, :], -float(SLOTS), None, ALU.add)\
                        .then_inc(m["keys_ready"], 1)
                    def gathered(half):
                        for q in range(half * KT + 1, (half + 1) * KT, 2):
                            dve.wait_ge(m["gather_ps"], r * 2 * KT + q + 1)
                            nc.vector.tensor_copy(xsT[:, q % KT, half * BANK:(half + 1) * BANK],
                                                  ps[:, 5 + q % 3, :]).then_inc(m["gather_dve"], 1)

                    gathered(0)
                    dve.wait_ge(m["cw_ps"], r + 1)
                    for e in range(2):
                        rows = slice(e * SLOTS, (e + 1) * SLOTS)
                        both = ps[rows, 0, 0:NE].rearrange("p (i e) -> p i e", e=2)
                        last = nc.vector.tensor_copy(cw_slots[rows, :], both[:, :, e])
                    last.then_inc(m["cw_ready"], 1)
                    for i in range(PAIRS + 1):
                        n = r * PAIRS + i
                        if i > 0:
                            dve.wait_ge(m["actT_ps"], n)
                            nc.vector.tensor_copy(actT, ps[:, 5, 0:FT * P]
                                                  .rearrange("p (f n) -> p f n", n=P))\
                                .then_inc(m["actT_ready"], 1)
                        if i < PAIRS:
                            dve.wait_ge(m["silu_done"], n + 1)
                            if i == 0:
                                dve.wait_ge(m["cw_ready"], r + 1)
                            stt(act_sl, ps[:, 4, FF:2 * FF], cw_slots[:, i:i + 1], silu_a,
                                ALU.mult, ALU.mult).then_inc(m["act_done"], 1)
                        if i > 0:
                            dve.wait_ge(m["y_done"], n)
                            if i > 1:
                                dve.wait_ge(m["scattered"], r * (PAIRS - 1) + i - 1)
                            nc.vector.tensor_copy(y_slots[:, BANK:2 * BANK], ps[:, 7, :])\
                                .then_inc(m["y_dve"], 1)
                        if i == PAIRS // 2 - 2:
                            gathered(1)
                    dve.wait_ge(m["z_scaled"], 1)
                    for i in range(4):
                        cols = slice((i % 2) * BANK, (i % 2 + 1) * BANK)
                        dve.wait_ge(m["sums_done"], r * 4 + i + 1)
                        last = tt(z[:, i // 2, cols], z[:, i // 2, cols], ps[:, i, :], ALU.add)
                    last.then_inc(m["z_added"], 1)
                    dve.wait_ge(m["z_added"], r + 1)
                for i in range(4):
                    nc.vector.nop().then_inc(z_ready, 1)

            mixer_residual(0)
            layer_norm(0)
            mixture(0)
            layer_norm(1)

            for u in range(3):
                for t in range(TT):
                    dve.wait_ge(sproj_done, 2 * u + t + 1)
                    if u < 2:
                        tt(q_rows[:, t, u * BANK:(u + 1) * BANK], ps[:, 2 * u + t, :],
                           swa_bias[:, u * BANK:(u + 1) * BANK], ALU.add)
                    else:
                        then(tt(q_rows[:, t, HS * HD:QKW], ps[:, 4 + t, 0:KVH * HD],
                                swa_bias[:, HS * HD:QKW], ALU.add))
            for win, part, t in ((0, slice(0, P), 0), (1, slice(0, P), 1), (2, slice(0, CHUNK), 1),
                                 (2, slice(CHUNK, P), 0)):
                last = tt(v_win[part, win, :], ps[part, 4 + t, KVH * HD:2 * KVH * HD],
                          swa_bias[part, QKW:SWA_IN], ALU.add)
            last.then_inc(sproj_read, 1)
            dve.wait_ge(sproj_read, 1)
            for t in range(TT):
                if t:
                    dve.wait_ge(rot_done, t)
                x = q_rows[:, t, :].rearrange("p (h n) -> p h n", n=32)
                c = cos[:, S + 32 * t:S + 32 * (t + 1)].unsqueeze(1).to_broadcast([P, NROT, 32])
                then(tt(swA.rearrange("p (h n) -> p h n", n=32), x, c, ALU.mult))
                dve.wait_ge(rotB_done, t + 1)
                xa = swA.rearrange("p (h a n) -> p h a n", a=2, n=32)
                xb = swB.rearrange("p (h a n) -> p h a n", a=2, n=32)
                y = q_rows[:, t, 0:HS * HD].rearrange("p (i g a n) -> p g i a n", i=HPG, g=KVH, a=2)
                yk = q_rows[:, t, HS * HD:QKW].rearrange("p (h a n) -> p h a n", a=2, n=32)
                for half, first, second, op in ((0, xa, xb, ALU.subtract), (1, xb, xa, ALU.add)):
                    for g in range(KVH):
                        heads = slice(g * HPG, (g + 1) * HPG)
                        tt(y[:, g, :, half, :], first[:, heads, 0, :], second[:, heads, 1, :], op)
                    last = tt(yk[:, :, half, :], first[:, HS:, 0, :], second[:, HS:, 1, :], op)
                last.then_inc(rot_done, 1)
            def row_max(c):
                width = P if c else CHUNK
                s = ps[:, 2 + 2 * (c % 2):4 + 2 * (c % 2), :].rearrange("p b (i n) -> p (b i) n", n=P)
                dve.wait_ge(swa_scores, c + 1)
                then(nc.vector.tensor_reduce(s_max[:, :], s[:, :, 0:width], AX.X, ALU.max))
                then(stt(s_max[:, :], s_max[:, :], HD ** -0.5, sinks[:, :], ALU.mult, ALU.max))
                then(ts(s_negm[:, c % 2, :], s_max[:, :], -1.0, None, ALU.mult))
                tt(s_dsink[:, c % 2, :], sinks[:, :], s_negm[:, c % 2, :], ALU.add)\
                    .then_inc(max_done, 1)

            row_max(0)
            row_max(1)
            for c in range(4):
                width = P if c else CHUNK
                dve.wait_ge(exp_done, c + 1)
                then(tt(s_rden[:, :], s_sum[:, c % 2, :], s_esink[:, c % 2, :], ALU.add))
                then(nc.vector.reciprocal(s_rden[:, :], s_rden[:, :]))
                tt(probs[:, c % 2, :, 0:width], probs[:, c % 2, :, 0:width],
                   s_rden[:, :].unsqueeze(2).to_broadcast([P, 8, width]), ALU.mult)\
                    .then_inc(probs_ready, 1)
                if c + 2 < 4:
                    row_max(c + 2)
                dve.wait_ge(probsT_ps, c + 1)
                if c:
                    dve.wait_ge(pv_done, c)
                for half in range(2):
                    nc.vector.tensor_copy(probsT[0:width, 4 * half:4 * half + 4, :],
                                          ps[0:width, 6 + half, :].rearrange("p (i n) -> p i n", n=P))\
                        .then_inc(probsT_ready, 1)
                dve.wait_ge(pv_done, c + 1)
                nc.vector.tensor_copy(oT[:, :, c * CHUNK:(c + 1) * CHUNK],
                                      ps[:, c % 2, :].rearrange("p (i n) -> p i n", n=CHUNK))\
                    .then_inc(oT_ready, 1)
            mixer_residual(1)
            layer_norm(2)
            mixture(1)
            layer_norm(3)

        @block.gpsimd
        def _(pool):
            nc.gpsimd.memset(minus_half[:, :], -0.5).then_inc(pool_const, 1)
            pool.dma_start(ln_rows[:, :, :], d["ln_rows"][0:1].to_broadcast([P, 2, D])).then_inc(ln_in, 16)
            pool.wait_ge(pool_const, 1)
            count = [1]

            def inverse_std(t):
                nc.gpsimd.tensor_scalar(var_eps[:, t:t + 1], mean_var[:, t, 1:2], LN_EPS, None, ALU.add)\
                    .then_inc(pool_const, 1)
                count[0] += 1
                pool.wait_ge(pool_const, count[0])
                return nc.gpsimd.tensor_tensor(rstd[:, t:t + 1], var_eps[:, t:t + 1], minus_half[:, :],
                                               ALU.pow)

            for h in range(HR):
                for t in range(TT):
                    pool.wait_ge(gn_stats, 2 * h + t + 1)
                    if h > 0:
                        pool.wait_ge(y_ready, 2 * (h - 1) + t + 1)
                    inverse_std(t).then_inc(gn_rstd, 1)

            def layer_norm(n):
                for t in range(TT):
                    pool.wait_ge(ln_stats, 2 * n + t + 1)
                    if n == 0:
                        pool.wait_ge(y_ready, 2 * HR)
                    inverse_std(t).then_inc(ln_rstd, 1)
                if n < 3:
                    pool.wait_ge(x_ready, 4 * n + 4)
                    pool.dma_start(ln_rows[:, :, :], d["ln_rows"][n + 1:n + 2].to_broadcast([P, 2, D]))\
                        .then_inc(ln_in, 16)

            layer_norm(0)
            layer_norm(1)
            pool.wait_ge(sproj_read, 1)
            for t in range(TT):
                if t:
                    pool.wait_ge(rot_done, t)
                x = q_rows[:, t, :].rearrange("p (h n) -> p h n", n=32)
                s = sin[:, S + 32 * t:S + 32 * (t + 1)].unsqueeze(1).to_broadcast([P, NROT, 32])
                nc.gpsimd.tensor_tensor(swB.rearrange("p (h n) -> p h n", n=32), x, s, ALU.mult)\
                    .then_inc(rotB_done, 1)
            layer_norm(2)
            layer_norm(3)


def shape_constants():
    c = np.zeros((P, C_END), np.float32)
    c[:, C_FREQ_R] = 10000.0 ** (-np.arange(0, DK, 2, dtype=np.float64) / DK)
    c[:, C_FREQ_S:C_FREQ_S + 32] = 10000.0 ** (-np.arange(0, HD, 2, dtype=np.float64) / HD)
    c[:, C_IDENT:C_IDENT + P] = np.eye(P)
    c[:, C_TRI:C_TRI + P] = np.triu(np.ones((P, P)), 1)
    c[:, C_ONES:C_ONES + P] = 1.0
    c[:, C_IOTA:C_IOTA + SLOTS] = np.arange(SLOTS)
    c[:, C_TIE:C_TIE + G] = np.arange(G, 0, -1)
    log_gamma = np.log1p(-(2.0 ** (-5.0 - np.arange(HR, dtype=np.float64))))
    m, n = np.arange(S)[:, None], np.arange(S)[None, :]
    seen = m // CHUNK <= n // CHUNK
    full = np.exp(log_gamma[:, None, None] * np.abs(n - m)) * seen * DK ** -0.5
    decay = np.concatenate([full[:, 0:P, :], full[:, P:S, P:S]], axis=2).transpose(1, 0, 2)
    return c, np.ascontiguousarray(decay.astype(np.float32))


def kernel(x, positions, ret_w_in, ret_w_out, ret_gn_gain, swa_w_in, swa_b_in, swa_sinks, swa_w_out,
           moe_w_group, moe_b_group, moe_w_router, moe_b_router, moe_w_in, moe_w_out, ln_gain, ln_bias):
    import concourse.bacc as bacc
    from concourse.bass_utils import run_bass_kernel_spmd as run

    def tiles(w):
        return w.reshape(-1, P, w.shape[-1]).transpose(1, 0, 2)

    def lay(a):
        return np.ascontiguousarray(np.asarray(a))

    w_in = tiles(np.asarray(ret_w_in)[0])
    qw, vw = HR * DK, HR * DV
    ret_units = []
    for h in range(HR):
        q, k = w_in[:, :, h * DK:(h + 1) * DK], w_in[:, :, qw + h * DK:qw + (h + 1) * DK]
        ret_units.append(np.concatenate([q, k], axis=2))
        for first in (2 * qw, 2 * qw + vw):
            ret_units.append(w_in[:, :, first + h * DV:first + (h + 1) * DV])
    swa = tiles(np.asarray(swa_w_in)[0])
    consts, decay = shape_constants()
    x0 = np.asarray(x)[0]
    swa_out = np.asarray(swa_w_out)[0].reshape(KVH, HPG, HD, D).transpose(0, 2, 1, 3)
    sink_rows = np.repeat(np.asarray(swa_sinks)[0].reshape(8, 2), CHUNK, axis=1).T
    arrays = {
        "x_rows": x0.reshape(TT, P, D).transpose(1, 0, 2),
        "x_cols": tiles(x0.T),
        "pos_row": np.asarray(positions).reshape(1, S),
        "pos_col": np.asarray(positions).reshape(TT, P).T,
        "consts": consts,
        "decay": decay,
        "w_ret_in": np.stack([u.reshape(P, UNIT) for u in ret_units]),
        "w_ret_out": np.asarray(ret_w_out)[0].reshape(HR, DV // P, P, D).transpose(0, 2, 1, 3)
        .reshape(HR, P, UNIT),
        "w_swa_in": np.stack([swa[:, :, u * BANK:(u + 1) * BANK].reshape(P, UNIT) for u in range(2)]),
        "w_swa_kv": swa[:, :, HS * HD:SWA_IN].reshape(P, -1),
        "w_swa_out": swa_out.reshape(P, HPG * D),
        "w_moe_in": np.asarray(moe_w_in).reshape(2, G * E, KT, P, 2 * FF).transpose(0, 1, 3, 2, 4)
        .reshape(2, G * E, P, UNIT),
        "w_moe_out": np.asarray(moe_w_out).reshape(2, G * E // 2, 2 * FT, P, D).transpose(0, 1, 3, 2, 4)
        .reshape(2, G * E // 2, P, UNIT),
        "ln_rows": np.stack([np.asarray(ln_gain), np.asarray(ln_bias)], axis=2).reshape(4, 2, D),
        "w_router": np.stack([np.concatenate([tiles(np.asarray(moe_w_group)[i]),
                                              tiles(np.asarray(moe_w_router)[i])], axis=2)
                              for i in range(2)], axis=1),
        "b_router": np.concatenate([np.asarray(moe_b_group), np.asarray(moe_b_router)], axis=1)
        .reshape(1, 2 * NR),
        "gn_gain": np.asarray(ret_gn_gain)[0].reshape(HR * DV // P, P).T,
        "sinks": sink_rows,
        "swa_bias": np.asarray(swa_b_in).reshape(1, SWA_IN),
    }
    nc = bacc.Bacc("TRN2", target_bir_lowering=False, num_devices=1)
    feeds, d = {}, {}
    for name, a in arrays.items():
        feeds[f"in_{name}"] = lay(a)
        d[name] = nc.dram_tensor(f"in_{name}", feeds[f"in_{name}"].shape,
                                 mybir.dt.from_np(feeds[f"in_{name}"].dtype), kind="ExternalInput").ap()
    out = nc.dram_tensor("out", (1, S, D), F32, kind="ExternalOutput").ap()
    build(nc, d, out)
    return run(nc, [feeds], core_ids=[0]).results[0]["out"]
```

```python
from contextlib import ExitStack

import numpy as np

import concourse.bass as bass
from concourse import mybir

F32 = mybir.dt.float32
F32R = mybir.dt.float32r
BF16 = mybir.dt.bfloat16
I32 = mybir.dt.int32
ALU = mybir.AluOpType
ACT = mybir.ActivationFunctionType
AX = mybir.AxisListType

P = 128
S = 256
TT = S // P
D = 1024
KT = D // P
BANK = 512
UNIT = 2048
RING = 10
RET_RING = 8
CHUNK = 64
ALPHA = (2.0 * 2) ** 0.25
LN_EPS = 1e-5

HR, DK, DV = 4, 256, 512
HS, KVH, HD = 16, 2, 64
HPG = HS // KVH
QKW = HS * HD + KVH * HD
SWA_IN = QKW + KVH * HD
NROT = QKW // (HD // 2)

G, E, FF = 4, 4, 256
FT = FF // P
NR = G + G * E
NE = G * E
SLOTS = 64
PAIRS = NE // 2
NSL = NE * SLOTS
ROUNDS_MAX = -(-S // SLOTS)
assert 2 * SLOTS == P and 2 * FF == BANK

RET_UNITS = 2 * (3 * HR + HR)
PAIR_UNITS = 6
MOE_UNITS = PAIRS * PAIR_UNITS
SWA_UNITS = 9
MOE_SLOT = (0, (SWA_UNITS + MOE_UNITS) % RING)
SWA_SLOT = MOE_UNITS % RING
assert RET_UNITS % RET_RING == 0 and SWA_UNITS == RING - 1

PIECE = UNIT // 2
HEAD_PIECES = 12
PIECES = HR * HEAD_PIECES
SPLIT_BUFS = 3
SPLIT_PRODUCTS = ((0, 0), (0, 1), (1, 0))

C_FREQ_R, C_FREQ_S, C_IDENT, C_TRI, C_ONES, C_IOTA, C_TIE, C_OVER, C_END = np.cumsum(
    [0, 1, 32, P, P, P, SLOTS, G, ROUNDS_MAX - 1]).tolist()
NANG = S + TT * 32
TWO_PI = 2.0 * np.pi
TWO_PI_A = 6.28125
TWO_PI_B = float(np.round((TWO_PI - TWO_PI_A) * 2**22) / 2**22)
TWO_PI_C = TWO_PI - TWO_PI_A - TWO_PI_B
ROUND_MAGIC = 1.5 * 2**23
PI_BELOW = 3.1415925


def build(nc, d, out):
    with ExitStack() as ctx:
        def sb(name, shape, dt=F32):
            return ctx.enter_context(nc.sbuf_tensor(name, shape, dt))

        def sem(name):
            return ctx.enter_context(nc.semaphore(name))

        ps = ctx.enter_context(nc.psum_tensor("ps", [P, 8, BANK], F32))
        ring_low = sb("ring_low", [P, RET_RING, UNIT])
        x_tok = sb("x_tok", [P, TT, D])
        z = sb("z", [P, TT, D])
        ln_rows = sb("ln_rows", [P, 2, D])
        swa_bias = sb("swa_bias", [P, SWA_IN])
        cst = sb("cst", [P, C_END])
        sin = sb("sin", [P, NANG])
        cos = sb("cos", [P, NANG])
        pos_i = sb("pos_i", [P, S + TT], I32)
        w_router = sb("w_router", [P, 2, KT, NR])
        b_router = sb("b_router", [P, 2, NR])
        gn_gain = sb("gn_gain", [P, HR * DV // P])
        sinks = sb("sinks", [P, 8])
        stats = sb("stats", [P, TT, 2, 6])
        mean_var = sb("mean_var", [P, TT, 2])
        rstd = sb("rstd", [P, TT])
        var_eps = sb("var_eps", [P, TT])
        minus_half = sb("minus_half", [P, 1])

        ident = cst[:, C_IDENT:C_IDENT + P]
        tri_ones = sb("tri_ones", [P, 2 * P], BF16)
        tri, ones = tri_ones[:, 0:P], tri_ones[:, P:2 * P]
        iota = cst[:, C_IOTA:C_IOTA + SLOTS]
        tie = cst[:, C_TIE:C_TIE + G]

        def carve(of, start, *dims):
            n = int(np.prod(dims))
            view = of[:, start:start + n]
            names = "abcd"[:len(dims)]
            if len(dims) > 1:
                view = view.rearrange(f"p ({' '.join(names)}) -> p {' '.join(names)}",
                                      **{c: k for c, k in zip(names[1:], dims[1:])})
            return view, start + n

        s_max = sb("s_max", [P, 8])
        s_negm = sb("s_negm", [P, 2, 8])
        s_dsink = sb("s_dsink", [P, 2, 8])
        s_esink = sb("s_esink", [P, 2, 8])
        s_sum = sb("s_sum", [P, 2, 8])
        s_rden = sb("s_rden", [P, 8])
        logits = sb("logits", [P, TT, NR])
        r_first = sb("r_first", [P, TT, 1 + G])
        r_second = sb("r_second", [P, TT, 1 + G])
        r_rest = sb("r_rest", [P, TT, NR])
        r_eq = sb("r_eq", [P, TT, NR])
        r_tie = sb("r_tie", [P, TT, 1 + G])
        oh_first = sb("oh_first", [P, TT, NR])
        oh_second = sb("oh_second", [P, TT, NR])
        r_diff = sb("r_diff", [P, TT, G])
        r_exp = sb("r_exp", [P, TT, G])
        r_gate = sb("r_gate", [P, TT])
        r_dt = sb("r_dt", [P, TT, 1 + G])
        r_et = sb("r_et", [P, TT, 1 + G])
        r_w1 = sb("r_w1", [P, TT, 1 + G])
        r_w2 = sb("r_w2", [P, TT, 1 + G])
        combine = sb("combine", [P, TT, NE])
        chosen = sb("chosen", [P, TT, NE], BF16)
        picked = sb("picked", [P, TT, NE])
        weight = sb("weight", [P, TT, NE])
        cw_slots = sb("cw_slots", [P, PAIRS])
        key = sb("key", [P, TT, NE])
        n_over = sb("n_over", [1, ROUNDS_MAX + 1])
        more_rounds = sb("more_rounds", [1, 1], I32)

        with ExitStack() as phase:
            work = phase.enter_context(nc.sbuf_tensor("ret_parts", [P, 4096 + SPLIT_BUFS * 2 * PIECE],
                                                      F32R))
            xT_parts, o = carve(work, 0, 2, KT, S)
            w_parts, o = carve(work, o, SPLIT_BUFS, 2, PIECE)
            work = phase.enter_context(nc.sbuf_tensor("ret_work", [P, 13696], F32))
            qT, o = carve(work, 0, 2, 2, S)
            kT, o = carve(work, o, 2, 2, S)
            v_ret, o = carve(work, o, 2, TT, DV)
            g_ret, o = carve(work, o, 2, TT, DV)
            yT_start = o
            yT, o = carve(work, o, HR * DV // P, S)
            rotA, o = carve(work, o, 2, S)
            rotB, o = carve(work, o, 2, S)
            prT, o = carve(work, o, 2, 3 * P)
            decay, o = carve(work, o, HR, 3 * P)
            assert o <= 13696, o
            angle, end = carve(work, yT_start, NANG)
            turns, end = carve(work, end, NANG)
        ring_high = sb("ring_high", [P, RING - RET_RING, UNIT])
        xT = sb("xT", [P, KT, S])
        with ExitStack() as phase:
            work = phase.enter_context(nc.sbuf_tensor("moe_work", [P, 8960], F32))
            xsT, o = carve(work, 0, KT, NSL)
            silu_a, o = carve(work, o, FF)
            act_sl, o = carve(work, o, FF)
            actT, o = carve(work, o, FT, P)
            assert o == 8960, o
            work = phase.enter_context(nc.sbuf_tensor("moe_parts", [P, 10240], F32R))
            x_parts, o = carve(work, 0, 2, TT, D)
            onehot, o = carve(work, o, TT, NSL)
            onehotT, o = carve(work, o, PAIRS, S)
            y_parts, o = carve(work, o, 2, D)
            assert o == 10240, o
        with ExitStack() as phase:
            work = phase.enter_context(nc.sbuf_tensor("swa_work", [P, 11264], F32))
            q_rows, o = carve(work, 0, TT, QKW)
            rot_cos, o = carve(work, o, 2, BANK)
            rot_sin, o = carve(work, o, 2, BANK)
            unrotated, o = carve(work, o, 2, BANK)
            sqT, o = carve(work, o, 4, HPG, CHUNK)
            skT, o = carve(work, o, 6 * CHUNK)
            v_win, o = carve(work, o, 3, P)
            probs, o = carve(work, o, 2, 8, P)
            probsT, o = carve(work, o, 8, P)
            assert o <= 11264, o
            oT = carve(work, TT * QKW, HPG, S)[0]

        trig_in = sem("trig_in")
        xT_in = [sem("xT_in0"), sem("xT_in1")]
        x_in = sem("x_in")
        decay_in = sem("decay_in")
        params_in = sem("params_in")
        ln_in = sem("ln_in")
        out_stored = sem("out_stored")
        loaded = [[sem(f"loaded{L}_{s}") for s in range(RING)] for L in range(2)]
        dve_step = sem("dve_step")
        angles_done = sem("angles_done")
        tri_ready = sem("tri_ready")
        trig_done = sem("trig_done")
        x_split_high = sem("x_split_high")
        x_split_low = sem("x_split_low")
        w_high = sem("w_high")
        w_low = sem("w_low")
        w_used = sem("w_used")
        rope_read = sem("rope_read")
        vg_done = sem("vg_done")
        qk_ready = sem("qk_ready")
        ret_scores = sem("ret_scores")
        ret_masked = sem("ret_masked")
        ret_o = sem("ret_o")
        gn_stats = sem("gn_stats")
        gn_rstd = sem("gn_rstd")
        gn_gated = sem("gn_gated")
        y_ready = sem("y_ready")
        yT_ps = sem("yT_ps")
        yT_ready = sem("yT_ready")
        mix_done = sem("mix_done")
        mix_out_used = sem("mix_out_used")
        z_ready = sem("z_ready")
        ln_stats = sem("ln_stats")
        ln_rstd = sem("ln_rstd")
        x_ready = sem("x_ready")
        pool_const = sem("pool_const")
        xT_ps = sem("xT_ps")
        xT_ready = sem("xT_ready")
        sproj_done = sem("sproj_done")
        sproj_read = sem("sproj_read")
        rotB_done = sem("rotB_done")
        rot_done = sem("rot_done")
        sqk_ps = sem("sqk_ps")
        sqk_ready = sem("sqk_ready")
        swa_scores = sem("swa_scores")
        max_done = sem("max_done")
        exp_done = sem("exp_done")
        probs_ready = sem("probs_ready")
        probsT_ps = sem("probsT_ps")
        probsT_ready = sem("probsT_ready")
        pv_done = sem("pv_done")
        oT_ready = sem("oT_ready")
        M = [{n: sem(f"{n}{L}") for n in (
            "logits_ps", "exp_arg", "exp_val", "chosen_ready", "rank_ps", "rounds_ready",
            "keys_ready", "onehot_ready", "combine_ready", "gather_ps", "gather_act", "gather_dve",
            "ohT_ps", "ohT_ready", "cw_ps", "cw_ready", "h_half", "h_done", "silu_done", "act_done", "actT_ps",
            "actT_ready", "y_done", "y_high", "y_low", "x_high", "x_low", "scattered", "sums_done",
            "z_scaled", "z_added")} for L in range(2)]

        def load_rounds(eng, L):
            eng.wait_ge(M[L]["rounds_ready"], 1)
            return eng.value_load(more_rounds[0:1, 0:1], min_val=0, max_val=ROUNDS_MAX - 1) + 1

        def slot_of(slot):
            return ring_low[:, slot, :] if slot < RET_RING else ring_high[:, slot - RET_RING, :]

        x_staged = z[:, :, :].rearrange("p t n -> p (t n)").rearrange("p (k n) -> p k n", k=KT)

        block = ctx.enter_context(nc.Block())

        @block.sync
        def _(sp):
            def load(L, slot, src):
                sp.dma_start(slot_of(slot), src).then_inc(loaded[L][slot], 16)

            def ret_unit_used(u):
                m = u // 2
                if m < 3 * HR:
                    sp.wait_ge(w_low, 2 * (u + 1))
                elif m < 4 * HR - 1:
                    sp.wait_ge(mix_out_used, m - 3 * HR + 1)
                else:
                    sp.wait_ge(mix_done, 4)

            def swa_unit_used(u):
                if u < 5:
                    sp.wait_ge(sproj_done, 2 * ((u + 1) // 2) + 2)
                elif u < SWA_UNITS - 1:
                    sp.wait_ge(mix_out_used, HR - 1 + u - 5 + 1)
                else:
                    sp.wait_ge(mix_done, 8)

            def moe_unit_used(L, r, n):
                pair, kind = divmod(n, PAIR_UNITS)
                used = "h_half" if kind < 2 else "h_done" if kind < 4 else "y_done"
                sp.wait_ge(M[L][used], r * PAIRS + pair + 1)

            def mixture(L, slot_used):
                def round_units(before):
                    for n in range(MOE_UNITS):
                        before(n)
                        pair, kind = divmod(n, PAIR_UNITS)
                        half = kind // 2 if kind < 4 else kind % 2
                        cols = slice(half * UNIT, (half + 1) * UNIT)
                        src = d["w_moe_in"][L, 2 * pair + kind % 2] if kind < 4 else d["w_moe_out"][L, pair]
                        load(L, (MOE_SLOT[L] + n) % RING, src[:, cols])

                round_units(lambda n: moe_unit_used(L, 0, n - RING) if n >= RING else slot_used(n))
                rounds = load_rounds(sp, L)
                with sp.If(rounds > 1):
                    with sp.Fori(1, rounds) as r:
                        def before(n):
                            if n >= RING:
                                moe_unit_used(L, r, n - RING)
                            else:
                                moe_unit_used(L, r - 1, max(range(n, MOE_UNITS, RING)))
                        round_units(before)
                return rounds

            for half in range(2):
                ks = slice(half * KT // 2, (half + 1) * KT // 2)
                sp.dma_start(x_staged[:, ks, :], d["x_cols"][:, ks, :]).then_inc(xT_in[half], 16)
            for u in range(RET_UNITS):
                if u >= RET_RING:
                    ret_unit_used(u - RET_RING)
                m, cols = u // 2, slice(u % 2 * UNIT, (u % 2 + 1) * UNIT)
                load(0, u % RET_RING, (d["w_ret_in"][m] if m < 3 * HR else d["w_ret_out"][m - 3 * HR])[:, cols])
                if u == 0:
                    sp.dma_start(pos_i[:, 0:S], d["pos_row"].to_broadcast([P, S])).then_inc(trig_in, 16)
                    sp.dma_start(pos_i[:, S:S + TT], d["pos_col"]).then_inc(trig_in, 16)
                    sp.dma_start(cst[:, :], d["consts"]).then_inc(trig_in, 16)
            rounds = mixture(0, lambda n: ret_unit_used(RET_UNITS - RET_RING + n) if n < RET_RING else
                             sp.wait_ge(w_used, PIECES))
            for u in range(SWA_UNITS):
                moe_unit_used(0, rounds - 1, MOE_UNITS - RING + u)
                if u == 0:
                    src = d["w_swa_kv"]
                elif u < 5:
                    src = d["w_swa_in"][(u - 1) // 2][:, (u - 1) % 2 * UNIT:((u - 1) % 2 + 1) * UNIT]
                else:
                    src = d["w_swa_out"][:, (u - 5) * UNIT:(u - 4) * UNIT]
                load(1, (SWA_SLOT + u) % RING, src)
            mixture(1, lambda n: swa_unit_used(n - 1) if n else
                    moe_unit_used(0, rounds - 1, MOE_UNITS - 1))
            for t in range(TT):
                sp.wait_ge(x_ready, 4 * 3 + 2 * t + 2)
                sp.dma_start(out.rearrange("a (t p) n -> p (a t) n", p=P)[:, t, :],
                             x_tok[:, t, :]).then_inc(out_stored, 16)
            sp.wait_ge(out_stored, 16 * TT)

        @block.tensor
        def _(pe):
            mm = nc.tensor.matmul

            def ret_matrix(m):
                for u in (2 * m, 2 * m + 1):
                    pe.wait_ge(loaded[0][u % RET_RING], 16 * (u // RET_RING + 1))
                return ring_low[:, 2 * m % RET_RING:2 * m % RET_RING + 2, :].rearrange("p s n -> p (s n)")

            def piece(p, k):
                pe.wait_ge(w_low, p + 1)
                return w_parts[:, p % SPLIT_BUFS, :, :].rearrange("p a (k n) -> p a k n", k=k)

            def project_qk(h):
                for j in range(2):
                    if h > 0:
                        pe.wait_ge(vg_done, 4 * (h - 1) + 2 + j)
                    for half in range(2):
                        w = piece(HEAD_PIECES * h + 2 * j + half, KT)
                        for k in range(KT):
                            if h == 0 and j == 0 and half == 0 and k % (KT // 2) == 0:
                                pe.wait_ge(x_split_low, 1 + 2 * k // KT)
                            for n, (a, b) in enumerate(SPLIT_PRODUCTS):
                                last = mm(ps[:, j, half * S:(half + 1) * S], w[:, b, k, :],
                                          xT_parts[:, a, k, :], start=(k == 0 and n == 0),
                                          stop=(k == KT - 1 and n == 2))
                        last.then_inc(w_used, 1)

            def project_vg(h, j):
                if j == 1:
                    if h > 0:
                        pe.wait_ge(vg_done, 4 * h)
                    pe.wait_ge(rope_read, 2 * h + 1)
                else:
                    pe.wait_ge(rope_read, 2 * h + 2)
                    pe.wait_ge(vg_done, 4 * h + 1)
                for i in range(4):
                    w = piece(HEAD_PIECES * h + 4 * j + i, 2)
                    for t in range(TT):
                        for k in range(2):
                            for n, (a, b) in enumerate(SPLIT_PRODUCTS):
                                last = mm(ps[:, (2 * j + t) % 3, :],
                                          xT_parts[:, a, 2 * i + k, t * P:(t + 1) * P], w[:, b, k, :],
                                          start=(i == 0 and k == 0 and n == 0),
                                          stop=(i == 3 and k == 1 and n == 2))
                    last.then_inc(w_used, 1)

            def ret_score(h):
                pe.wait_ge(qk_ready, 2 * h + 2)
                if h > 0:
                    pe.wait_ge(ret_masked, h)
                q, k = qT[:, h % 2], kT[:, h % 2]
                for half in range(2):
                    mm(ps[:, 3, 0:S], k[:, half, 0:P], q[:, half, :], start=(half == 0), stop=(half == 1))
                for half in range(2):
                    last = mm(ps[:, 3, S:S + P], k[:, half, P:S], q[:, half, P:S],
                              start=(half == 0), stop=(half == 1))
                last.then_inc(ret_scores, 1)

            def ret_value(h):
                pe.wait_ge(ret_masked, h + 1)
                pe.wait_ge(vg_done, 4 * h + 2)
                if h > 0:
                    pe.wait_ge(gn_gated, 2 * h)
                pr, v = prT[:, h % 2], v_ret[:, h % 2]
                mm(ps[:, 4, :], pr[:, 0:P], v[:, 0], start=True, stop=True).then_inc(ret_o, 1)
                mm(ps[:, 5, :], pr[:, P:S], v[:, 0], start=True, stop=False)
                mm(ps[:, 5, :], pr[:, S:S + P], v[:, 1], start=False, stop=True).then_inc(ret_o, 1)

            def ret_transpose(h):
                if h == 0:
                    pe.wait_ge(trig_in, 48)
                for t in range(TT):
                    pe.wait_ge(y_ready, 2 * h + t + 1)
                    if h > 0:
                        pe.wait_ge(yT_ready, 2 * (h - 1) + t + 1)
                    for j in range(DV // P):
                        last = nc.tensor.transpose(ps[:, 6 + t, j * P:(j + 1) * P],
                                                   g_ret[:, h % 2, t, j * P:(j + 1) * P], ident)
                    last.then_inc(yT_ps, 1)

            def ret_output(h):
                w = ret_matrix(3 * HR + h).rearrange("p (k n) -> p k n", n=D)
                pe.wait_ge(yT_ready, 2 * h + 2)
                if h == 0:
                    pe.wait_ge(vg_done, 4 * HR)
                    pe.wait_ge(ret_masked, HR)
                for t in range(TT):
                    for n in range(2):
                        for k in range(DV // P):
                            last = mm(ps[:, 2 * t + n, :], yT[:, h * 4 + k, t * P:(t + 1) * P],
                                      w[:, k, n * BANK:(n + 1) * BANK], start=(h == 0 and k == 0),
                                      stop=(h == HR - 1 and k == DV // P - 1))
                        if h == HR - 1:
                            last.then_inc(mix_done, 1)
                if h < HR - 1:
                    last.then_inc(mix_out_used, 1)

            def transpose_x(n):
                for t in range(TT):
                    for half in range(2):
                        pe.wait_ge(x_ready, 4 * n + 2 * t + half + 1)
                        for j in range(4):
                            k = 4 * half + j
                            last = nc.tensor.transpose(ps[:, 4 + 2 * t + half, j * P:(j + 1) * P],
                                                       x_tok[:, t, k * P:(k + 1) * P], ident)
                        last.then_inc(xT_ps, 1)

            def mixture(L, used):
                m = M[L]
                transpose_x(2 * L)
                for t in range(TT):
                    pe.wait_ge(xT_ready, 8 * L + 2 * t + 2)
                    if t == 0:
                        pe.wait_ge(params_in, 80)
                        pe.wait_ge(z_ready, 8 * L + 4)
                    for k in range(KT):
                        last = mm(ps[:, 0, t * 32:t * 32 + NR], xT[:, k, t * P:(t + 1) * P],
                                  w_router[:, L, k, :], start=(k == 0), stop=(k == KT - 1))
                    last.then_inc(m["logits_ps"], 1)
                pe.wait_ge(tri_ready, 1)
                pe.wait_ge(m["chosen_ready"], 1)
                mm(ps[:, 1, 0:NE], tri, chosen[:, 0, :], start=True, stop=True)
                mm(ps[:, 1, NE:2 * NE], ones, chosen[:, 0, :], start=True, stop=False)
                mm(ps[:, 1, NE:2 * NE], tri, chosen[:, 1, :], start=False, stop=True)
                mm(ps[:, 1, 2 * NE:3 * NE], ones, chosen[:, 0, :], start=True, stop=False)
                mm(ps[:, 1, 2 * NE:3 * NE], ones, chosen[:, 1, :], start=False, stop=True)\
                    .then_inc(m["rank_ps"], 1)
                rounds = load_rounds(pe, L)

                def unit(i, kind, n, r):
                    u = PAIR_UNITS * i + kind
                    slot = (MOE_SLOT[L] + u) % RING
                    a_round = len(range(u % RING, MOE_UNITS, RING))
                    pe.wait_ge(loaded[L][slot], (r * a_round + u // RING + used(slot) + 1) * 16)
                    return slot_of(slot).rearrange("p (k n) -> p k n", n=n)

                def hidden(i, half, r):
                    w = [unit(i, 2 * half + e, 2 * FF, r) for e in range(2)]
                    for k in range(KT // 2):
                        for e in range(2):
                            last = mm(ps[e * SLOTS:(e + 1) * SLOTS, 4 + i % 2, :],
                                      xsT[:, half * KT // 2 + k, (2 * i + e) * SLOTS:(2 * i + e + 1) * SLOTS],
                                      w[e][:, k, :], start=(half == 0 and k == 0),
                                      stop=(half == 1 and k == KT // 2 - 1))
                    last.then_inc(m["h_done" if half else "h_half"], 1)

                def transpose_act(i, base):
                    pe.wait_ge(m["act_done"], base + i + 1)
                    for f in range(FT):
                        last = nc.tensor.transpose(ps[:, 4 + i % 2, f * P:(f + 1) * P],
                                                   act_sl[:, f * P:(f + 1) * P], ident)
                    last.then_inc(m["actT_ps"], 1)

                def project_back(i, base, r):
                    w = [unit(i, 4 + e, D, r) for e in range(2)]
                    pe.wait_ge(m["actT_ready"], base + i + 1)
                    for f in range(FT):
                        for n in range(2):
                            for e in range(2):
                                last = mm(ps[e * SLOTS:(e + 1) * SLOTS, 6 + n, :],
                                          actT[:, f, e * SLOTS:(e + 1) * SLOTS],
                                          w[e][:, f, n * BANK:(n + 1) * BANK],
                                          start=(f == 0), stop=(f == FT - 1))
                    last.then_inc(m["y_done"], 1)

                def scatter(i, base):
                    pe.wait_ge(m["y_low"], base + i + 1)
                    for t in range(TT):
                        for n in range(2):
                            for part in range(2):
                                last = mm(ps[:, 2 * t + n, :], onehotT[:, i, t * P:(t + 1) * P],
                                          y_parts[:, part, n * BANK:(n + 1) * BANK],
                                          start=(i == 0 and part == 0),
                                          stop=(i == PAIRS - 1 and part == 1))
                            if i == PAIRS - 1:
                                last.then_inc(m["sums_done"], 1)
                    if i < PAIRS - 1:
                        last.then_inc(m["scattered"], 1)

                def transpose_onehot():
                    for i in range(PAIRS):
                        for t in range(TT):
                            c = (i * TT + t) * P
                            last = nc.tensor.transpose(ps[:, c // BANK, c % BANK:c % BANK + P],
                                                       onehot[:, t, i * P:(i + 1) * P].bitcast(F32), ident)
                        if i % 2:
                            last.then_inc(m["ohT_ps"], 1)

                def gather(r, half):
                    for q in range(half * KT, (half + 1) * KT):
                        if q % KT >= 3 or half:
                            pe.wait_ge(m["gather_act" if (q - 3) % 2 == 0 else "gather_dve"],
                                       r * KT + (q - 3) // 2 + 1)
                        for part in range(2):
                            for t in range(TT):
                                last = mm(ps[:, 5 + q % 3, :],
                                          x_parts[:, part, t, q % KT * P:(q % KT + 1) * P],
                                          onehot[:, t, half * BANK:(half + 1) * BANK],
                                          start=(part == 0 and t == 0), stop=(part == 1 and t == TT - 1))
                        last.then_inc(m["gather_ps"], 1)

                def slot_weights():
                    pe.wait_ge(m["combine_ready"], 1)
                    for i in range(PAIRS):
                        for t in range(TT):
                            last = mm(ps[:, 0, 2 * i:2 * i + 2],
                                      onehot[:, t, i * P:(i + 1) * P].bitcast(F32),
                                      combine[:, t, 2 * i:2 * i + 2], start=(t == 0), stop=(t == TT - 1))
                    last.then_inc(m["cw_ps"], 1)

                with pe.Fori(0, rounds) as r:
                    base = r * PAIRS
                    pe.wait_ge(m["onehot_ready"], r + 1)
                    pe.wait_ge(m["x_low"], TT)
                    gather(r, 0)
                    for i in range(PAIRS):
                        if i in (0, PAIRS // 2 - 1):
                            half = 2 * (i + 1) // PAIRS
                            pe.wait_ge(m["gather_act"], r * KT + (half + 1) * KT // 2)
                            pe.wait_ge(m["gather_dve"], r * KT + (half + 1) * KT // 2)
                        hidden(i, 0, r)
                        if i == 0:
                            slot_weights()
                        else:
                            transpose_act(i - 1, base)
                            if i == 2:
                                pe.wait_ge(m["ohT_ready"], r * 4 + 4)
                            if i > 1:
                                scatter(i - 2, base)
                            project_back(i - 1, base, r)
                        if i == PAIRS // 2 - 2:
                            pe.wait_ge(m["y_low"], base + i)
                            gather(r, 1)
                        hidden(i, 1, r)
                        if i == 0:
                            pe.wait_ge(m["cw_ready"], r + 1)
                            transpose_onehot()
                    transpose_act(PAIRS - 1, base)
                    scatter(PAIRS - 2, base)
                    project_back(PAIRS - 1, base, r)
                    scatter(PAIRS - 1, base)

            def attention():
                transpose_x(1)
                for u in range(3):
                    n = BANK if u else 2 * KVH * HD
                    first, end = ((0, 1), (1, 3), (3, 5))[u]
                    w = []
                    for i in range(first, end):
                        pe.wait_ge(loaded[1][(SWA_SLOT + i) % RING], 16)
                        w.append(slot_of((SWA_SLOT + i) % RING).rearrange("p (k n) -> p k n", n=n))
                    in_unit = KT // len(w)
                    for t in range(TT):
                        if u == 0:
                            pe.wait_ge(xT_ready, 4 + 2 * t + 2)
                        if u == 0:
                            pe.wait_ge(xT_ready, 4 + 4)
                        if u == 1 and t == 0:
                            pe.wait_ge(z_ready, 8)
                        for k in range(KT):
                            last = mm(ps[:, (4, 0, 2)[u] + t, 0:n], xT[:, k, t * P:(t + 1) * P],
                                      w[k // in_unit][:, k % in_unit, :],
                                      start=(k == 0), stop=(k == KT - 1))
                        last.then_inc(sproj_done, 1)
                for t in range(TT):
                    pe.wait_ge(rot_done, 5 + t)
                    for i in range(HPG):
                        last = nc.tensor.transpose(
                            ps[:, (6, 0)[t] + i // 4, (i % 4) * P:(i % 4 + 1) * P],
                            q_rows[:, t, i * P:(i + 1) * P], ident)
                        if i % 4 == 3:
                            last.then_inc(sqk_ps, 1)
                    nc.tensor.transpose(ps[:, 4 + t, 0:P], q_rows[:, t, HS * HD:QKW], ident)\
                        .then_inc(sqk_ps, 1)

                def scores(c):
                    width = P if c else CHUNK
                    start = (0, 0, 4 * CHUNK, 2 * CHUNK)[c]
                    if c == 0:
                        pe.wait_ge(sqk_ready, 4 * TT)
                    if c >= 2:
                        pe.wait_ge(exp_done, c - 1)
                    for kv in range(KVH):
                        rows = slice(kv * HD, (kv + 1) * HD)
                        for pair in range(HPG // 2):
                            last = mm(ps[:, 2 + 2 * (c % 2) + kv, pair * P:pair * P + width],
                                      sqT[rows, c, 2 * pair:2 * pair + 2, :].rearrange("p a n -> p (a n)"),
                                      skT[rows, start:start + width], start=True, stop=True)
                    last.then_inc(swa_scores, 1)

                def transpose_probs(c):
                    width = P if c else CHUNK
                    pe.wait_ge(probs_ready, c + 1)
                    if c >= 1:
                        pe.wait_ge(probsT_ready, 2 * c)
                    for i in range(8):
                        last = nc.tensor.transpose(ps[0:width, 6 + i // 4, (i % 4) * P:(i % 4 + 1) * P],
                                                   probs[:, c % 2, i, 0:width], ident)
                    last.then_inc(probsT_ps, 1)

                def values(c):
                    width = P if c else CHUNK
                    pe.wait_ge(probsT_ready, 2 * c + 2)
                    if c >= 2:
                        pe.wait_ge(oT_ready, c - 1)
                    for kv in range(KVH):
                        last = mm(ps[kv * HD:(kv + 1) * HD, c % 2, :],
                                  v_win[0:width, (0, 0, 2, 1)[c], kv * HD:(kv + 1) * HD],
                                  probsT[0:width, 4 * kv:4 * kv + 4, :], start=True, stop=True)
                    last.then_inc(pv_done, 1)

                scores(0)
                scores(1)
                for c in range(4):
                    if c + 2 < 4:
                        scores(c + 2)
                    transpose_probs(c)
                    values(c)
                pe.wait_ge(oT_ready, 4)
                for u in range(4):
                    first, n = 2 * u, 2
                    slot = (SWA_SLOT + 5 + u) % RING
                    pe.wait_ge(loaded[1][slot], 16)
                    w = slot_of(slot).rearrange("p (k n) -> p k n", n=D)
                    for t in range(TT):
                        for half in range(2):
                            for k in range(n):
                                last = mm(ps[:, 2 * t + half, :], oT[:, first + k, t * P:(t + 1) * P],
                                          w[:, k, half * BANK:(half + 1) * BANK],
                                          start=(first + k == 0), stop=(first + k == HPG - 1))
                            if u == 3:
                                last.then_inc(mix_done, 1)
                    if u < 3:
                        last.then_inc(mix_out_used, 1)

            for h in range(HR):
                project_qk(h)
                if h > 0:
                    ret_score(h - 1)
                project_vg(h, 1)
                if h > 0:
                    ret_value(h - 1)
                project_vg(h, 2)
                if h > 0:
                    ret_transpose(h - 1)
            ret_score(HR - 1)
            ret_value(HR - 1)
            ret_output(0)
            ret_output(1)
            ret_transpose(HR - 1)
            ret_output(2)
            ret_output(3)
            mixture(0, lambda slot: len(range(slot, RET_UNITS, RET_RING)) if slot < RET_RING else 0)
            attention()
            mixture(1, lambda slot: int((slot - SWA_SLOT) % RING < SWA_UNITS))

        @block.scalar
        def _(act):
            af = nc.scalar.activation
            def rotary_tables():
                act.wait_ge(angles_done, 1)
                af(sin[:, :], angle, ACT.Sin).then_inc(trig_done, 1)
                act.wait_ge(angles_done, 2)
                af(cos[:, :], turns, ACT.Sin).then_inc(trig_done, 1)
                act.dma_start(decay, d["decay"]).then_inc(decay_in, 16)
                act.dma_start(gn_gain[:, :], d["gn_gain"]).then_inc(params_in, 16)
                act.dma_start(w_router[:, :, :, :], d["w_router"]).then_inc(params_in, 16)
                act.dma_start(b_router[:, :, :].rearrange("p l n -> p (l n)"),
                              d["b_router"].to_broadcast([P, 2 * NR])).then_inc(params_in, 16)
                act.dma_start(sinks[:, :], d["sinks"]).then_inc(params_in, 16)
                act.dma_start(swa_bias[:, :], d["swa_bias"].to_broadcast([P, SWA_IN])).then_inc(params_in, 16)
                act.dma_start(x_tok[:, :, :], d["x_rows"]).then_inc(x_in, 16)

            def split_high(p):
                u = p // 2
                act.wait_ge(loaded[0][u % RET_RING], 16 * (u // RET_RING + 1))
                if p >= SPLIT_BUFS:
                    act.wait_ge(w_used, p - SPLIT_BUFS + 1)
                af(w_parts[:, p % SPLIT_BUFS, 0, :], ring_low[:, u % RET_RING, p % 2 * PIECE:(p % 2 + 1) * PIECE],
                   ACT.Copy).then_inc(w_high, 1)

            def copy_out(h, j, t):
                act.wait_ge(w_used, HEAD_PIECES * h + 4 * (j + 1))
                if h >= 2 and t == 0:
                    if j == 1:
                        act.wait_ge(ret_o, 2 * (h - 1))
                    else:
                        act.wait_ge(yT_ps, 2 * (h - 1))
                dst = (v_ret if j == 1 else g_ret)[:, h % 2, t, :]
                af(dst, ps[:, (2 * j + t) % 3, :], ACT.Copy if j == 1 else ACT.Silu)\
                    .then_inc(vg_done, 1)

            def scale_y(h):
                for t in range(TT):
                    act.wait_ge(gn_gated, 2 * h + t + 1)
                    act.wait_ge(gn_rstd, 2 * h + t + 1)
                    y = g_ret[:, h % 2, t, :]
                    af(y, y, ACT.Copy, scale=rstd[:, t:t + 1]).then_inc(y_ready, 1)

            for half in range(2):
                ks = slice(half * KT // 2, (half + 1) * KT // 2)
                act.wait_ge(xT_in[half], 16)
                af(xT_parts[:, 0, ks, :], x_staged[:, ks, :], ACT.Copy).then_inc(x_split_high, 1)
                split_high(half)
            for p in range(PIECES):
                h, step = divmod(p, HEAD_PIECES)
                if p + SPLIT_BUFS - 1 < PIECES:
                    split_high(p + SPLIT_BUFS - 1)
                if p == 1:
                    rotary_tables()
                if step == 0 and h > 0:
                    copy_out(h - 1, 2, 0)
                    copy_out(h - 1, 2, 1)
                if step == 8:
                    copy_out(h, 1, 0)
                    copy_out(h, 1, 1)
                if step == 10 and h > 0:
                    scale_y(h - 1)
            copy_out(HR - 1, 2, 0)
            copy_out(HR - 1, 2, 1)
            scale_y(HR - 1)

            def copy_xT(n, t):
                for half in range(2):
                    act.wait_ge(xT_ps, 4 * n + 2 * t + half + 1)
                    af(xT[:, 4 * half:4 * half + 4, t * P:(t + 1) * P],
                       ps[:, 4 + 2 * t + half, :].rearrange("p (k n) -> p k n", n=P), ACT.Copy)\
                        .then_inc(xT_ready, 1)

            def mixture(L):
                m = M[L]
                for t in range(TT):
                    copy_xT(2 * L, t)
                    af(x_parts[:, 0, t, :], x_tok[:, t, :], ACT.Copy).then_inc(m["x_high"], 1)
                act.wait_ge(x_ready, 8 * L + 4)
                af(z[:, :, :], x_tok[:, :, :], ACT.Copy, scale=ALPHA).then_inc(m["z_scaled"], 1)
                act.wait_ge(m["exp_arg"], 1)
                af(r_exp[:, :, :], r_diff[:, :, :], ACT.Exp).then_inc(m["exp_val"], 1)
                act.wait_ge(m["exp_arg"], 2)
                af(r_et[:, :, :], r_dt[:, :, :], ACT.Exp).then_inc(m["exp_val"], 1)
                rounds = load_rounds(act, L)
                with act.Fori(0, rounds) as r:
                    def gathered(half):
                        for q in range(half * KT, (half + 1) * KT, 2):
                            act.wait_ge(m["gather_ps"], r * 2 * KT + q + 1)
                            af(xsT[:, q % KT, half * BANK:(half + 1) * BANK], ps[:, 5 + q % 3, :],
                               ACT.Copy).then_inc(m["gather_act"], 1)

                    gathered(0)
                    for i in range(PAIRS + 1):
                        if i > 0:
                            act.wait_ge(m["y_done"], r * PAIRS + i)
                            if i > 1:
                                act.wait_ge(m["scattered"], r * (PAIRS - 1) + i - 1)
                            for n in range(2):
                                af(y_parts[:, 0, n * BANK:(n + 1) * BANK], ps[:, 6 + n, :], ACT.Copy)\
                                    .then_inc(m["y_high"], 1)
                        if i == PAIRS // 2 - 2:
                            gathered(1)
                        if i < PAIRS:
                            act.wait_ge(m["h_done"], r * PAIRS + i + 1)
                            af(silu_a, ps[:, 4 + i % 2, 0:FF], ACT.Silu).then_inc(m["silu_done"], 1)
                        if i == 0:
                            for j in range(4):
                                act.wait_ge(m["ohT_ps"], r * 4 + j + 1)
                                af(onehotT[:, 2 * j:2 * j + 2, :],
                                   ps[:, j, :].rearrange("p (g n) -> p g n", n=S), ACT.Copy)\
                                    .then_inc(m["ohT_ready"], 1)

            mixture(0)

            for t in range(TT):
                copy_xT(1, t)
            for t in range(TT):
                for half in range(2):
                    act.wait_ge(sqk_ps, 3 * t + half + 1)
                    af(sqT[:, 2 * t:2 * t + 2, 4 * half:4 * half + 4, :].rearrange("p c i n -> p i c n"),
                       ps[:, (6, 0)[t] + half, :].rearrange("p (i c n) -> p i c n", i=4, c=2), ACT.Copy)\
                        .then_inc(sqk_ready, 1)
                act.wait_ge(sqk_ps, 3 * t + 3)
                af(skT[:, t * P:(t + 1) * P], ps[:, 4 + t, 0:P], ACT.Copy).then_inc(sqk_ready, 1)
                at, of = ((5, CHUNK), (4, 0))[t]
                af(skT[:, at * CHUNK:(at + 1) * CHUNK], ps[:, 4 + t, of:of + CHUNK], ACT.Copy)\
                    .then_inc(sqk_ready, 1)
            for c in range(4):
                width = P if c else CHUNK
                act.wait_ge(max_done, c + 1)
                if c >= 2:
                    act.wait_ge(probsT_ps, c - 1)
                for i in range(8):
                    af(probs[:, c % 2, i, 0:width], ps[:, 2 + 2 * (c % 2) + i // 4, (i % 4) * P:(i % 4) * P + width],
                       ACT.Exp, bias=s_negm[:, c % 2, i:i + 1], scale=HD ** -0.5, accum_out=s_sum[:, c % 2, i:i + 1])
                af(s_esink[:, c % 2, :], s_dsink[:, c % 2, :], ACT.Exp).then_inc(exp_done, 1)
            mixture(1)

        @block.vector
        def _(dve):
            tt, ts = nc.vector.tensor_tensor, nc.vector.tensor_scalar
            stt = nc.vector.scalar_tensor_tensor
            steps = [0]

            def then(ins):
                steps[0] += 1
                ins.then_inc(dve_step, 1)
                dve.wait_ge(dve_step, steps[0])

            def split_low(p):
                dve.wait_ge(w_high, p + 1)
                u, b = p // 2, p % SPLIT_BUFS
                tt(w_parts[:, b, 1, :], ring_low[:, u % RET_RING, p % 2 * PIECE:(p % 2 + 1) * PIECE],
                   w_parts[:, b, 0, :].bitcast(F32), ALU.subtract).then_inc(w_low, 1)

            for half in range(2):
                ks = slice(half * KT // 2, (half + 1) * KT // 2)
                dve.wait_ge(x_split_high, half + 1)
                tt(xT_parts[:, 1, ks, :], x_staged[:, ks, :], xT_parts[:, 0, ks, :].bitcast(F32),
                   ALU.subtract).then_inc(x_split_low, 1)
                split_low(half)

            dve.wait_ge(trig_in, 48)
            then(nc.vector.tensor_copy(turns[:, 0:S + TT], pos_i[:, :]))
            ts(angle[:, 0:S], turns[:, 0:S], cst[:, C_FREQ_R:C_FREQ_R + 1], None, ALU.mult)
            for t in range(TT):
                last = ts(angle[:, S + 32 * t:S + 32 * (t + 1)], cst[:, C_FREQ_S:C_FREQ_S + 32],
                          turns[:, S + t:S + t + 1], None, ALU.mult)
            then(last)
            then(ts(turns, angle, 1.0 / TWO_PI, ROUND_MAGIC, ALU.mult, ALU.add))
            then(ts(turns, turns, ROUND_MAGIC, None, ALU.subtract))
            for part in (TWO_PI_A, TWO_PI_B, TWO_PI_C):
                then(stt(angle, turns, -part, angle, ALU.mult, ALU.add))
            then(ts(angle, angle, PI_BELOW, -PI_BELOW, ALU.min, ALU.max))
            stt(turns, angle, -1.0, angle, ALU.mult, ALU.min).then_inc(angles_done, 1)
            dve.wait_ge(angles_done, 1)
            ts(turns, turns, np.pi / 2, None, ALU.add).then_inc(angles_done, 1)

            nc.vector.tensor_copy(tri_ones[:, :], cst[:, C_TRI:C_TRI + 2 * P]).then_inc(tri_ready, 1)

            def rotate(h, j):
                if h == 0 and j == 0:
                    dve.wait_ge(trig_done, 2)
                dve.wait_ge(w_used, HEAD_PIECES * h + 2 * j + 2)
                if h or j:
                    dve.wait_ge(qk_ready, 2 * h + j)
                x = ps[:, j, :].rearrange("p (a n) -> p a n", a=2)
                tt(rotA, x, cos[:, 0:S].unsqueeze(1).to_broadcast([P, 2, S]), ALU.mult)
                tt(rotB, x, sin[:, 0:S].unsqueeze(1).to_broadcast([P, 2, S]), ALU.mult)\
                    .then_inc(rope_read, 1)
                dve.wait_ge(rope_read, 2 * h + j + 1)
                if h >= 2:
                    dve.wait_ge(ret_scores, h - 1)
                dst = (qT if j == 0 else kT)[:, h % 2]
                tt(dst[:, 0], rotA[:, 0], rotB[:, 1], ALU.subtract)
                tt(dst[:, 1], rotB[:, 0], rotA[:, 1], ALU.add).then_inc(qk_ready, 1)

            def mask(h):
                dve.wait_ge(ret_scores, h + 1)
                if h == 0:
                    dve.wait_ge(decay_in, 16)
                if h >= 2:
                    dve.wait_ge(ret_o, 2 * (h - 1))
                tt(prT[:, h % 2], ps[:, 3, 0:3 * P], decay[:, h], ALU.mult).then_inc(ret_masked, 1)

            def norm_gate(h):
                for t in range(TT):
                    dve.wait_ge(ret_o, 2 * h + t + 1)
                    then(nc.vector.bn_stats(stats[:, t, 0, :], ps[:, 4 + t, :]))
                    if h > 0:
                        dve.wait_ge(gn_rstd, 2 * h)
                    nc.vector.bn_aggr(mean_var[:, t, :], stats[:, t, 0, :]).then_inc(gn_stats, 1)
                for t in range(TT):
                    dve.wait_ge(gn_stats, 2 * h + t + 1)
                    dve.wait_ge(vg_done, 4 * h + 2 + t + 1)
                    y = g_ret[:, h % 2, t, :]
                    stt(y, ps[:, 4 + t, :], mean_var[:, t, 0:1], y, ALU.subtract, ALU.mult)\
                        .then_inc(gn_gated, 1)

            def copy_yT(h):
                for t in range(TT):
                    dve.wait_ge(yT_ps, 2 * h + t + 1)
                    if h == 0 and t == 0:
                        dve.wait_ge(params_in, 80)
                    tt(yT[:, 4 * h:4 * h + 4, t * P:(t + 1) * P],
                       ps[:, 6 + t, :].rearrange("p (k n) -> p k n", n=P),
                       gn_gain[:, 4 * h:4 * h + 4].unsqueeze(2).to_broadcast([P, 4, P]), ALU.mult)\
                        .then_inc(yT_ready, 1)

            for p in range(PIECES):
                h, step = divmod(p, HEAD_PIECES)
                if p + SPLIT_BUFS - 1 < PIECES:
                    split_low(p + SPLIT_BUFS - 1)
                if step == 1 and h > 1:
                    copy_yT(h - 2)
                if step in (2, 4):
                    rotate(h, step // 2 - 1)
                if step == 5 and h > 0:
                    mask(h - 1)
                if step == 8 and h > 0:
                    norm_gate(h - 1)
            copy_yT(HR - 2)
            mask(HR - 1)
            norm_gate(HR - 1)
            copy_yT(HR - 1)

            def mixer_residual(L):
                for i in range(4):
                    dve.wait_ge(mix_done, 4 * L + i + 1)
                    if L == 0 and i == 0:
                        dve.wait_ge(x_in, 16)
                    cols = slice((i % 2) * BANK, (i % 2 + 1) * BANK)
                    stt(z[:, i // 2, cols], x_tok[:, i // 2, cols], ALPHA, ps[:, i, :],
                        ALU.mult, ALU.add).then_inc(z_ready, 1)

            def layer_norm(n):
                for t in range(TT):
                    dve.wait_ge(z_ready, 4 * n + 2 * t + 2)
                    for half in range(2):
                        last = nc.vector.bn_stats(stats[:, t, half, :],
                                                  z[:, t, half * BANK:(half + 1) * BANK])
                    then(last)
                    nc.vector.bn_aggr(mean_var[:, t, :], stats[:, t, :, :].rearrange("p a b -> p (a b)"))\
                        .then_inc(ln_stats, 1)
                    dve.wait_ge(ln_stats, 2 * n + t + 1)
                    if t == 0:
                        dve.wait_ge(ln_in, 16 * (n + 1))
                    then(stt(z[:, t, :], z[:, t, :], mean_var[:, t, 0:1], ln_rows[:, 0, :],
                             ALU.subtract, ALU.mult))
                    dve.wait_ge(ln_rstd, 2 * n + t + 1)
                    for half in range(2):
                        cols = slice(half * BANK, (half + 1) * BANK)
                        stt(x_tok[:, t, cols], z[:, t, cols], rstd[:, t:t + 1], ln_rows[:, 1, cols],
                            ALU.mult, ALU.add).then_inc(x_ready, 1)

            def by_row(a):
                return a[:, :, :].rearrange("p t (r n) -> p (t r) n", n=G)

            def over_row(a):
                return a[:, :, :].rearrange("p t r -> p (t r)").unsqueeze(2)\
                    .to_broadcast([P, TT * (1 + G), G])

            def first_max(dst, top, values):
                then(nc.vector.tensor_reduce(top[:, :, :].rearrange("p t r -> p (t r)"), by_row(values),
                                             AX.X, ALU.max))
                then(tt(by_row(r_eq), by_row(values), over_row(top), ALU.is_equal))
                then(tt(by_row(r_eq), by_row(r_eq),
                        tie.unsqueeze(1).to_broadcast([P, TT * (1 + G), G]), ALU.mult))
                then(nc.vector.tensor_reduce(r_tie[:, :, :].rearrange("p t r -> p (t r)"), by_row(r_eq),
                                             AX.X, ALU.max))
                then(tt(by_row(dst), by_row(r_eq), over_row(r_tie), ALU.is_equal))

            def mixture(L):
                m = M[L]
                for t in range(TT):
                    dve.wait_ge(m["x_high"], t + 1)
                    tt(x_parts[:, 1, t, :], x_tok[:, t, :], x_parts[:, 0, t, :].bitcast(F32),
                       ALU.subtract).then_inc(m["x_low"], 1)
                dve.wait_ge(m["logits_ps"], 2)
                then(tt(logits[:, :, :], ps[:, 0, 0:2 * 32].rearrange("p (t n) -> p t n", t=TT)[:, :, 0:NR],
                        b_router[:, L:L + 1, :].to_broadcast([P, TT, NR]), ALU.add))
                first_max(oh_first, r_first, logits)
                tt(r_diff[:, :, :], logits[:, :, 0:G], r_first[:, :, 0:1].to_broadcast([P, TT, G]),
                   ALU.subtract).then_inc(m["exp_arg"], 1)
                then(stt(r_rest[:, :, :], oh_first[:, :, :], -3e38, logits[:, :, :], ALU.mult, ALU.add))
                first_max(oh_second, r_second, r_rest)
                of_group = oh_first[:, :, 0:G].unsqueeze(3).to_broadcast([P, TT, G, E])
                then(tt(picked[:, :, :], oh_first[:, :, G:NR], oh_second[:, :, G:NR], ALU.add))
                tt(chosen[:, :, :].rearrange("p t (g e) -> p t g e", g=G), of_group,
                   picked[:, :, :].rearrange("p t (g e) -> p t g e", g=G), ALU.mult)\
                    .then_inc(m["chosen_ready"], 1)
                tt(r_dt[:, :, :], r_second[:, :, :], r_first[:, :, :], ALU.subtract)\
                    .then_inc(m["exp_arg"], 1)
                dve.wait_ge(m["rank_ps"], 1)
                dve.wait_ge(m["chosen_ready"], 1)
                stt(key[:, :, :].rearrange("p t g -> p (t g)"), ps[:, 1, 0:TT * NE], 1.0,
                    chosen[:, :, :].rearrange("p t g -> p (t g)"), ALU.add, ALU.mult)\
                    .then_inc(m["keys_ready"], 1)
                then(nc.vector.tensor_reduce(n_over[0:1, 0:1], ps[0:1, 1, 2 * NE:3 * NE], AX.X, ALU.max))
                then(tt(n_over[0:1, 1:ROUNDS_MAX], cst[0:1, C_OVER:C_OVER + ROUNDS_MAX - 1],
                        n_over[0:1, 0:1].to_broadcast([1, ROUNDS_MAX - 1]), ALU.is_lt))
                then(nc.vector.tensor_reduce(n_over[0:1, ROUNDS_MAX:ROUNDS_MAX + 1],
                                             n_over[0:1, 1:ROUNDS_MAX], AX.X, ALU.add))
                nc.vector.tensor_copy(more_rounds[0:1, 0:1], n_over[0:1, ROUNDS_MAX:ROUNDS_MAX + 1])\
                    .then_inc(m["rounds_ready"], 1)

                def token_to_slot(r):
                    dve.wait_ge(m["keys_ready"], r + 1)
                    for t in range(TT):
                        last = tt(onehot[:, t, :].rearrange("p (e n) -> p e n", n=SLOTS),
                                  iota.unsqueeze(1).to_broadcast([P, NE, SLOTS]),
                                  key[:, t, :].unsqueeze(2).to_broadcast([P, NE, SLOTS]), ALU.is_equal)
                    last.then_inc(m["onehot_ready"], 1)

                token_to_slot(0)
                dve.wait_ge(m["exp_val"], 1)
                then(nc.vector.tensor_reduce(r_gate[:, :], r_exp[:, :, :], AX.X, ALU.add))
                then(nc.vector.reciprocal(r_gate[:, :], r_gate[:, :]))
                dve.wait_ge(m["exp_val"], 2)
                then(ts(r_w1[:, :, :], r_et[:, :, :], 1.0, None, ALU.add))
                then(nc.vector.reciprocal(r_w1[:, :, :], r_w1[:, :, :]))
                then(tt(r_w1[:, :, :], r_w1[:, :, :],
                        r_gate[:, :].unsqueeze(2).to_broadcast([P, TT, 1 + G]), ALU.mult))
                then(tt(r_w2[:, :, :], r_w1[:, :, :], r_et[:, :, :], ALU.mult))
                tt(by_row(r_eq), by_row(oh_first), over_row(r_w1), ALU.mult)
                then(tt(by_row(oh_second), by_row(oh_second), over_row(r_w2), ALU.mult))
                then(tt(weight[:, :, :], r_eq[:, :, G:NR], oh_second[:, :, G:NR], ALU.add))
                tt(combine[:, :, :].rearrange("p t (g e) -> p t g e", g=G), of_group,
                   weight[:, :, :].rearrange("p t (g e) -> p t g e", g=G), ALU.mult)\
                    .then_inc(m["combine_ready"], 1)
                rounds = load_rounds(dve, L)
                with dve.Fori(0, rounds) as r:
                    def gathered(half):
                        for q in range(half * KT + 1, (half + 1) * KT, 2):
                            dve.wait_ge(m["gather_ps"], r * 2 * KT + q + 1)
                            nc.vector.tensor_copy(xsT[:, q % KT, half * BANK:(half + 1) * BANK],
                                                  ps[:, 5 + q % 3, :]).then_inc(m["gather_dve"], 1)

                    gathered(0)
                    dve.wait_ge(m["cw_ps"], r + 1)
                    for e in range(2):
                        rows = slice(e * SLOTS, (e + 1) * SLOTS)
                        both = ps[rows, 0, 0:NE].rearrange("p (i e) -> p i e", e=2)
                        last = nc.vector.tensor_copy(cw_slots[rows, :], both[:, :, e])
                    last.then_inc(m["cw_ready"], 1)
                    for i in range(PAIRS + 1):
                        n = r * PAIRS + i
                        if i > 0:
                            dve.wait_ge(m["actT_ps"], n)
                            nc.vector.tensor_copy(actT, ps[:, 4 + (i - 1) % 2, 0:FT * P]
                                                  .rearrange("p (f n) -> p f n", n=P))\
                                .then_inc(m["actT_ready"], 1)
                        if i > 0:
                            for b in range(2):
                                cols = slice(b * BANK, (b + 1) * BANK)
                                dve.wait_ge(m["y_high"], 2 * n - 1 + b)
                                last = tt(y_parts[:, 1, cols], ps[:, 6 + b, :],
                                          y_parts[:, 0, cols].bitcast(F32), ALU.subtract)
                            last.then_inc(m["y_low"], 1)
                        if i == PAIRS // 2 - 2:
                            gathered(1)
                        if i < PAIRS:
                            dve.wait_ge(m["silu_done"], n + 1)
                            if i == 0:
                                dve.wait_ge(m["cw_ready"], r + 1)
                            stt(act_sl, ps[:, 4 + i % 2, FF:2 * FF], cw_slots[:, i:i + 1], silu_a,
                                ALU.mult, ALU.mult).then_inc(m["act_done"], 1)
                        if i == PAIRS // 2:
                            dve.wait_ge(m["onehot_ready"], r + 1)
                            ts(key[:, :, :], key[:, :, :], -float(SLOTS), None, ALU.add)\
                                .then_inc(m["keys_ready"], 1)
                            token_to_slot(r + 1)
                    dve.wait_ge(m["z_scaled"], 1)
                    for i in range(4):
                        cols = slice((i % 2) * BANK, (i % 2 + 1) * BANK)
                        dve.wait_ge(m["sums_done"], r * 4 + i + 1)
                        last = tt(z[:, i // 2, cols], z[:, i // 2, cols], ps[:, i, :], ALU.add)
                    last.then_inc(m["z_added"], 1)
                    dve.wait_ge(m["z_added"], r + 1)
                for i in range(4):
                    nc.vector.nop().then_inc(z_ready, 1)

            mixer_residual(0)
            layer_norm(0)
            mixture(0)
            layer_norm(1)

            for n in range(6):
                part, t = n // 2, n % 2
                dve.wait_ge(sproj_done, n + 1)
                if n >= 2:
                    dve.wait_ge(rotB_done, n - 1)
                    dve.wait_ge(rot_done, n - 1)
                heads = HPG if part else KVH
                width = heads * HD
                bank = (4, 0, 2)[part] + t
                cols = slice((HS * HD, 0, BANK)[part], (HS * HD, 0, BANK)[part] + width)
                x = unrotated[:, n % 2, 0:width]
                tt(x, ps[:, bank, 0:width], swa_bias[:, cols], ALU.add).then_inc(sproj_read, 1)
                if part == 0:
                    for win, rows in (((0, slice(0, P)), (2, slice(CHUNK, P))),
                                      ((1, slice(0, P)), (2, slice(0, CHUNK))))[t]:
                        tt(v_win[rows, win, :], ps[rows, bank, KVH * HD:2 * KVH * HD],
                           swa_bias[rows, QKW:SWA_IN], ALU.add)
                dve.wait_ge(sproj_read, n + 1)
                c = cos[:, S + 32 * t:S + 32 * (t + 1)].unsqueeze(1).to_broadcast([P, 2 * heads, 32])
                a, b = rot_cos[:, n % 2, 0:width], rot_sin[:, n % 2, 0:width]
                then(tt(a.rearrange("p (h n) -> p h n", n=32), x.rearrange("p (h n) -> p h n", n=32), c,
                        ALU.mult))
                dve.wait_ge(rotB_done, n + 1)
                a = a.rearrange("p (h a n) -> p h a n", a=2, n=32)
                b = b.rearrange("p (h a n) -> p h a n", a=2, n=32)
                if part:
                    y = q_rows[:, t, 0:HS * HD].rearrange("p (i g a n) -> p g i a n", i=HPG, g=KVH,
                                                          a=2)[:, part - 1]
                else:
                    y = q_rows[:, t, HS * HD:QKW].rearrange("p (h a n) -> p h a n", a=2, n=32)
                tt(y[:, :, 0, :], a[:, :, 0, :], b[:, :, 1, :], ALU.subtract)
                tt(y[:, :, 1, :], b[:, :, 0, :], a[:, :, 1, :], ALU.add).then_inc(rot_done, 1)

            def row_max(c):
                width = P if c else CHUNK
                s = ps[:, 2 + 2 * (c % 2):4 + 2 * (c % 2), :].rearrange("p b (i n) -> p (b i) n", n=P)
                dve.wait_ge(swa_scores, c + 1)
                then(nc.vector.tensor_reduce(s_max[:, :], s[:, :, 0:width], AX.X, ALU.max))
                then(stt(s_max[:, :], s_max[:, :], HD ** -0.5, sinks[:, :], ALU.mult, ALU.max))
                then(ts(s_negm[:, c % 2, :], s_max[:, :], -1.0, None, ALU.mult))
                tt(s_dsink[:, c % 2, :], sinks[:, :], s_negm[:, c % 2, :], ALU.add)\
                    .then_inc(max_done, 1)

            row_max(0)
            row_max(1)
            for c in range(4):
                width = P if c else CHUNK
                dve.wait_ge(exp_done, c + 1)
                then(tt(s_rden[:, :], s_sum[:, c % 2, :], s_esink[:, c % 2, :], ALU.add))
                then(nc.vector.reciprocal(s_rden[:, :], s_rden[:, :]))
                tt(probs[:, c % 2, :, 0:width], probs[:, c % 2, :, 0:width],
                   s_rden[:, :].unsqueeze(2).to_broadcast([P, 8, width]), ALU.mult)\
                    .then_inc(probs_ready, 1)
                if c + 2 < 4:
                    row_max(c + 2)
                dve.wait_ge(probsT_ps, c + 1)
                if c:
                    dve.wait_ge(pv_done, c)
                for half in range(2):
                    nc.vector.tensor_copy(probsT[0:width, 4 * half:4 * half + 4, :],
                                          ps[0:width, 6 + half, :].rearrange("p (i n) -> p i n", n=P))\
                        .then_inc(probsT_ready, 1)
                dve.wait_ge(pv_done, c + 1)
                nc.vector.tensor_copy(oT[:, :, c * CHUNK:(c + 1) * CHUNK],
                                      ps[:, c % 2, :].rearrange("p (i n) -> p i n", n=CHUNK))\
                    .then_inc(oT_ready, 1)
            mixer_residual(1)
            layer_norm(2)
            mixture(1)
            layer_norm(3)

        @block.gpsimd
        def _(pool):
            nc.gpsimd.memset(minus_half[:, :], -0.5).then_inc(pool_const, 1)
            pool.wait_ge(w_used, 4)
            pool.dma_start(ln_rows[:, :, :], d["ln_rows"][0:1].to_broadcast([P, 2, D])).then_inc(ln_in, 16)
            pool.wait_ge(pool_const, 1)
            count = [1]

            def inverse_std(t):
                nc.gpsimd.tensor_scalar(var_eps[:, t:t + 1], mean_var[:, t, 1:2], LN_EPS, None, ALU.add)\
                    .then_inc(pool_const, 1)
                count[0] += 1
                pool.wait_ge(pool_const, count[0])
                return nc.gpsimd.tensor_tensor(rstd[:, t:t + 1], var_eps[:, t:t + 1], minus_half[:, :],
                                               ALU.pow)

            for h in range(HR):
                for t in range(TT):
                    pool.wait_ge(gn_stats, 2 * h + t + 1)
                    if h > 0:
                        pool.wait_ge(y_ready, 2 * (h - 1) + t + 1)
                    inverse_std(t).then_inc(gn_rstd, 1)

            def layer_norm(n):
                for t in range(TT):
                    pool.wait_ge(ln_stats, 2 * n + t + 1)
                    if n == 0:
                        pool.wait_ge(y_ready, 2 * HR)
                    inverse_std(t).then_inc(ln_rstd, 1)
                if n < 3:
                    pool.wait_ge(x_ready, 4 * n + 4)
                    pool.dma_start(ln_rows[:, :, :], d["ln_rows"][n + 1:n + 2].to_broadcast([P, 2, D]))\
                        .then_inc(ln_in, 16)

            layer_norm(0)
            layer_norm(1)
            for n in range(6):
                pool.wait_ge(sproj_read, n + 1)
                if n >= 2:
                    pool.wait_ge(rot_done, n - 1)
                heads = HPG if n // 2 else KVH
                t = n % 2
                s = sin[:, S + 32 * t:S + 32 * (t + 1)].unsqueeze(1).to_broadcast([P, 2 * heads, 32])
                nc.gpsimd.tensor_tensor(
                    rot_sin[:, n % 2, 0:heads * HD].rearrange("p (h n) -> p h n", n=32),
                    unrotated[:, n % 2, 0:heads * HD].rearrange("p (h n) -> p h n", n=32), s, ALU.mult)\
                    .then_inc(rotB_done, 1)
            layer_norm(2)
            layer_norm(3)


def shape_constants():
    c = np.zeros((P, C_END), np.float32)
    c[:, C_FREQ_R] = 10000.0 ** (-np.arange(0, DK, 2, dtype=np.float64) / DK)
    c[:, C_FREQ_S:C_FREQ_S + 32] = 10000.0 ** (-np.arange(0, HD, 2, dtype=np.float64) / HD)
    c[:, C_IDENT:C_IDENT + P] = np.eye(P)
    c[:, C_TRI:C_TRI + P] = np.triu(np.ones((P, P)), 1)
    c[:, C_ONES:C_ONES + P] = 1.0
    c[:, C_IOTA:C_IOTA + SLOTS] = np.arange(1, SLOTS + 1)
    c[:, C_OVER:C_OVER + ROUNDS_MAX - 1] = np.arange(1, ROUNDS_MAX) * SLOTS + 0.5
    c[:, C_TIE:C_TIE + G] = np.arange(G, 0, -1)
    log_gamma = np.log1p(-(2.0 ** (-5.0 - np.arange(HR, dtype=np.float64))))
    m, n = np.arange(S)[:, None], np.arange(S)[None, :]
    seen = m // CHUNK <= n // CHUNK
    full = np.exp(log_gamma[:, None, None] * np.abs(n - m)) * seen * DK ** -0.5
    decay = np.concatenate([full[:, 0:P, :], full[:, P:S, P:S]], axis=2).transpose(1, 0, 2)
    return c, np.ascontiguousarray(decay.astype(np.float32))


def kernel(x, positions, ret_w_in, ret_w_out, ret_gn_gain, swa_w_in, swa_b_in, swa_sinks, swa_w_out,
           moe_w_group, moe_b_group, moe_w_router, moe_b_router, moe_w_in, moe_w_out, ln_gain, ln_bias):
    import concourse.bacc as bacc
    from concourse.bass_utils import run_bass_kernel_spmd as run

    def tiles(w):
        return w.reshape(-1, P, w.shape[-1]).transpose(1, 0, 2)

    def lay(a):
        return np.ascontiguousarray(np.asarray(a))

    w_in = tiles(np.asarray(ret_w_in)[0])
    qw, vw = HR * DK, HR * DV
    ret_units = []
    for h in range(HR):
        q, k = w_in[:, :, h * DK:(h + 1) * DK], w_in[:, :, qw + h * DK:qw + (h + 1) * DK]
        ret_units.append(np.stack([a[:, :, half * P:(half + 1) * P] for a in (q, k)
                                   for half in range(2)], axis=1))
        for first in (2 * qw, 2 * qw + vw):
            ret_units.append(w_in[:, :, first + h * DV:first + (h + 1) * DV])
    swa = tiles(np.asarray(swa_w_in)[0])
    consts, decay = shape_constants()
    x0 = np.asarray(x)[0]
    swa_out = np.asarray(swa_w_out)[0].reshape(KVH, HPG, HD, D).transpose(0, 2, 1, 3)
    sink_rows = np.repeat(np.asarray(swa_sinks)[0].reshape(8, 2), CHUNK, axis=1).T
    arrays = {
        "x_rows": x0.reshape(TT, P, D).transpose(1, 0, 2),
        "x_cols": tiles(x0.T),
        "pos_row": np.asarray(positions).reshape(1, S),
        "pos_col": np.asarray(positions).reshape(TT, P).T,
        "consts": consts,
        "decay": decay,
        "w_ret_in": np.stack([u.reshape(P, 2 * UNIT) for u in ret_units]),
        "w_ret_out": np.asarray(ret_w_out)[0].reshape(HR, DV // P, P, D).transpose(0, 2, 1, 3)
        .reshape(HR, P, 2 * UNIT),
        "w_swa_in": np.stack([swa[:, :, u * BANK:(u + 1) * BANK].reshape(P, 2 * UNIT)
                              for u in range(2)]),
        "w_swa_kv": swa[:, :, HS * HD:SWA_IN].reshape(P, -1),
        "w_swa_out": swa_out.reshape(P, HPG * D),
        "w_moe_in": np.asarray(moe_w_in).reshape(2, G * E, KT, P, 2 * FF).transpose(0, 1, 3, 2, 4)
        .reshape(2, G * E, P, 2 * UNIT),
        "w_moe_out": np.asarray(moe_w_out).reshape(2, G * E // 2, 2 * FT, P, D).transpose(0, 1, 3, 2, 4)
        .reshape(2, G * E // 2, P, 2 * UNIT),
        "ln_rows": np.stack([np.asarray(ln_gain), np.asarray(ln_bias)], axis=2).reshape(4, 2, D),
        "w_router": np.stack([np.concatenate([tiles(np.asarray(moe_w_group)[i]),
                                              tiles(np.asarray(moe_w_router)[i])], axis=2)
                              for i in range(2)], axis=1),
        "b_router": np.concatenate([np.asarray(moe_b_group), np.asarray(moe_b_router)], axis=1)
        .reshape(1, 2 * NR),
        "gn_gain": np.asarray(ret_gn_gain)[0].reshape(HR * DV // P, P).T,
        "sinks": sink_rows,
        "swa_bias": np.asarray(swa_b_in).reshape(1, SWA_IN),
    }
    nc = bacc.Bacc("TRN2", target_bir_lowering=False, num_devices=1)
    feeds, d = {}, {}
    for name, a in arrays.items():
        feeds[f"in_{name}"] = lay(a)
        d[name] = nc.dram_tensor(f"in_{name}", feeds[f"in_{name}"].shape,
                                 mybir.dt.from_np(feeds[f"in_{name}"].dtype), kind="ExternalInput").ap()
    out = nc.dram_tensor("out", (1, S, D), F32, kind="ExternalOutput").ap()
    build(nc, d, out)
    return run(nc, [feeds], core_ids=[0]).results[0]["out"]
```

```python
from contextlib import ExitStack

import numpy as np

import concourse.bass as bass
from concourse import mybir

F32 = mybir.dt.float32
F32R = mybir.dt.float32r
BF16 = mybir.dt.bfloat16
I32 = mybir.dt.int32
ALU = mybir.AluOpType
ACT = mybir.ActivationFunctionType
AX = mybir.AxisListType

P = 128
S = 256
TT = S // P
D = 1024
KT = D // P
BANK = 512
UNIT = 2048
RING = 11
RET_RING = 8
CHUNK = 64
ALPHA = (2.0 * 2) ** 0.25
LN_EPS = 1e-5

HR, DK, DV = 4, 256, 512
HS, KVH, HD = 16, 2, 64
HPG = HS // KVH
QKW = HS * HD + KVH * HD
SWA_IN = QKW + KVH * HD
NROT = QKW // (HD // 2)

G, E, FF = 4, 4, 256
FT = FF // P
NR = G + G * E
NE = G * E
SLOTS = 64
PAIRS = NE // 2
NSL = NE * SLOTS
ROUNDS_MAX = -(-S // SLOTS)
GATHERS = ((0, NSL // 4), (NSL // 4, NSL // 2), (NSL // 2, NSL))
assert 2 * SLOTS == P and 2 * FF == BANK

EVACUATIONS = len(GATHERS) * KT // 2

RET_UNITS = 2 * (3 * HR + HR)
MOE_ORDER = [u for i in range(PAIRS + 1) for u in (
    [(i, 0), (i, 1)] * (i < PAIRS) + [(i - 1, 4), (i - 1, 5)] * (i > 0) + [(i, 2), (i, 3)] * (i < PAIRS))]
MOE_UNITS = len(MOE_ORDER)
SWA_UNITS = 9
MOE_SLOT = (0, (MOE_UNITS + SWA_UNITS) % RING)
SWA_SLOT = MOE_UNITS % RING
MOE_BEFORE_SWA = RING - SWA_UNITS
assert RET_UNITS % RET_RING == 0 and 0 < MOE_BEFORE_SWA < RING

PIECE = UNIT // 2
HEAD_PIECES = 12
IN_PIECES = HR * HEAD_PIECES
PIECES = IN_PIECES + HR * DV // P
SWA_IN_PIECES = 10
SWA_PIECES = 2 * SWA_UNITS
FIRST_BY_POOL = 2
SPLIT_BUFS = 3
SPLIT_PRODUCTS = ((0, 0), (0, 1), (1, 0))

C_FREQ_R, C_FREQ_S, C_IDENT, C_TRI, C_ONES, C_IOTA, C_TIE, C_OVER, C_END = np.cumsum(
    [0, 1, 32, P, P, P, SLOTS, G, ROUNDS_MAX - 1]).tolist()
NANG = S + TT * 32
TWO_PI = 2.0 * np.pi
TWO_PI_A = 6.28125
TWO_PI_B = float(np.round((TWO_PI - TWO_PI_A) * 2**22) / 2**22)
TWO_PI_C = TWO_PI - TWO_PI_A - TWO_PI_B
ROUND_MAGIC = 1.5 * 2**23
PI_BELOW = 3.1415925


def build(nc, d, out):
    with ExitStack() as ctx:
        def sb(name, shape, dt=F32):
            return ctx.enter_context(nc.sbuf_tensor(name, shape, dt))

        def sem(name):
            return ctx.enter_context(nc.semaphore(name))

        ps = ctx.enter_context(nc.psum_tensor("ps", [P, 8, BANK], F32))
        ring_low = sb("ring_low", [P, RET_RING, UNIT])
        x_tok = sb("x_tok", [P, TT, D])
        z = sb("z", [P, TT, D])
        ln_rows = sb("ln_rows", [P, 2, D])
        cst = sb("cst", [P, C_END])
        sin = sb("sin", [P, NANG])
        cos = sb("cos", [P, NANG])
        pos_i = sb("pos_i", [P, S + TT], I32)
        w_router = sb("w_router", [P, 2, KT, NR])
        b_router = sb("b_router", [P, 2, NR])
        gn_gain = sb("gn_gain", [P, HR * DV // P])
        sinks = sb("sinks", [P, 8])
        stats = sb("stats", [P, TT, 2, 6])
        mean_var = sb("mean_var", [P, TT, 2])
        rstd = sb("rstd", [P, TT])
        var_eps = sb("var_eps", [P, TT])
        minus_half = sb("minus_half", [P, 1])

        ident = cst[:, C_IDENT:C_IDENT + P]
        tri_ones = sb("tri_ones", [P, 2 * P], BF16)
        tri, ones = tri_ones[:, 0:P], tri_ones[:, P:2 * P]
        iota = cst[:, C_IOTA:C_IOTA + SLOTS]
        tie = cst[:, C_TIE:C_TIE + G]

        def carve(of, start, *dims):
            n = int(np.prod(dims))
            view = of[:, start:start + n]
            names = "abcd"[:len(dims)]
            if len(dims) > 1:
                view = view.rearrange(f"p ({' '.join(names)}) -> p {' '.join(names)}",
                                      **{c: k for c, k in zip(names[1:], dims[1:])})
            return view, start + n

        s_max = sb("s_max", [P, 8])
        s_negm = sb("s_negm", [P, 2, 8])
        s_dsink = sb("s_dsink", [P, 2, 8])
        s_esink = sb("s_esink", [P, 2, 8])
        s_sum = sb("s_sum", [P, 2, 8])
        s_rden = sb("s_rden", [P, 8])
        logits = sb("logits", [P, TT, NR])
        r_first = sb("r_first", [P, TT, 1 + G])
        r_second = sb("r_second", [P, TT, 1 + G])
        r_rest = sb("r_rest", [P, TT, NR])
        r_eq = sb("r_eq", [P, TT, NR])
        r_tie = sb("r_tie", [P, TT, 1 + G])
        oh_first = sb("oh_first", [P, TT, NR])
        oh_second = sb("oh_second", [P, TT, NR])
        r_diff = sb("r_diff", [P, TT, G])
        r_exp = sb("r_exp", [P, TT, G])
        r_gate = sb("r_gate", [P, TT])
        r_dt = sb("r_dt", [P, TT, 1 + G])
        r_et = sb("r_et", [P, TT, 1 + G])
        r_w1 = sb("r_w1", [P, TT, 1 + G])
        r_w2 = sb("r_w2", [P, TT, 1 + G])
        combine = sb("combine", [P, TT, NE])
        chosen = sb("chosen", [P, TT, NE], BF16)
        picked = sb("picked", [P, TT, NE])
        weight = sb("weight", [P, TT, NE])
        cw_slots = sb("cw_slots", [P, PAIRS])
        key = sb("key", [P, TT, NE])
        n_over = sb("n_over", [1, ROUNDS_MAX + 1])
        more_rounds = sb("more_rounds", [1, 1], I32)

        with ExitStack() as phase:
            work = phase.enter_context(nc.sbuf_tensor("ret_parts", [P, 12288 + SPLIT_BUFS * 2 * PIECE],
                                                      F32R))
            xT_parts, o = carve(work, 0, 2, KT, S)
            w_parts, o = carve(work, o, SPLIT_BUFS, 2, PIECE)
            yT_parts, o = carve(work, o, 2, HR * DV // P, S)
            work = phase.enter_context(nc.sbuf_tensor("ret_work", [P, 7936], F32))
            qT, o = carve(work, 0, 2, 2, S)
            kT, o = carve(work, o, 2, 2, S)
            v_ret, o = carve(work, o, 2, TT, DV)
            g_start = o
            g_ret, o = carve(work, o, 2, TT, DV)
            rotA, o = carve(work, o, 2, S)
            rotB, o = carve(work, o, 2, S)
            prT, o = carve(work, o, 2, 3 * P)
            assert o == 7936, o
            angle, end = carve(work, g_start, NANG)
            turns, end = carve(work, end, NANG)
        ring_high = sb("ring_high", [P, RING - RET_RING, UNIT])
        swa_bias = sb("swa_bias", [P, SWA_IN])
        with ExitStack() as phase:
            work = phase.enter_context(nc.sbuf_tensor("moe_work", [P, 8960], F32))
            xsT, o = carve(work, 0, KT, NSL)
            silu_a, o = carve(work, o, FF)
            act_sl, o = carve(work, o, FF)
            actT, o = carve(work, o, FT, P)
            assert o == 8960, o
            xT = carve(work, 0, KT, S)[0]
            work = phase.enter_context(nc.sbuf_tensor("moe_parts", [P, 10240], F32R))
            x_parts, o = carve(work, 0, 2, TT, D)
            onehot, o = carve(work, o, TT, NSL)
            onehotT, o = carve(work, o, PAIRS, S)
            y_parts, o = carve(work, o, 2, D)
            assert o == 10240, o
        with ExitStack() as phase:
            work = phase.enter_context(nc.sbuf_tensor("swa_parts", [P, 4096 + SPLIT_BUFS * 2 * PIECE],
                                                      F32R))
            swa_w_parts, at = carve(work, 0, SPLIT_BUFS, 2, PIECE)
            swa_xT_parts, o = carve(work, at, 2, KT, S)
            oT_parts, o = carve(work, at, 2, HPG, S)
            work = phase.enter_context(nc.sbuf_tensor("swa_work", [P, 9216], F32))
            q_rows, o = carve(work, 0, TT, QKW)
            rot_cos, o = carve(work, o, 2, BANK)
            rot_sin, o = carve(work, o, 2, BANK)
            unrotated, o = carve(work, o, 2, BANK)
            sqT, o = carve(work, o, 4, HPG, CHUNK)
            skT, o = carve(work, o, 6 * CHUNK)
            v_win, o = carve(work, o, 3, P)
            probsT, o = carve(work, o, 8, P)
            assert o == 9216, o
            probs = carve(work, TT * QKW, 2, 8, P)[0]

        trig_in = sem("trig_in")
        xT_in = [sem("xT_in0"), sem("xT_in1")]
        first_piece_in = sem("first_piece_in")
        x_in = sem("x_in")
        decay_in = sem("decay_in")
        params_in = sem("params_in")
        bias_in = sem("bias_in")
        ln_in = sem("ln_in")
        out_stored = sem("out_stored")
        loaded = [[sem(f"loaded{L}_{s}") for s in range(RING)] for L in range(2)]
        dve_step = sem("dve_step")
        angles_done = sem("angles_done")
        tri_ready = sem("tri_ready")
        trig_done = sem("trig_done")
        x_split_high = sem("x_split_high")
        x_split_low = sem("x_split_low")
        w_high = sem("w_high")
        w_low = sem("w_low")
        w_used = sem("w_used")
        rope_read = sem("rope_read")
        vg_done = sem("vg_done")
        qk_ready = sem("qk_ready")
        ret_scores = sem("ret_scores")
        ret_masked = sem("ret_masked")
        ret_o = sem("ret_o")
        gn_stats = sem("gn_stats")
        gn_rstd = sem("gn_rstd")
        gn_gated = sem("gn_gated")
        y_ready = sem("y_ready")
        yT_ps = sem("yT_ps")
        yT_scaled = sem("yT_scaled")
        yT_high = sem("yT_high")
        yT_ready = sem("yT_ready")
        mix_done = sem("mix_done")
        z_ready = sem("z_ready")
        ln_stats = sem("ln_stats")
        ln_rstd = sem("ln_rstd")
        x_ready = sem("x_ready")
        pool_const = sem("pool_const")
        xT_ps = sem("xT_ps")
        xT_ready = sem("xT_ready")
        swa_w_high = sem("swa_w_high")
        swa_w_low_pool = sem("swa_w_low_pool")
        swa_w_low = sem("swa_w_low")
        swa_w_used = sem("swa_w_used")
        swa_x_high = sem("swa_x_high")
        swa_x_low = sem("swa_x_low")
        oT_high = sem("oT_high")
        sproj_done = sem("sproj_done")
        sproj_read = sem("sproj_read")
        rotB_done = sem("rotB_done")
        rot_done = sem("rot_done")
        sqk_ps = sem("sqk_ps")
        sqk_ready = sem("sqk_ready")
        swa_scores = sem("swa_scores")
        max_done = sem("max_done")
        exp_done = sem("exp_done")
        probs_ready = sem("probs_ready")
        probsT_ps = sem("probsT_ps")
        probsT_ready = sem("probsT_ready")
        pv_done = sem("pv_done")
        oT_ready = sem("oT_ready")
        M = [{n: sem(f"{n}{L}") for n in (
            "logits_ps", "exp_arg", "exp_val", "chosen_ready", "rank_ps", "rounds_ready",
            "keys_ready", "onehot_ready", "combine_ready", "gather_ps", "gather_act", "gather_dve",
            "ohT_ps", "ohT_ready", "cw_ps", "cw_ready", "h_half", "h_done", "silu_done", "act_done", "actT_ps",
            "actT_ready", "y_done", "y_high", "y_low", "x_high", "x_low", "scattered", "sums_done",
            "z_scaled", "z_added")} for L in range(2)]

        def load_rounds(eng, L):
            eng.wait_ge(M[L]["rounds_ready"], 1)
            return eng.value_load(more_rounds[0:1, 0:1], min_val=0, max_val=ROUNDS_MAX - 1) + 1

        def slot_of(slot):
            return ring_low[:, slot, :] if slot < RET_RING else ring_high[:, slot - RET_RING, :]

        def swa_piece(p):
            return slot_of((SWA_SLOT + p // 2) % RING)[:, p % 2 * PIECE:(p % 2 + 1) * PIECE]

        scaled_yT = [r.rearrange("p a n -> p (a n)").rearrange("p (k n) -> p k n", n=P)
                     for r in (rotA, rotB)]
        z_flat = z[:, :, :].rearrange("p t n -> p (t n)")
        x_staged = z_flat.rearrange("p (k n) -> p k n", k=KT)
        decay = z_flat[:, 0:HR * 3 * P].rearrange("p (h n) -> p h n", h=HR)

        block = ctx.enter_context(nc.Block())

        @block.sync
        def _(sp):
            def load(L, slot, src):
                sp.dma_start(slot_of(slot), src).then_inc(loaded[L][slot], 16)

            def ret_unit_used(u):
                sp.wait_ge(w_low, 2 * (u + 1))

            def swa_unit_used(u):
                if 2 * u < FIRST_BY_POOL:
                    sp.wait_ge(swa_w_low_pool, 2 * (u + 1))
                else:
                    sp.wait_ge(swa_w_low, 2 * (u + 1) - FIRST_BY_POOL)

            def moe_unit_used(L, r, n):
                pair, kind = MOE_ORDER[n]
                used = "h_half" if kind < 2 else "h_done" if kind < 4 else "y_done"
                sp.wait_ge(M[L][used], r * PAIRS + pair + 1)

            def mixture(L, slot_used):
                def round_units(before):
                    for n in range(MOE_UNITS):
                        before(n)
                        pair, kind = MOE_ORDER[n]
                        half = kind // 2 if kind < 4 else kind % 2
                        cols = slice(half * UNIT, (half + 1) * UNIT)
                        src = d["w_moe_in"][L, 2 * pair + kind % 2] if kind < 4 else d["w_moe_out"][L, pair]
                        load(L, (MOE_SLOT[L] + n) % RING, src[:, cols])

                round_units(lambda n: moe_unit_used(L, 0, n - RING) if n >= RING else slot_used(n))
                rounds = load_rounds(sp, L)
                with sp.If(rounds > 1):
                    with sp.Fori(1, rounds) as r:
                        def before(n):
                            if n >= RING:
                                moe_unit_used(L, r, n - RING)
                            else:
                                moe_unit_used(L, r - 1, max(range(n, MOE_UNITS, RING)))
                        round_units(before)
                return rounds

            sp.dma_start(ring_low[:, 0, 0:PIECE], d["w_ret_in"][0][:, 0:PIECE]).then_inc(first_piece_in, 16)
            for half in range(2):
                ks = slice(half * KT // 2, (half + 1) * KT // 2)
                sp.dma_start(x_staged[:, ks, :], d["x_cols"][:, ks, :]).then_inc(xT_in[half], 16)
            for u in range(RET_UNITS):
                if u >= RET_RING:
                    ret_unit_used(u - RET_RING)
                m, cols = u // 2, slice(u % 2 * UNIT, (u % 2 + 1) * UNIT)
                if u == 0:
                    sp.dma_start(ring_low[:, 0, PIECE:UNIT], d["w_ret_in"][0][:, PIECE:UNIT])\
                        .then_inc(loaded[0][0], 16)
                else:
                    src = d["w_ret_in"][m] if m < 3 * HR else d["w_ret_out"][m - 3 * HR]
                    load(0, u % RET_RING, src[:, cols])
                if u == 0:
                    sp.dma_start(pos_i[:, 0:S], d["pos_row"].to_broadcast([P, S])).then_inc(trig_in, 16)
                    sp.dma_start(pos_i[:, S:S + TT], d["pos_col"]).then_inc(trig_in, 16)
                    sp.dma_start(cst[:, :], d["consts"]).then_inc(trig_in, 16)
            def ret_memory_free(n):
                if n < RET_RING:
                    ret_unit_used(RET_UNITS - RET_RING + n)
                elif n < RET_RING + 2:
                    sp.wait_ge(w_used, IN_PIECES)
                else:
                    sp.wait_ge(mix_done, 4)

            rounds = mixture(0, ret_memory_free)
            for u in range(SWA_UNITS):
                moe_unit_used(0, rounds - 1, MOE_UNITS - RING + u)
                if u == 0:
                    src = d["w_swa_kv"]
                elif u < 5:
                    src = d["w_swa_in"][(u - 1) // 2][:, (u - 1) % 2 * UNIT:((u - 1) % 2 + 1) * UNIT]
                else:
                    src = d["w_swa_out"][:, (u - 5) * UNIT:(u - 4) * UNIT]
                load(1, (SWA_SLOT + u) % RING, src)
            mixture(1, lambda n: swa_unit_used(n - MOE_BEFORE_SWA) if n >= MOE_BEFORE_SWA else
                    moe_unit_used(0, rounds - 1, MOE_UNITS - MOE_BEFORE_SWA + n))
            for t in range(TT):
                sp.wait_ge(x_ready, 4 * 3 + 2 * t + 2)
                sp.dma_start(out.rearrange("a (t p) n -> p (a t) n", p=P)[:, t, :],
                             x_tok[:, t, :]).then_inc(out_stored, 16)
            sp.wait_ge(out_stored, 16 * TT)

        @block.tensor
        def _(pe):
            mm = nc.tensor.matmul

            def piece(p, k):
                pe.wait_ge(w_low, p + 1)
                return w_parts[:, p % SPLIT_BUFS, :, :].rearrange("p a (k n) -> p a k n", k=k)

            def project_qk(h):
                for j in range(2):
                    if h > 0:
                        pe.wait_ge(vg_done, 4 * (h - 1) + 2 + j)
                    for half in range(2):
                        w = piece(HEAD_PIECES * h + 2 * j + half, KT)
                        for k in range(KT):
                            if h == 0 and j == 0 and half == 0 and k % (KT // 2) == 0:
                                pe.wait_ge(x_split_low, 1 + 2 * k // KT)
                            for n, (a, b) in enumerate(SPLIT_PRODUCTS):
                                last = mm(ps[:, j, half * S:(half + 1) * S], w[:, b, k, :],
                                          xT_parts[:, a, k, :], start=(k == 0 and n == 0),
                                          stop=(k == KT - 1 and n == 2))
                        last.then_inc(w_used, 1)

            def project_vg(h, j):
                if j == 1:
                    if h > 0:
                        pe.wait_ge(vg_done, 4 * h)
                    pe.wait_ge(rope_read, 2 * h + 1)
                else:
                    pe.wait_ge(rope_read, 2 * h + 2)
                    pe.wait_ge(vg_done, 4 * h + 1)
                for i in range(4):
                    w = piece(HEAD_PIECES * h + 4 * j + i, 2)
                    for t in range(TT):
                        for k in range(2):
                            for n, (a, b) in enumerate(SPLIT_PRODUCTS):
                                last = mm(ps[:, (2 * j + t) % 3, :],
                                          xT_parts[:, a, 2 * i + k, t * P:(t + 1) * P], w[:, b, k, :],
                                          start=(i == 0 and k == 0 and n == 0),
                                          stop=(i == 3 and k == 1 and n == 2))
                    last.then_inc(w_used, 1)

            def ret_score(h):
                pe.wait_ge(qk_ready, 2 * h + 2)
                if h > 0:
                    pe.wait_ge(ret_masked, h)
                q, k = qT[:, h % 2], kT[:, h % 2]
                for half in range(2):
                    mm(ps[:, 3, 0:S], k[:, half, 0:P], q[:, half, :], start=(half == 0), stop=(half == 1))
                for half in range(2):
                    last = mm(ps[:, 3, S:S + P], k[:, half, P:S], q[:, half, P:S],
                              start=(half == 0), stop=(half == 1))
                last.then_inc(ret_scores, 1)

            def ret_value(h):
                pe.wait_ge(ret_masked, h + 1)
                pe.wait_ge(vg_done, 4 * h + 2)
                if h > 0:
                    pe.wait_ge(gn_gated, 2 * h)
                pr, v = prT[:, h % 2], v_ret[:, h % 2]
                mm(ps[:, 4, :], pr[:, 0:P], v[:, 0], start=True, stop=True).then_inc(ret_o, 1)
                mm(ps[:, 5, :], pr[:, P:S], v[:, 0], start=True, stop=False)
                mm(ps[:, 5, :], pr[:, S:S + P], v[:, 1], start=False, stop=True).then_inc(ret_o, 1)

            def ret_transpose(h):
                if h == 0:
                    pe.wait_ge(trig_in, 48)
                for t in range(TT):
                    pe.wait_ge(y_ready, 2 * h + t + 1)
                    if h > 0:
                        pe.wait_ge(yT_ready, 2 * (h - 1) + t + 1)
                    for j in range(DV // P):
                        last = nc.tensor.transpose(ps[:, 6 + t, j * P:(j + 1) * P],
                                                   g_ret[:, h % 2, t, j * P:(j + 1) * P], ident)
                    last.then_inc(yT_ps, 1)

            def ret_output(h):
                pe.wait_ge(yT_ready, 2 * h + 2)
                if h == 0:
                    pe.wait_ge(vg_done, 4 * HR)
                    pe.wait_ge(ret_masked, HR)
                for k in range(DV // P):
                    w = piece(IN_PIECES + h * DV // P + k, 1)
                    for t in range(TT):
                        for n in range(2):
                            for i, (a, b) in enumerate(SPLIT_PRODUCTS):
                                last = mm(ps[:, 2 * t + n, :], yT_parts[:, a, h * 4 + k, t * P:(t + 1) * P],
                                          w[:, b, 0, n * BANK:(n + 1) * BANK],
                                          start=(h == 0 and k == 0 and i == 0),
                                          stop=(h == HR - 1 and k == DV // P - 1 and i == 2))
                            if h == HR - 1 and k == DV // P - 1:
                                last.then_inc(mix_done, 1)
                    if not (h == HR - 1 and k == DV // P - 1):
                        last.then_inc(w_used, 1)

            def transpose_x(n, t):
                for half in range(2):
                    pe.wait_ge(x_ready, 4 * n + 2 * t + half + 1)
                    for j in range(4):
                        k = 4 * half + j
                        last = nc.tensor.transpose(ps[:, 4 + 2 * t + half, j * P:(j + 1) * P],
                                                   x_tok[:, t, k * P:(k + 1) * P], ident)
                    last.then_inc(xT_ps, 1)

            def mixture(L, used):
                m = M[L]
                for t in range(TT):
                    transpose_x(2 * L, t)
                    pe.wait_ge(xT_ready, 4 * L + 2 * t + 2)
                    if t == 0:
                        pe.wait_ge(params_in, 64)
                        pe.wait_ge(z_ready, 8 * L + 4)
                    for k in range(KT):
                        last = mm(ps[:, 0, t * 32:t * 32 + NR], xT[:, k, t * P:(t + 1) * P],
                                  w_router[:, L, k, :], start=(k == 0), stop=(k == KT - 1))
                    last.then_inc(m["logits_ps"], 1)
                pe.wait_ge(tri_ready, 1)
                pe.wait_ge(m["chosen_ready"], 1)
                mm(ps[:, 1, 0:NE], tri, chosen[:, 0, :], start=True, stop=True)
                mm(ps[:, 1, NE:2 * NE], ones, chosen[:, 0, :], start=True, stop=False)
                mm(ps[:, 1, NE:2 * NE], tri, chosen[:, 1, :], start=False, stop=True)
                mm(ps[:, 1, 2 * NE:3 * NE], ones, chosen[:, 0, :], start=True, stop=False)
                mm(ps[:, 1, 2 * NE:3 * NE], ones, chosen[:, 1, :], start=False, stop=True)\
                    .then_inc(m["rank_ps"], 1)
                rounds = load_rounds(pe, L)

                def unit(i, kind, n, r):
                    u = MOE_ORDER.index((i, kind))
                    slot = (MOE_SLOT[L] + u) % RING
                    a_round = len(range(u % RING, MOE_UNITS, RING))
                    pe.wait_ge(loaded[L][slot], (r * a_round + u // RING + used(slot) + 1) * 16)
                    return slot_of(slot).rearrange("p (k n) -> p k n", n=n)

                def hidden(i, half, r):
                    w = [unit(i, 2 * half + e, 2 * FF, r) for e in range(2)]
                    for k in range(KT // 2):
                        for e in range(2):
                            last = mm(ps[e * SLOTS:(e + 1) * SLOTS, 4 + i % 2, :],
                                      xsT[:, half * KT // 2 + k, (2 * i + e) * SLOTS:(2 * i + e + 1) * SLOTS],
                                      w[e][:, k, :], start=(half == 0 and k == 0),
                                      stop=(half == 1 and k == KT // 2 - 1))
                    last.then_inc(m["h_done" if half else "h_half"], 1)

                def transpose_act(i, base):
                    pe.wait_ge(m["act_done"], base + i + 1)
                    for f in range(FT):
                        last = nc.tensor.transpose(ps[:, 4 + i % 2, f * P:(f + 1) * P],
                                                   act_sl[:, f * P:(f + 1) * P], ident)
                    last.then_inc(m["actT_ps"], 1)

                def project_back(i, base, r):
                    w = [unit(i, 4 + e, D, r) for e in range(2)]
                    pe.wait_ge(m["actT_ready"], base + i + 1)
                    for f in range(FT):
                        for n in range(2):
                            for e in range(2):
                                last = mm(ps[e * SLOTS:(e + 1) * SLOTS, 6 + n, :],
                                          actT[:, f, e * SLOTS:(e + 1) * SLOTS],
                                          w[e][:, f, n * BANK:(n + 1) * BANK],
                                          start=(f == 0), stop=(f == FT - 1))
                    last.then_inc(m["y_done"], 1)

                def scatter(i, base):
                    for n in range(2):
                        pe.wait_ge(m["y_low"], 2 * (base + i) + n + 1)
                        for t in range(TT):
                            for part in range(2):
                                last = mm(ps[:, 2 * t + n, :], onehotT[:, i, t * P:(t + 1) * P],
                                          y_parts[:, part, n * BANK:(n + 1) * BANK],
                                          start=(i == 0 and part == 0),
                                          stop=(i == PAIRS - 1 and part == 1))
                            if i == PAIRS - 1:
                                last.then_inc(m["sums_done"], 1)
                    if i < PAIRS - 1:
                        last.then_inc(m["scattered"], 1)

                def transpose_onehot():
                    for i in range(PAIRS):
                        for t in range(TT):
                            c = (i * TT + t) * P
                            last = nc.tensor.transpose(ps[:, c // BANK, c % BANK:c % BANK + P],
                                                       onehot[:, t, i * P:(i + 1) * P].bitcast(F32), ident)
                        if i % 2:
                            last.then_inc(m["ohT_ps"], 1)

                def gather(r, part):
                    slots = slice(*GATHERS[part])
                    for q in range(part * KT, (part + 1) * KT):
                        if q >= 3:
                            pe.wait_ge(m["gather_act" if (q - 3) % 2 == 0 else "gather_dve"],
                                       r * EVACUATIONS + (q - 3) // 2 + 1)
                        for a in range(2):
                            for t in range(TT):
                                last = mm(ps[:, 5 + q % 3, 0:slots.stop - slots.start],
                                          x_parts[:, a, t, q % KT * P:(q % KT + 1) * P],
                                          onehot[:, t, slots],
                                          start=(a == 0 and t == 0), stop=(a == 1 and t == TT - 1))
                        last.then_inc(m["gather_ps"], 1)

                def gathered(r, part):
                    for name in ("gather_act", "gather_dve"):
                        pe.wait_ge(m[name], r * EVACUATIONS + (part + 1) * KT // 2)

                def slot_weights():
                    pe.wait_ge(m["combine_ready"], 1)
                    for i in range(PAIRS):
                        for t in range(TT):
                            last = mm(ps[:, 0, 2 * i:2 * i + 2],
                                      onehot[:, t, i * P:(i + 1) * P].bitcast(F32),
                                      combine[:, t, 2 * i:2 * i + 2], start=(t == 0), stop=(t == TT - 1))
                    last.then_inc(m["cw_ps"], 1)

                with pe.Fori(0, rounds) as r:
                    base = r * PAIRS
                    pe.wait_ge(m["onehot_ready"], 2 * r + 1)
                    pe.wait_ge(m["x_low"], TT)
                    gather(r, 0)
                    for i in range(PAIRS):
                        if i == 0:
                            gathered(r, 0)
                        elif i == 1:
                            gathered(r, 1)
                        elif i == PAIRS // 2 - 1:
                            gathered(r, 2)
                        hidden(i, 0, r)
                        if i == 0:
                            pe.wait_ge(m["onehot_ready"], 2 * r + 2)
                            slot_weights()
                            gather(r, 1)
                        else:
                            transpose_act(i - 1, base)
                            if i == 2:
                                pe.wait_ge(m["ohT_ready"], r * 4 + 4)
                            if i > 1:
                                scatter(i - 2, base)
                            project_back(i - 1, base, r)
                        hidden(i, 1, r)
                        if i == PAIRS // 2 - 2:
                            pe.wait_ge(m["y_low"], 2 * (base + i))
                            gather(r, 2)
                        if i == 0:
                            pe.wait_ge(m["cw_ready"], r + 1)
                            transpose_onehot()
                    scatter(PAIRS - 2, base)
                    transpose_act(PAIRS - 1, base)
                    project_back(PAIRS - 1, base, r)
                    scatter(PAIRS - 1, base)

            def attention():
                for t in range(TT):
                    transpose_x(1, t)
                def piece(p, k):
                    if p < FIRST_BY_POOL:
                        pe.wait_ge(swa_w_low_pool, p + 1)
                    else:
                        pe.wait_ge(swa_w_low, p - FIRST_BY_POOL + 1)
                    return swa_w_parts[:, p % SPLIT_BUFS, :, :].rearrange("p a (k n) -> p a k n", k=k)

                for p in range(SWA_IN_PIECES):
                    part, tiles = (0, 4) if p < 2 else ((p + 2) // 4, 2)
                    first = 4 * p if p < 2 else (p - 2) % 4 * 2
                    n = BANK if part else 2 * KVH * HD
                    w = piece(p, tiles)
                    if p == 2:
                        pe.wait_ge(z_ready, 8)
                    for t in range(TT):
                        if p == 0:
                            pe.wait_ge(swa_x_low, 2 * t + 2)
                        for k in range(tiles):
                            for i, (a, b) in enumerate(SPLIT_PRODUCTS):
                                last = mm(ps[:, (4, 0, 2)[part] + t, 0:n],
                                          swa_xT_parts[:, a, first + k, t * P:(t + 1) * P], w[:, b, k, :],
                                          start=(first + k == 0 and i == 0),
                                          stop=(first + k == KT - 1 and i == 2))
                        if t == 0 and first + tiles == KT:
                            last.then_inc(sproj_done, 1)
                    last.then_inc(swa_w_used, 1)
                for t in range(TT):
                    pe.wait_ge(rot_done, 5 + t)
                    for i in range(HPG):
                        last = nc.tensor.transpose(
                            ps[:, (6, 0)[t] + i // 4, (i % 4) * P:(i % 4 + 1) * P],
                            q_rows[:, t, i * P:(i + 1) * P], ident)
                        if i % 4 == 3:
                            last.then_inc(sqk_ps, 1)
                    nc.tensor.transpose(ps[:, 4 + t, 0:P], q_rows[:, t, HS * HD:QKW], ident)\
                        .then_inc(sqk_ps, 1)

                def scores(c):
                    width = P if c else CHUNK
                    start = (0, 0, 4 * CHUNK, 2 * CHUNK)[c]
                    if c == 0:
                        pe.wait_ge(sqk_ready, 4 * TT)
                    if c >= 2:
                        pe.wait_ge(exp_done, c - 1)
                    for kv in range(KVH):
                        rows = slice(kv * HD, (kv + 1) * HD)
                        for pair in range(HPG // 2):
                            last = mm(ps[:, 2 + 2 * (c % 2) + kv, pair * P:pair * P + width],
                                      sqT[rows, c, 2 * pair:2 * pair + 2, :].rearrange("p a n -> p (a n)"),
                                      skT[rows, start:start + width], start=True, stop=True)
                    last.then_inc(swa_scores, 1)

                def transpose_probs(c):
                    width = P if c else CHUNK
                    pe.wait_ge(probs_ready, c + 1)
                    if c >= 1:
                        pe.wait_ge(probsT_ready, 2 * c)
                    for i in range(8):
                        last = nc.tensor.transpose(ps[0:width, 6 + i // 4, (i % 4) * P:(i % 4 + 1) * P],
                                                   probs[:, c % 2, i, 0:width], ident)
                    last.then_inc(probsT_ps, 1)

                def values(c):
                    width = P if c else CHUNK
                    pe.wait_ge(probsT_ready, 2 * c + 2)
                    if c >= 2:
                        pe.wait_ge(oT_ready, c - 1)
                    for kv in range(KVH):
                        last = mm(ps[kv * HD:(kv + 1) * HD, c % 2, :],
                                  v_win[0:width, (0, 0, 2, 1)[c], kv * HD:(kv + 1) * HD],
                                  probsT[0:width, 4 * kv:4 * kv + 4, :], start=True, stop=True)
                    last.then_inc(pv_done, 1)

                scores(0)
                scores(1)
                for c in range(4):
                    if c + 2 < 4:
                        scores(c + 2)
                    transpose_probs(c)
                    values(c)
                pe.wait_ge(oT_ready, 4)
                for k in range(HPG):
                    w = piece(SWA_IN_PIECES + k, 1)
                    for t in range(TT):
                        for n in range(2):
                            for i, (a, b) in enumerate(SPLIT_PRODUCTS):
                                last = mm(ps[:, 2 * t + n, :], oT_parts[:, a, k, t * P:(t + 1) * P],
                                          w[:, b, 0, n * BANK:(n + 1) * BANK],
                                          start=(k == 0 and i == 0), stop=(k == HPG - 1 and i == 2))
                            if k == HPG - 1:
                                last.then_inc(mix_done, 1)
                    if k < HPG - 1:
                        last.then_inc(swa_w_used, 1)

            for h in range(HR):
                project_qk(h)
                if h > 0:
                    ret_score(h - 1)
                project_vg(h, 1)
                if h > 0:
                    ret_value(h - 1)
                project_vg(h, 2)
                if h > 0:
                    ret_transpose(h - 1)
            ret_score(HR - 1)
            ret_value(HR - 1)
            ret_output(0)
            ret_output(1)
            ret_transpose(HR - 1)
            ret_output(2)
            ret_output(3)
            mixture(0, lambda slot: len(range(slot, RET_UNITS, RET_RING)) if slot < RET_RING else 0)
            attention()
            mixture(1, lambda slot: int((slot - SWA_SLOT) % RING < SWA_UNITS))

        @block.scalar
        def _(act):
            af = nc.scalar.activation

            def rotary_tables():
                act.wait_ge(angles_done, 1)
                af(sin[:, :], angle, ACT.Sin).then_inc(trig_done, 1)
                act.wait_ge(angles_done, 2)
                af(cos[:, :], turns, ACT.Sin).then_inc(trig_done, 1)

            def later_loads():
                act.wait_ge(x_split_low, 2)
                act.dma_start(decay, d["decay"]).then_inc(decay_in, 16)
                act.dma_start(gn_gain[:, :], d["gn_gain"]).then_inc(params_in, 16)
                act.dma_start(w_router[:, :, :, :], d["w_router"]).then_inc(params_in, 16)
                act.dma_start(b_router[:, :, :].rearrange("p l n -> p (l n)"),
                              d["b_router"].to_broadcast([P, 2 * NR])).then_inc(params_in, 16)
                act.dma_start(sinks[:, :], d["sinks"]).then_inc(params_in, 16)
                act.dma_start(x_tok[:, :, :], d["x_rows"]).then_inc(x_in, 16)

            def split_high(p):
                u = p // 2
                if p == 0:
                    act.wait_ge(first_piece_in, 16)
                else:
                    act.wait_ge(loaded[0][u % RET_RING], 16 * (u // RET_RING + 1))
                if p >= SPLIT_BUFS:
                    act.wait_ge(w_used, p - SPLIT_BUFS + 1)
                af(w_parts[:, p % SPLIT_BUFS, 0, :], ring_low[:, u % RET_RING, p % 2 * PIECE:(p % 2 + 1) * PIECE],
                   ACT.Copy).then_inc(w_high, 1)

            def copy_out(h, j, t):
                act.wait_ge(w_used, HEAD_PIECES * h + 4 * (j + 1))
                if h >= 2 and t == 0:
                    if j == 1:
                        act.wait_ge(ret_o, 2 * (h - 1))
                    else:
                        act.wait_ge(yT_ps, 2 * (h - 1))
                dst = (v_ret if j == 1 else g_ret)[:, h % 2, t, :]
                af(dst, ps[:, (2 * j + t) % 3, :], ACT.Copy if j == 1 else ACT.Silu)\
                    .then_inc(vg_done, 1)

            def scale_y(h):
                for t in range(TT):
                    act.wait_ge(gn_gated, 2 * h + t + 1)
                    act.wait_ge(gn_rstd, 2 * h + t + 1)
                    y = g_ret[:, h % 2, t, :]
                    af(y, y, ACT.Copy, scale=rstd[:, t:t + 1]).then_inc(y_ready, 1)

            def yT_high_part(h):
                for t in range(TT):
                    act.wait_ge(yT_scaled, 2 * h + t + 1)
                    af(yT_parts[:, 0, 4 * h:4 * h + 4, t * P:(t + 1) * P], scaled_yT[t], ACT.Copy)\
                        .then_inc(yT_high, 1)

            for half in range(2):
                ks = slice(half * KT // 2, (half + 1) * KT // 2)
                act.wait_ge(xT_in[half], 16)
                af(xT_parts[:, 0, ks, :], x_staged[:, ks, :], ACT.Copy).then_inc(x_split_high, 1)
                split_high(half)
            for p in range(PIECES):
                h = min(p // HEAD_PIECES, HR)
                step = p - h * HEAD_PIECES
                if p + SPLIT_BUFS - 1 < PIECES:
                    split_high(p + SPLIT_BUFS - 1)
                if p == 1:
                    rotary_tables()
                    later_loads()
                if step == 0 and h > 0:
                    copy_out(h - 1, 2, 0)
                    copy_out(h - 1, 2, 1)
                if step == 1 and h > 1:
                    yT_high_part(h - 2)
                if step == 8 and h < HR:
                    copy_out(h, 1, 0)
                    copy_out(h, 1, 1)
                if step == (10 if h < HR else 4) and h > 0:
                    scale_y(h - 1)
                if h == HR and step == 9:
                    yT_high_part(HR - 1)

            def copy_xT(n, t):
                for half in range(2):
                    act.wait_ge(xT_ps, 4 * n + 2 * t + half + 1)
                    dst = (swa_xT_parts[:, 0] if n == 1 else xT)[:, 4 * half:4 * half + 4, t * P:(t + 1) * P]
                    af(dst, ps[:, 4 + 2 * t + half, :].rearrange("p (k n) -> p k n", n=P), ACT.Copy)\
                        .then_inc(swa_x_high if n == 1 else xT_ready, 1)

            def swa_split_high(p):
                u = p // 2
                act.wait_ge(loaded[1][(SWA_SLOT + u) % RING], 16)
                if p >= SPLIT_BUFS:
                    act.wait_ge(swa_w_used, p - SPLIT_BUFS + 1)
                af(swa_w_parts[:, p % SPLIT_BUFS, 0, :], swa_piece(p), ACT.Copy).then_inc(swa_w_high, 1)

            def mixture(L):
                m = M[L]
                for t in range(TT):
                    copy_xT(2 * L, t)
                    af(x_parts[:, 0, t, :], x_tok[:, t, :], ACT.Copy).then_inc(m["x_high"], 1)
                if L == 0:
                    act.dma_start(swa_bias[:, :], d["swa_bias"].to_broadcast([P, SWA_IN]))\
                        .then_inc(bias_in, 16)
                act.wait_ge(x_ready, 8 * L + 4)
                af(z[:, :, :], x_tok[:, :, :], ACT.Copy, scale=ALPHA).then_inc(m["z_scaled"], 1)
                act.wait_ge(m["exp_arg"], 1)
                af(r_exp[:, :, :], r_diff[:, :, :], ACT.Exp).then_inc(m["exp_val"], 1)
                act.wait_ge(m["exp_arg"], 2)
                af(r_et[:, :, :], r_dt[:, :, :], ACT.Exp).then_inc(m["exp_val"], 1)
                rounds = load_rounds(act, L)
                with act.Fori(0, rounds) as r:
                    def gathered(part):
                        slots = slice(*GATHERS[part])
                        for q in range(part * KT, (part + 1) * KT, 2):
                            act.wait_ge(m["gather_ps"], r * 2 * EVACUATIONS + q + 1)
                            af(xsT[:, q % KT, slots], ps[:, 5 + q % 3, 0:slots.stop - slots.start],
                               ACT.Copy).then_inc(m["gather_act"], 1)

                    gathered(0)
                    gathered(1)
                    for i in range(PAIRS + 1):
                        if i > 0:
                            act.wait_ge(m["y_done"], r * PAIRS + i)
                            if i > 1:
                                act.wait_ge(m["scattered"], r * (PAIRS - 1) + i - 1)
                            for n in range(2):
                                af(y_parts[:, 0, n * BANK:(n + 1) * BANK], ps[:, 6 + n, :], ACT.Copy)\
                                    .then_inc(m["y_high"], 1)
                        if i == PAIRS // 2 - 2:
                            gathered(2)
                        if i < PAIRS:
                            act.wait_ge(m["h_done"], r * PAIRS + i + 1)
                            af(silu_a, ps[:, 4 + i % 2, 0:FF], ACT.Silu).then_inc(m["silu_done"], 1)
                        if i == 0:
                            for j in range(4):
                                act.wait_ge(m["ohT_ps"], r * 4 + j + 1)
                                af(onehotT[:, 2 * j:2 * j + 2, :],
                                   ps[:, j, :].rearrange("p (g n) -> p g n", n=S), ACT.Copy)\
                                    .then_inc(m["ohT_ready"], 1)

            mixture(0)

            for p in range(SPLIT_BUFS):
                swa_split_high(p)
            for t in range(TT):
                copy_xT(1, t)
            for p in range(SPLIT_BUFS, SWA_IN_PIECES + SPLIT_BUFS):
                swa_split_high(p)
            for t in range(TT):
                for half in range(2):
                    act.wait_ge(sqk_ps, 3 * t + half + 1)
                    af(sqT[:, 2 * t:2 * t + 2, 4 * half:4 * half + 4, :].rearrange("p c i n -> p i c n"),
                       ps[:, (6, 0)[t] + half, :].rearrange("p (i c n) -> p i c n", i=4, c=2), ACT.Copy)\
                        .then_inc(sqk_ready, 1)
                act.wait_ge(sqk_ps, 3 * t + 3)
                af(skT[:, t * P:(t + 1) * P], ps[:, 4 + t, 0:P], ACT.Copy).then_inc(sqk_ready, 1)
                at, of = ((5, CHUNK), (4, 0))[t]
                af(skT[:, at * CHUNK:(at + 1) * CHUNK], ps[:, 4 + t, of:of + CHUNK], ACT.Copy)\
                    .then_inc(sqk_ready, 1)

            def oT_high_part(c):
                act.wait_ge(pv_done, c + 1)
                af(oT_parts[:, 0, :, c * CHUNK:(c + 1) * CHUNK],
                   ps[:, c % 2, :].rearrange("p (i n) -> p i n", n=CHUNK), ACT.Copy).then_inc(oT_high, 1)

            for c in range(4):
                width = P if c else CHUNK
                act.wait_ge(max_done, c + 1)
                if c >= 2:
                    act.wait_ge(probsT_ps, c - 1)
                for i in range(8):
                    af(probs[:, c % 2, i, 0:width], ps[:, 2 + 2 * (c % 2) + i // 4, (i % 4) * P:(i % 4) * P + width],
                       ACT.Exp, bias=s_negm[:, c % 2, i:i + 1], scale=HD ** -0.5, accum_out=s_sum[:, c % 2, i:i + 1])
                af(s_esink[:, c % 2, :], s_dsink[:, c % 2, :], ACT.Exp).then_inc(exp_done, 1)
                if c >= 2:
                    oT_high_part(c - 2)
            for c in (2, 3):
                oT_high_part(c)
            for p in range(SWA_IN_PIECES + SPLIT_BUFS, SWA_PIECES):
                swa_split_high(p)
            mixture(1)

        @block.vector
        def _(dve):
            tt, ts = nc.vector.tensor_tensor, nc.vector.tensor_scalar
            stt = nc.vector.scalar_tensor_tensor
            steps = [0]

            def then(ins):
                steps[0] += 1
                ins.then_inc(dve_step, 1)
                dve.wait_ge(dve_step, steps[0])

            def split_low(p):
                dve.wait_ge(w_high, p + 1)
                u, b = p // 2, p % SPLIT_BUFS
                tt(w_parts[:, b, 1, :], ring_low[:, u % RET_RING, p % 2 * PIECE:(p % 2 + 1) * PIECE],
                   w_parts[:, b, 0, :].bitcast(F32), ALU.subtract).then_inc(w_low, 1)

            for half in range(2):
                ks = slice(half * KT // 2, (half + 1) * KT // 2)
                dve.wait_ge(x_split_high, half + 1)
                tt(xT_parts[:, 1, ks, :], x_staged[:, ks, :], xT_parts[:, 0, ks, :].bitcast(F32),
                   ALU.subtract).then_inc(x_split_low, 1)
                split_low(half)

            dve.wait_ge(trig_in, 48)
            then(nc.vector.tensor_copy(turns[:, 0:S + TT], pos_i[:, :]))
            ts(angle[:, 0:S], turns[:, 0:S], cst[:, C_FREQ_R:C_FREQ_R + 1], None, ALU.mult)
            for t in range(TT):
                last = ts(angle[:, S + 32 * t:S + 32 * (t + 1)], cst[:, C_FREQ_S:C_FREQ_S + 32],
                          turns[:, S + t:S + t + 1], None, ALU.mult)
            then(last)
            then(ts(turns, angle, 1.0 / TWO_PI, ROUND_MAGIC, ALU.mult, ALU.add))
            then(ts(turns, turns, ROUND_MAGIC, None, ALU.subtract))
            for part in (TWO_PI_A, TWO_PI_B, TWO_PI_C):
                then(stt(angle, turns, -part, angle, ALU.mult, ALU.add))
            then(ts(angle, angle, PI_BELOW, -PI_BELOW, ALU.min, ALU.max))
            stt(turns, angle, -1.0, angle, ALU.mult, ALU.min).then_inc(angles_done, 1)
            dve.wait_ge(angles_done, 1)
            ts(turns, turns, np.pi / 2, None, ALU.add).then_inc(angles_done, 1)

            nc.vector.tensor_copy(tri_ones[:, :], cst[:, C_TRI:C_TRI + 2 * P]).then_inc(tri_ready, 1)

            def rotate(h, j):
                if h == 0 and j == 0:
                    dve.wait_ge(trig_done, 2)
                dve.wait_ge(w_used, HEAD_PIECES * h + 2 * j + 2)
                if h or j:
                    dve.wait_ge(qk_ready, 2 * h + j)
                if h > 1:
                    dve.wait_ge(yT_ready, 2 * (h - 1))
                x = ps[:, j, :].rearrange("p (a n) -> p a n", a=2)
                tt(rotA, x, cos[:, 0:S].unsqueeze(1).to_broadcast([P, 2, S]), ALU.mult)
                tt(rotB, x, sin[:, 0:S].unsqueeze(1).to_broadcast([P, 2, S]), ALU.mult)\
                    .then_inc(rope_read, 1)
                dve.wait_ge(rope_read, 2 * h + j + 1)
                if h >= 2:
                    dve.wait_ge(ret_scores, h - 1)
                dst = (qT if j == 0 else kT)[:, h % 2]
                tt(dst[:, 0], rotA[:, 0], rotB[:, 1], ALU.subtract)
                tt(dst[:, 1], rotB[:, 0], rotA[:, 1], ALU.add).then_inc(qk_ready, 1)

            def mask(h):
                dve.wait_ge(ret_scores, h + 1)
                if h == 0:
                    dve.wait_ge(decay_in, 16)
                if h >= 2:
                    dve.wait_ge(ret_o, 2 * (h - 1))
                tt(prT[:, h % 2], ps[:, 3, 0:3 * P], decay[:, h], ALU.mult).then_inc(ret_masked, 1)

            def norm_gate(h):
                for t in range(TT):
                    dve.wait_ge(ret_o, 2 * h + t + 1)
                    then(nc.vector.bn_stats(stats[:, t, 0, :], ps[:, 4 + t, :]))
                    if h > 0:
                        dve.wait_ge(gn_rstd, 2 * h)
                    nc.vector.bn_aggr(mean_var[:, t, :], stats[:, t, 0, :]).then_inc(gn_stats, 1)
                for t in range(TT):
                    dve.wait_ge(gn_stats, 2 * h + t + 1)
                    dve.wait_ge(vg_done, 4 * h + 2 + t + 1)
                    y = g_ret[:, h % 2, t, :]
                    stt(y, ps[:, 4 + t, :], mean_var[:, t, 0:1], y, ALU.subtract, ALU.mult)\
                        .then_inc(gn_gated, 1)

            def split_yT(h):
                dve.wait_ge(qk_ready, min(2 * (h + 2), 2 * HR))
                for t in range(TT):
                    dve.wait_ge(yT_ps, 2 * h + t + 1)
                    if h == 0 and t == 0:
                        dve.wait_ge(params_in, 64)
                    tt(scaled_yT[t], ps[:, 6 + t, :].rearrange("p (k n) -> p k n", n=P),
                       gn_gain[:, 4 * h:4 * h + 4].unsqueeze(2).to_broadcast([P, 4, P]), ALU.mult)\
                        .then_inc(yT_scaled, 1)
                for t in range(TT):
                    dve.wait_ge(yT_high, 2 * h + t + 1)
                    high, low = (yT_parts[:, a, 4 * h:4 * h + 4, t * P:(t + 1) * P] for a in range(2))
                    tt(low, scaled_yT[t], high.bitcast(F32), ALU.subtract).then_inc(yT_ready, 1)

            for p in range(PIECES):
                h = min(p // HEAD_PIECES, HR)
                step = p - h * HEAD_PIECES
                if p + SPLIT_BUFS - 1 < PIECES:
                    split_low(p + SPLIT_BUFS - 1)
                if step == 1 and h > 1:
                    split_yT(h - 2)
                if step in (2, 4) and h < HR:
                    rotate(h, step // 2 - 1)
                if step == (5 if h < HR else 0) and h > 0:
                    mask(h - 1)
                if step == (8 if h < HR else 2) and h > 0:
                    norm_gate(h - 1)
                if h == HR and step == 9:
                    split_yT(HR - 1)

            def mixer_residual(L):
                for i in range(4):
                    dve.wait_ge(mix_done, 4 * L + i + 1)
                    if L == 0 and i == 0:
                        dve.wait_ge(x_in, 16)
                    cols = slice((i % 2) * BANK, (i % 2 + 1) * BANK)
                    stt(z[:, i // 2, cols], x_tok[:, i // 2, cols], ALPHA, ps[:, i, :],
                        ALU.mult, ALU.add).then_inc(z_ready, 1)

            def layer_norm(n):
                for t in range(TT):
                    dve.wait_ge(z_ready, 4 * n + 2 * t + 2)
                    for half in range(2):
                        last = nc.vector.bn_stats(stats[:, t, half, :],
                                                  z[:, t, half * BANK:(half + 1) * BANK])
                    then(last)
                    nc.vector.bn_aggr(mean_var[:, t, :], stats[:, t, :, :].rearrange("p a b -> p (a b)"))\
                        .then_inc(ln_stats, 1)
                    dve.wait_ge(ln_stats, 2 * n + t + 1)
                    if t == 0:
                        dve.wait_ge(ln_in, 16 * (n + 1))
                    then(stt(z[:, t, :], z[:, t, :], mean_var[:, t, 0:1], ln_rows[:, 0, :],
                             ALU.subtract, ALU.mult))
                    dve.wait_ge(ln_rstd, 2 * n + t + 1)
                    for half in range(2):
                        cols = slice(half * BANK, (half + 1) * BANK)
                        stt(x_tok[:, t, cols], z[:, t, cols], rstd[:, t:t + 1], ln_rows[:, 1, cols],
                            ALU.mult, ALU.add).then_inc(x_ready, 1)

            def by_row(a):
                return a[:, :, :].rearrange("p t (r n) -> p (t r) n", n=G)

            def over_row(a):
                return a[:, :, :].rearrange("p t r -> p (t r)").unsqueeze(2)\
                    .to_broadcast([P, TT * (1 + G), G])

            def first_max(dst, top, values):
                then(nc.vector.tensor_reduce(top[:, :, :].rearrange("p t r -> p (t r)"), by_row(values),
                                             AX.X, ALU.max))
                then(tt(by_row(r_eq), by_row(values), over_row(top), ALU.is_equal))
                then(tt(by_row(r_eq), by_row(r_eq),
                        tie.unsqueeze(1).to_broadcast([P, TT * (1 + G), G]), ALU.mult))
                then(nc.vector.tensor_reduce(r_tie[:, :, :].rearrange("p t r -> p (t r)"), by_row(r_eq),
                                             AX.X, ALU.max))
                then(tt(by_row(dst), by_row(r_eq), over_row(r_tie), ALU.is_equal))

            def mixture(L):
                m = M[L]
                for t in range(TT):
                    dve.wait_ge(m["x_high"], t + 1)
                    tt(x_parts[:, 1, t, :], x_tok[:, t, :], x_parts[:, 0, t, :].bitcast(F32),
                       ALU.subtract).then_inc(m["x_low"], 1)
                dve.wait_ge(m["logits_ps"], 2)
                then(tt(logits[:, :, :], ps[:, 0, 0:2 * 32].rearrange("p (t n) -> p t n", t=TT)[:, :, 0:NR],
                        b_router[:, L:L + 1, :].to_broadcast([P, TT, NR]), ALU.add))
                first_max(oh_first, r_first, logits)
                tt(r_diff[:, :, :], logits[:, :, 0:G], r_first[:, :, 0:1].to_broadcast([P, TT, G]),
                   ALU.subtract).then_inc(m["exp_arg"], 1)
                then(stt(r_rest[:, :, :], oh_first[:, :, :], -3e38, logits[:, :, :], ALU.mult, ALU.add))
                first_max(oh_second, r_second, r_rest)
                of_group = oh_first[:, :, 0:G].unsqueeze(3).to_broadcast([P, TT, G, E])
                then(tt(picked[:, :, :], oh_first[:, :, G:NR], oh_second[:, :, G:NR], ALU.add))
                tt(chosen[:, :, :].rearrange("p t (g e) -> p t g e", g=G), of_group,
                   picked[:, :, :].rearrange("p t (g e) -> p t g e", g=G), ALU.mult)\
                    .then_inc(m["chosen_ready"], 1)
                tt(r_dt[:, :, :], r_second[:, :, :], r_first[:, :, :], ALU.subtract)\
                    .then_inc(m["exp_arg"], 1)
                dve.wait_ge(m["rank_ps"], 1)
                dve.wait_ge(m["chosen_ready"], 1)
                stt(key[:, :, :].rearrange("p t g -> p (t g)"), ps[:, 1, 0:TT * NE], 1.0,
                    chosen[:, :, :].rearrange("p t g -> p (t g)"), ALU.add, ALU.mult)\
                    .then_inc(m["keys_ready"], 1)
                then(nc.vector.tensor_reduce(n_over[0:1, 0:1], ps[0:1, 1, 2 * NE:3 * NE], AX.X, ALU.max))
                then(tt(n_over[0:1, 1:ROUNDS_MAX], cst[0:1, C_OVER:C_OVER + ROUNDS_MAX - 1],
                        n_over[0:1, 0:1].to_broadcast([1, ROUNDS_MAX - 1]), ALU.is_lt))
                then(nc.vector.tensor_reduce(n_over[0:1, ROUNDS_MAX:ROUNDS_MAX + 1],
                                             n_over[0:1, 1:ROUNDS_MAX], AX.X, ALU.add))
                nc.vector.tensor_copy(more_rounds[0:1, 0:1], n_over[0:1, ROUNDS_MAX:ROUNDS_MAX + 1])\
                    .then_inc(m["rounds_ready"], 1)

                def token_to_slot(r, rest):
                    first, end = ((0, GATHERS[0][1] // SLOTS), (GATHERS[0][1] // SLOTS, NE))[rest]
                    dve.wait_ge(m["keys_ready"], r + 1)
                    for t in range(TT):
                        last = tt(onehot[:, t, first * SLOTS:end * SLOTS].rearrange("p (e n) -> p e n", n=SLOTS),
                                  iota.unsqueeze(1).to_broadcast([P, end - first, SLOTS]),
                                  key[:, t, first:end].unsqueeze(2).to_broadcast([P, end - first, SLOTS]),
                                  ALU.is_equal)
                    last.then_inc(m["onehot_ready"], 1)

                token_to_slot(0, 0)
                dve.wait_ge(m["exp_val"], 1)
                then(nc.vector.tensor_reduce(r_gate[:, :], r_exp[:, :, :], AX.X, ALU.add))
                then(nc.vector.reciprocal(r_gate[:, :], r_gate[:, :]))
                dve.wait_ge(m["exp_val"], 2)
                then(ts(r_w1[:, :, :], r_et[:, :, :], 1.0, None, ALU.add))
                then(nc.vector.reciprocal(r_w1[:, :, :], r_w1[:, :, :]))
                then(tt(r_w1[:, :, :], r_w1[:, :, :],
                        r_gate[:, :].unsqueeze(2).to_broadcast([P, TT, 1 + G]), ALU.mult))
                then(tt(r_w2[:, :, :], r_w1[:, :, :], r_et[:, :, :], ALU.mult))
                tt(by_row(r_eq), by_row(oh_first), over_row(r_w1), ALU.mult)
                then(tt(by_row(oh_second), by_row(oh_second), over_row(r_w2), ALU.mult))
                then(tt(weight[:, :, :], r_eq[:, :, G:NR], oh_second[:, :, G:NR], ALU.add))
                tt(combine[:, :, :].rearrange("p t (g e) -> p t g e", g=G), of_group,
                   weight[:, :, :].rearrange("p t (g e) -> p t g e", g=G), ALU.mult)\
                    .then_inc(m["combine_ready"], 1)
                rounds = load_rounds(dve, L)
                with dve.Fori(0, rounds) as r:
                    def gathered(part):
                        slots = slice(*GATHERS[part])
                        for q in range(part * KT + 1, (part + 1) * KT, 2):
                            dve.wait_ge(m["gather_ps"], r * 2 * EVACUATIONS + q + 1)
                            nc.vector.tensor_copy(xsT[:, q % KT, slots],
                                                  ps[:, 5 + q % 3, 0:slots.stop - slots.start])\
                                .then_inc(m["gather_dve"], 1)

                    gathered(0)
                    token_to_slot(r, 1)
                    dve.wait_ge(m["cw_ps"], r + 1)
                    for e in range(2):
                        rows = slice(e * SLOTS, (e + 1) * SLOTS)
                        both = ps[rows, 0, 0:NE].rearrange("p (i e) -> p i e", e=2)
                        last = nc.vector.tensor_copy(cw_slots[rows, :], both[:, :, e])
                    last.then_inc(m["cw_ready"], 1)
                    gathered(1)
                    for i in range(PAIRS + 1):
                        n = r * PAIRS + i
                        if i > 0:
                            dve.wait_ge(m["actT_ps"], n)
                            nc.vector.tensor_copy(actT, ps[:, 4 + (i - 1) % 2, 0:FT * P]
                                                  .rearrange("p (f n) -> p f n", n=P))\
                                .then_inc(m["actT_ready"], 1)
                        if i > 0:
                            for b in range(2):
                                cols = slice(b * BANK, (b + 1) * BANK)
                                dve.wait_ge(m["y_high"], 2 * n - 1 + b)
                                tt(y_parts[:, 1, cols], ps[:, 6 + b, :],
                                   y_parts[:, 0, cols].bitcast(F32), ALU.subtract)\
                                    .then_inc(m["y_low"], 1)
                        if i == PAIRS // 2 - 2:
                            gathered(2)
                        if i < PAIRS:
                            dve.wait_ge(m["silu_done"], n + 1)
                            if i == 0:
                                dve.wait_ge(m["cw_ready"], r + 1)
                            stt(act_sl, ps[:, 4 + i % 2, FF:2 * FF], cw_slots[:, i:i + 1], silu_a,
                                ALU.mult, ALU.mult).then_inc(m["act_done"], 1)
                        if i == PAIRS // 2:
                            dve.wait_ge(m["onehot_ready"], 2 * r + 2)
                            ts(key[:, :, :], key[:, :, :], -float(SLOTS), None, ALU.add)\
                                .then_inc(m["keys_ready"], 1)
                            token_to_slot(r + 1, 0)
                    dve.wait_ge(m["z_scaled"], 1)
                    for n, i in enumerate((0, 2, 1, 3)):
                        cols = slice((i % 2) * BANK, (i % 2 + 1) * BANK)
                        dve.wait_ge(m["sums_done"], r * 4 + n + 1)
                        last = tt(z[:, i // 2, cols], z[:, i // 2, cols], ps[:, i, :], ALU.add)
                    last.then_inc(m["z_added"], 1)
                    dve.wait_ge(m["z_added"], r + 1)
                for i in range(4):
                    nc.vector.nop().then_inc(z_ready, 1)

            mixer_residual(0)
            layer_norm(0)
            mixture(0)
            layer_norm(1)

            def swa_split_low(p):
                dve.wait_ge(swa_w_high, p + 1)
                b = p % SPLIT_BUFS
                tt(swa_w_parts[:, b, 1, :], swa_piece(p), swa_w_parts[:, b, 0, :].bitcast(F32),
                   ALU.subtract).then_inc(swa_w_low, 1)

            for i in range(4):
                t, ks = i // 2, slice(i % 2 * 4, i % 2 * 4 + 4)
                dve.wait_ge(swa_x_high, i + 1)
                high, low = (swa_xT_parts[:, a, ks, t * P:(t + 1) * P] for a in range(2))
                tt(low, ps[:, 4 + i, :].rearrange("p (k n) -> p k n", n=P), high.bitcast(F32),
                   ALU.subtract).then_inc(swa_x_low, 1)
            swa_split_low(2)
            dve.wait_ge(bias_in, 16)
            for n in range(6):
                part, t = n // 2, n % 2
                for p in ((3, 4), (5,), (6, 7, 8), (9,), (), ())[n]:
                    swa_split_low(p)
                if t == 0:
                    dve.wait_ge(sproj_done, part + 1)
                else:
                    dve.wait_ge(swa_w_used, (2, 6, 10)[part])
                if n >= 2:
                    dve.wait_ge(rotB_done, n - 1)
                    dve.wait_ge(rot_done, n - 1)
                heads = HPG if part else KVH
                width = heads * HD
                bank = (4, 0, 2)[part] + t
                cols = slice((HS * HD, 0, BANK)[part], (HS * HD, 0, BANK)[part] + width)
                x = unrotated[:, n % 2, 0:width]
                tt(x, ps[:, bank, 0:width], swa_bias[:, cols], ALU.add).then_inc(sproj_read, 1)
                if part == 0:
                    for win, rows in (((0, slice(0, P)), (2, slice(CHUNK, P))),
                                      ((1, slice(0, P)), (2, slice(0, CHUNK))))[t]:
                        tt(v_win[rows, win, :], ps[rows, bank, KVH * HD:2 * KVH * HD],
                           swa_bias[rows, QKW:SWA_IN], ALU.add)
                dve.wait_ge(sproj_read, n + 1)
                c = cos[:, S + 32 * t:S + 32 * (t + 1)].unsqueeze(1).to_broadcast([P, 2 * heads, 32])
                a, b = rot_cos[:, n % 2, 0:width], rot_sin[:, n % 2, 0:width]
                then(tt(a.rearrange("p (h n) -> p h n", n=32), x.rearrange("p (h n) -> p h n", n=32), c,
                        ALU.mult))
                dve.wait_ge(rotB_done, n + 1)
                a = a.rearrange("p (h a n) -> p h a n", a=2, n=32)
                b = b.rearrange("p (h a n) -> p h a n", a=2, n=32)
                if part:
                    y = q_rows[:, t, 0:HS * HD].rearrange("p (i g a n) -> p g i a n", i=HPG, g=KVH,
                                                          a=2)[:, part - 1]
                else:
                    y = q_rows[:, t, HS * HD:QKW].rearrange("p (h a n) -> p h a n", a=2, n=32)
                tt(y[:, :, 0, :], a[:, :, 0, :], b[:, :, 1, :], ALU.subtract)
                tt(y[:, :, 1, :], b[:, :, 0, :], a[:, :, 1, :], ALU.add).then_inc(rot_done, 1)
            for p in range(SWA_IN_PIECES, SWA_IN_PIECES + SPLIT_BUFS):
                swa_split_low(p)

            def row_max(c):
                width = P if c else CHUNK
                s = ps[:, 2 + 2 * (c % 2):4 + 2 * (c % 2), :].rearrange("p b (i n) -> p (b i) n", n=P)
                dve.wait_ge(swa_scores, c + 1)
                then(nc.vector.tensor_reduce(s_max[:, :], s[:, :, 0:width], AX.X, ALU.max))
                then(stt(s_max[:, :], s_max[:, :], HD ** -0.5, sinks[:, :], ALU.mult, ALU.max))
                then(ts(s_negm[:, c % 2, :], s_max[:, :], -1.0, None, ALU.mult))
                tt(s_dsink[:, c % 2, :], sinks[:, :], s_negm[:, c % 2, :], ALU.add)\
                    .then_inc(max_done, 1)

            def normalise(c):
                width = P if c else CHUNK
                dve.wait_ge(exp_done, c + 1)
                then(tt(s_rden[:, :], s_sum[:, c % 2, :], s_esink[:, c % 2, :], ALU.add))
                then(nc.vector.reciprocal(s_rden[:, :], s_rden[:, :]))
                tt(probs[:, c % 2, :, 0:width], probs[:, c % 2, :, 0:width],
                   s_rden[:, :].unsqueeze(2).to_broadcast([P, 8, width]), ALU.mult)\
                    .then_inc(probs_ready, 1)

            row_max(0)
            row_max(1)
            normalise(0)
            row_max(2)
            for c in range(4):
                width = P if c else CHUNK
                dve.wait_ge(probsT_ps, c + 1)
                if c:
                    dve.wait_ge(pv_done, c)
                for half in range(2):
                    nc.vector.tensor_copy(probsT[0:width, 4 * half:4 * half + 4, :],
                                          ps[0:width, 6 + half, :].rearrange("p (i n) -> p i n", n=P))\
                        .then_inc(probsT_ready, 1)
                if c + 1 < 4:
                    normalise(c + 1)
                if c + 3 < 4:
                    row_max(c + 3)
                dve.wait_ge(oT_high, c + 1)
                high, low = (oT_parts[:, a, :, c * CHUNK:(c + 1) * CHUNK] for a in range(2))
                tt(low, ps[:, c % 2, :].rearrange("p (i n) -> p i n", n=CHUNK), high.bitcast(F32),
                   ALU.subtract).then_inc(oT_ready, 1)
            for p in range(SWA_IN_PIECES + SPLIT_BUFS, SWA_PIECES):
                swa_split_low(p)
            mixer_residual(1)
            layer_norm(2)
            mixture(1)
            layer_norm(3)

        @block.gpsimd
        def _(pool):
            nc.gpsimd.memset(minus_half[:, :], -0.5).then_inc(pool_const, 1)
            pool.wait_ge(w_used, 4)
            pool.dma_start(ln_rows[:, :, :], d["ln_rows"][0:1].to_broadcast([P, 2, D])).then_inc(ln_in, 16)
            pool.wait_ge(pool_const, 1)
            count = [1]

            def inverse_std(t):
                nc.gpsimd.tensor_scalar(var_eps[:, t:t + 1], mean_var[:, t, 1:2], LN_EPS, None, ALU.add)\
                    .then_inc(pool_const, 1)
                count[0] += 1
                pool.wait_ge(pool_const, count[0])
                return nc.gpsimd.tensor_tensor(rstd[:, t:t + 1], var_eps[:, t:t + 1], minus_half[:, :],
                                               ALU.pow)

            for h in range(HR):
                for t in range(TT):
                    pool.wait_ge(gn_stats, 2 * h + t + 1)
                    if h > 0:
                        pool.wait_ge(y_ready, 2 * (h - 1) + t + 1)
                    inverse_std(t).then_inc(gn_rstd, 1)

            def layer_norm(n):
                for t in range(TT):
                    pool.wait_ge(ln_stats, 2 * n + t + 1)
                    if n == 0:
                        pool.wait_ge(y_ready, 2 * HR)
                    inverse_std(t).then_inc(ln_rstd, 1)
                if n < 3:
                    pool.wait_ge(x_ready, 4 * n + 4)
                    pool.dma_start(ln_rows[:, :, :], d["ln_rows"][n + 1:n + 2].to_broadcast([P, 2, D]))\
                        .then_inc(ln_in, 16)

            layer_norm(0)
            for p in range(FIRST_BY_POOL):
                pool.wait_ge(swa_w_high, p + 1)
                nc.gpsimd.tensor_tensor(swa_w_parts[:, p, 1, :], swa_piece(p),
                                        swa_w_parts[:, p, 0, :].bitcast(F32), ALU.subtract)\
                    .then_inc(swa_w_low_pool, 1)
            layer_norm(1)
            for n in range(6):
                pool.wait_ge(sproj_read, n + 1)
                if n >= 2:
                    pool.wait_ge(rot_done, n - 1)
                heads = HPG if n // 2 else KVH
                t = n % 2
                s = sin[:, S + 32 * t:S + 32 * (t + 1)].unsqueeze(1).to_broadcast([P, 2 * heads, 32])
                nc.gpsimd.tensor_tensor(
                    rot_sin[:, n % 2, 0:heads * HD].rearrange("p (h n) -> p h n", n=32),
                    unrotated[:, n % 2, 0:heads * HD].rearrange("p (h n) -> p h n", n=32), s, ALU.mult)\
                    .then_inc(rotB_done, 1)
            layer_norm(2)
            layer_norm(3)


def shape_constants():
    c = np.zeros((P, C_END), np.float32)
    c[:, C_FREQ_R] = 10000.0 ** (-np.arange(0, DK, 2, dtype=np.float64) / DK)
    c[:, C_FREQ_S:C_FREQ_S + 32] = 10000.0 ** (-np.arange(0, HD, 2, dtype=np.float64) / HD)
    c[:, C_IDENT:C_IDENT + P] = np.eye(P)
    c[:, C_TRI:C_TRI + P] = np.triu(np.ones((P, P)), 1)
    c[:, C_ONES:C_ONES + P] = 1.0
    c[:, C_IOTA:C_IOTA + SLOTS] = np.arange(1, SLOTS + 1)
    c[:, C_OVER:C_OVER + ROUNDS_MAX - 1] = np.arange(1, ROUNDS_MAX) * SLOTS + 0.5
    c[:, C_TIE:C_TIE + G] = np.arange(G, 0, -1)
    log_gamma = np.log1p(-(2.0 ** (-5.0 - np.arange(HR, dtype=np.float64))))
    m, n = np.arange(S)[:, None], np.arange(S)[None, :]
    seen = m // CHUNK <= n // CHUNK
    full = np.exp(log_gamma[:, None, None] * np.abs(n - m)) * seen * DK ** -0.5
    decay = np.concatenate([full[:, 0:P, :], full[:, P:S, P:S]], axis=2).transpose(1, 0, 2)
    return c, np.ascontiguousarray(decay.astype(np.float32))


def kernel(x, positions, ret_w_in, ret_w_out, ret_gn_gain, swa_w_in, swa_b_in, swa_sinks, swa_w_out,
           moe_w_group, moe_b_group, moe_w_router, moe_b_router, moe_w_in, moe_w_out, ln_gain, ln_bias):
    import concourse.bacc as bacc
    from concourse.bass_utils import run_bass_kernel_spmd as run

    def tiles(w):
        return w.reshape(-1, P, w.shape[-1]).transpose(1, 0, 2)

    def lay(a):
        return np.ascontiguousarray(np.asarray(a))

    w_in = tiles(np.asarray(ret_w_in)[0])
    qw, vw = HR * DK, HR * DV
    ret_units = []
    for h in range(HR):
        q, k = w_in[:, :, h * DK:(h + 1) * DK], w_in[:, :, qw + h * DK:qw + (h + 1) * DK]
        ret_units.append(np.stack([a[:, :, half * P:(half + 1) * P] for a in (q, k)
                                   for half in range(2)], axis=1))
        for first in (2 * qw, 2 * qw + vw):
            ret_units.append(w_in[:, :, first + h * DV:first + (h + 1) * DV])
    swa = tiles(np.asarray(swa_w_in)[0])
    consts, decay = shape_constants()
    x0 = np.asarray(x)[0]
    swa_out = np.asarray(swa_w_out)[0].reshape(KVH, HPG, HD, D).transpose(0, 2, 1, 3)
    sink_rows = np.repeat(np.asarray(swa_sinks)[0].reshape(8, 2), CHUNK, axis=1).T
    arrays = {
        "x_rows": x0.reshape(TT, P, D).transpose(1, 0, 2),
        "x_cols": tiles(x0.T),
        "pos_row": np.asarray(positions).reshape(1, S),
        "pos_col": np.asarray(positions).reshape(TT, P).T,
        "consts": consts,
        "decay": decay,
        "w_ret_in": np.stack([u.reshape(P, 2 * UNIT) for u in ret_units]),
        "w_ret_out": np.asarray(ret_w_out)[0].reshape(HR, DV // P, P, D).transpose(0, 2, 1, 3)
        .reshape(HR, P, 2 * UNIT),
        "w_swa_in": np.stack([swa[:, :, u * BANK:(u + 1) * BANK].reshape(P, 2 * UNIT)
                              for u in range(2)]),
        "w_swa_kv": swa[:, :, HS * HD:SWA_IN].reshape(P, -1),
        "w_swa_out": swa_out.reshape(P, HPG * D),
        "w_moe_in": np.asarray(moe_w_in).reshape(2, G * E, KT, P, 2 * FF).transpose(0, 1, 3, 2, 4)
        .reshape(2, G * E, P, 2 * UNIT),
        "w_moe_out": np.asarray(moe_w_out).reshape(2, G * E // 2, 2 * FT, P, D).transpose(0, 1, 3, 2, 4)
        .reshape(2, G * E // 2, P, 2 * UNIT),
        "ln_rows": np.stack([np.asarray(ln_gain), np.asarray(ln_bias)], axis=2).reshape(4, 2, D),
        "w_router": np.stack([np.concatenate([tiles(np.asarray(moe_w_group)[i]),
                                              tiles(np.asarray(moe_w_router)[i])], axis=2)
                              for i in range(2)], axis=1),
        "b_router": np.concatenate([np.asarray(moe_b_group), np.asarray(moe_b_router)], axis=1)
        .reshape(1, 2 * NR),
        "gn_gain": np.asarray(ret_gn_gain)[0].reshape(HR * DV // P, P).T,
        "sinks": sink_rows,
        "swa_bias": np.asarray(swa_b_in).reshape(1, SWA_IN),
    }
    nc = bacc.Bacc("TRN2", target_bir_lowering=False, num_devices=1)
    feeds, d = {}, {}
    for name, a in arrays.items():
        feeds[f"in_{name}"] = lay(a)
        d[name] = nc.dram_tensor(f"in_{name}", feeds[f"in_{name}"].shape,
                                 mybir.dt.from_np(feeds[f"in_{name}"].dtype), kind="ExternalInput").ap()
    out = nc.dram_tensor("out", (1, S, D), F32, kind="ExternalOutput").ap()
    build(nc, d, out)
    return run(nc, [feeds], core_ids=[0]).results[0]["out"]
```
